# Optimizing a Trainium2 kernel written in Bass

```python
import functools
import jax
import jax.numpy as jnp
from jax import lax
import numpy as np

D_MODEL = 2048
BATCH = 1
SEQ = 512
DEPTH = 1
DEC_BATCH = 8
DEC_SEQ = 4
PAST_LEN = 4096
PAGE_SIZE = 128

HEAD_DIM = 64
N_ATT_HEADS = 16
N_KV_HEADS = 4
KV_GROUP = N_ATT_HEADS // N_KV_HEADS
ATT_WIDTH = N_ATT_HEADS * HEAD_DIM
N_RWKV_HEADS = 16
RWKV_WIDTH = N_RWKV_HEADS * HEAD_DIM
MIX_WIDTH = ATT_WIDTH + RWKV_WIDTH
ROPE_DIM = HEAD_DIM // 4
ROPE_THETA = 500000.0
MOBA_BLOCK = 256
MOBA_TOPK = 3
Q_BLOCK = 64
D_DECAY_LORA = 64
D_AAA_LORA = 64
D_GATE_LORA = 160
D_FF = 5632
CONV_W = 3
LN_EPS = 1e-5
GN_EPS = 64e-5
NEG_INF = -1e30
DN_ALPHA = (2.0 * DEPTH) ** 0.25
DN_BETA = (8.0 * DEPTH) ** -0.25

K_OFF = ATT_WIDTH
V_OFF = K_OFF + N_KV_HEADS * HEAD_DIM
ATT_END = V_OFF + N_KV_HEADS * HEAD_DIM
RWKV_PROJ = 3 * RWKV_WIDTH + D_DECAY_LORA + D_AAA_LORA + D_GATE_LORA
IN_WIDTH = ATT_END + RWKV_PROJ

kernel_name = "hymba_moba_rwkv7_deepnorm_convffn_step"

def layer_norm(x, g, b):
    xf = x.astype(jnp.float32)
    mu = jnp.mean(xf, axis=-1, keepdims=True)
    var = jnp.mean(jnp.square(xf - mu), axis=-1, keepdims=True)
    return ((xf - mu) * lax.rsqrt(var + LN_EPS) * g + b).astype(x.dtype)

def rope_partial(x, pos):
    half = ROPE_DIM // 2
    inv = jnp.power(ROPE_THETA, -(jnp.arange(half, dtype=jnp.float32) * 2.0 / ROPE_DIM))
    ang = pos.astype(jnp.float32)[:, None] * inv[None, :]
    cos = jnp.cos(ang)[:, None, :]
    sin = jnp.sin(ang)[:, None, :]
    xf = x.astype(jnp.float32)
    x1 = xf[..., :half]
    x2 = xf[..., half:ROPE_DIM]
    out = jnp.concatenate([x1 * cos - x2 * sin, x2 * cos + x1 * sin, xf[..., ROPE_DIM:]], axis=-1)
    return out.astype(x.dtype)

def moba_prompt_seq(q, k, v):
    S = q.shape[0]
    n_blk = -(-S // MOBA_BLOCK)
    n_cand = n_blk - 1
    topk = min(MOBA_TOPK, n_cand)
    pad = n_blk * MOBA_BLOCK - S
    kb = jnp.pad(k, ((0, pad), (0, 0), (0, 0))).reshape(n_blk, MOBA_BLOCK, N_KV_HEADS, HEAD_DIM)
    vb = jnp.pad(v, ((0, pad), (0, 0), (0, 0))).reshape(n_blk, MOBA_BLOCK, N_KV_HEADS, HEAD_DIM)
    kb_h = jnp.transpose(kb, (2, 0, 1, 3))
    vb_h = jnp.transpose(vb, (2, 0, 1, 3))
    kmean = jnp.mean(kb[:n_cand].astype(jnp.float32), axis=1)
    scale = HEAD_DIM ** -0.5
    kv_idx = jnp.arange(N_KV_HEADS)[None, :, None, None]
    blk_pos = jnp.arange(MOBA_BLOCK)
    nsel = topk * MOBA_BLOCK

    def chunk(args):
        qc, ci = args
        q0 = ci * Q_BLOCK
        own = q0 // MOBA_BLOCK
        qg = qc.reshape(Q_BLOCK, N_KV_HEADS, KV_GROUP, HEAD_DIM)
        q_pos = q0 + jnp.arange(Q_BLOCK)
        k_own = lax.dynamic_index_in_dim(kb, own, axis=0, keepdims=False)
        v_own = lax.dynamic_index_in_dim(vb, own, axis=0, keepdims=False)
        s_own = jnp.einsum('tcgd,scd->tcgs', qg, k_own, preferred_element_type=jnp.float32) * scale
        causal = (own * MOBA_BLOCK + blk_pos)[None, :] <= q_pos[:, None]
        s_own = jnp.where(causal[:, None, None, :], s_own, NEG_INF)
        if topk == 0:
            p = jax.nn.softmax(s_own, axis=-1)
            o = jnp.einsum('tcgs,scd->tcgd', p, v_own.astype(jnp.float32))
        else:
            gate = jnp.einsum('tcgd,ncd->tcgn', qg.astype(jnp.float32), kmean)
            gate = jnp.where(jnp.arange(n_cand) < own, gate, NEG_INF)
            _, sel = lax.top_k(gate, topk)
            valid = sel < own
            k_sel = kb_h[kv_idx, sel]
            v_sel = vb_h[kv_idx, sel]
            s_sel = jnp.einsum('tcgd,tcgjsd->tcgjs', qg, k_sel, preferred_element_type=jnp.float32) * scale
            s_sel = jnp.where(valid[..., None], s_sel, NEG_INF).reshape(Q_BLOCK, N_KV_HEADS, KV_GROUP, nsel)
            p = jax.nn.softmax(jnp.concatenate([s_sel, s_own], axis=-1), axis=-1)
            p_sel = p[..., :nsel].reshape(Q_BLOCK, N_KV_HEADS, KV_GROUP, topk, MOBA_BLOCK)
            o = (jnp.einsum('tcgjs,tcgjsd->tcgd', p_sel, v_sel.astype(jnp.float32))
                 + jnp.einsum('tcgs,scd->tcgd', p[..., nsel:], v_own.astype(jnp.float32)))
        return o.reshape(Q_BLOCK, ATT_WIDTH).astype(q.dtype)

    qs = q.reshape(S // Q_BLOCK, Q_BLOCK, N_ATT_HEADS, HEAD_DIM)
    out = lax.map(chunk, (qs, jnp.arange(S // Q_BLOCK, dtype=jnp.int32)))
    return out.reshape(S, ATT_WIDTH)

def moba_prompt(q, k, v):
    return lax.map(lambda qkv: moba_prompt_seq(qkv[0], qkv[1], qkv[2]), (q, k, v))

def moba_decode(q, k_new, v_new, cache_k, cache_v, page_table):
    Bd, T = q.shape[0], q.shape[1]
    past = page_table.shape[1] * PAGE_SIZE
    n_cand = past // MOBA_BLOCK
    topk = min(MOBA_TOPK, n_cand)
    own_start = n_cand * MOBA_BLOCK
    own_len = past - own_start
    ppb = MOBA_BLOCK // PAGE_SIZE
    scale = HEAD_DIM ** -0.5
    qg = q.reshape(Bd, T, N_KV_HEADS, KV_GROUP, HEAD_DIM)
    q_pos = past + jnp.arange(T)
    own_pages = page_table[:, own_start // PAGE_SIZE:]
    k_own = jnp.concatenate([cache_k[own_pages].reshape(Bd, own_len, N_KV_HEADS, HEAD_DIM).astype(k_new.dtype), k_new], axis=1)
    v_own = jnp.concatenate([cache_v[own_pages].reshape(Bd, own_len, N_KV_HEADS, HEAD_DIM).astype(v_new.dtype), v_new], axis=1)
    k_pos = own_start + jnp.arange(own_len + T)
    s_own = jnp.einsum('btcgd,bscd->btcgs', qg, k_own, preferred_element_type=jnp.float32) * scale
    causal = k_pos[None, :] <= q_pos[:, None]
    s_own = jnp.where(causal[None, :, None, None, :], s_own, NEG_INF)
    if topk == 0:
        p = jax.nn.softmax(s_own, axis=-1)
        o = jnp.einsum('btcgs,bscd->btcgd', p, v_own.astype(jnp.float32))
    else:
        k_full = cache_k[page_table[:, :own_start // PAGE_SIZE]].reshape(Bd, n_cand, MOBA_BLOCK, N_KV_HEADS, HEAD_DIM)
        kmean = jnp.mean(k_full.astype(jnp.float32), axis=2)
        gate = jnp.einsum('btcgd,bncd->btcgn', qg.astype(jnp.float32), kmean)
        _, sel = lax.top_k(gate, topk)
        logical = sel[..., None] * ppb + jnp.arange(ppb)
        phys = page_table[jnp.arange(Bd)[:, None, None, None, None, None], logical]
        kvi = jnp.arange(N_KV_HEADS)[None, None, :, None, None, None, None]
        rows = jnp.arange(PAGE_SIZE)
        nsel = topk * MOBA_BLOCK
        k_sel = cache_k[phys[..., None], rows, kvi].reshape(Bd, T, N_KV_HEADS, KV_GROUP, nsel, HEAD_DIM)
        v_sel = cache_v[phys[..., None], rows, kvi].reshape(Bd, T, N_KV_HEADS, KV_GROUP, nsel, HEAD_DIM)
        s_sel = jnp.einsum('btcgd,btcgsd->btcgs', qg, k_sel.astype(q.dtype), preferred_element_type=jnp.float32) * scale
        p = jax.nn.softmax(jnp.concatenate([s_sel, s_own], axis=-1), axis=-1)
        o = (jnp.einsum('btcgs,btcgsd->btcgd', p[..., :nsel], v_sel.astype(jnp.float32))
             + jnp.einsum('btcgs,bscd->btcgd', p[..., nsel:], v_own.astype(jnp.float32)))
    return o.reshape(Bd, T, ATT_WIDTH).astype(q.dtype)

def rwkv7_mix(z, z_last, wkv0, shift_mu, w0, w2, a0, a2, g2, k_k, k_a, r_k, gn_g, gn_b):
    B, T = z.shape[0], z.shape[1]
    f32 = jnp.float32
    z_cat = jnp.concatenate([z_last[:, None, :].astype(z.dtype), z], axis=1)
    zs = z + (z_cat[:, :-1] - z) * shift_mu
    splits = (RWKV_WIDTH, 2 * RWKV_WIDTH, 3 * RWKV_WIDTH, 3 * RWKV_WIDTH + D_DECAY_LORA,
              3 * RWKV_WIDTH + D_DECAY_LORA + D_AAA_LORA)
    r, k, v, w_lo, a_lo, g_lo = jnp.split(zs, splits, axis=-1)
    w = -jax.nn.softplus(-(w0 + jnp.tanh(w_lo) @ w2).astype(f32)) - 0.5
    decay = jnp.exp(-jnp.exp(w))
    a = jax.nn.sigmoid((a0 + a_lo @ a2).astype(f32))
    g = jax.nn.sigmoid(g_lo) @ g2
    r = r.astype(f32)
    k = k.astype(f32)
    v = v.astype(f32)
    kk = k * k_k
    k = k * (1.0 + (a - 1.0) * k_a)
    heads = lambda t: t.reshape(B, T, N_RWKV_HEADS, HEAD_DIM)
    r, k, v, a, decay, kk = (heads(r), heads(k), heads(v), heads(a), heads(decay), heads(kk))
    kk = kk / jnp.maximum(jnp.sqrt(jnp.sum(kk * kk, axis=-1, keepdims=True)), 1e-12)

    def step(S, inp):
        r_t, w_t, k_t, v_t, kk_t, a_t = inp
        sa = jnp.einsum('bhij,bhj->bhi', S, -kk_t)
        S = (S * w_t[:, :, None, :] + sa[..., :, None] * (kk_t * a_t)[..., None, :]
             + v_t[..., :, None] * k_t[..., None, :])
        return S, jnp.einsum('bhij,bhj->bhi', S, r_t)

    xs = tuple(jnp.swapaxes(t, 0, 1) for t in (r, decay, k, v, kk, a))
    S_T, o = lax.scan(step, wkv0.astype(f32), xs)
    o = jnp.swapaxes(o, 0, 1)
    mu = jnp.mean(o, axis=-1, keepdims=True)
    var = jnp.mean(jnp.square(o - mu), axis=-1, keepdims=True)
    on = ((o - mu) * lax.rsqrt(var + GN_EPS)).reshape(B, T, RWKV_WIDTH) * gn_g + gn_b
    bonus = jnp.sum(r * k * r_k.reshape(N_RWKV_HEADS, HEAD_DIM), axis=-1, keepdims=True) * v
    out = (on + bonus.reshape(B, T, RWKV_WIDTH)) * g
    return out.astype(z.dtype), z[:, -1], S_T.astype(wkv0.dtype)

def conv_ffn(x, hist, w_up, conv_w, conv_b, w_down):
    u = x @ w_up
    gp, up = u[..., :D_FF], u[..., D_FF:]
    zc = jnp.concatenate([hist.astype(gp.dtype), gp], axis=1)
    conv = lax.conv_general_dilated(zc, conv_w[:, None, :].astype(zc.dtype), window_strides=(1,), padding='VALID',
                                    dimension_numbers=('NWC', 'WIO', 'NWC'), feature_group_count=D_FF) + conv_b
    h = jax.nn.silu(conv) * up
    return h @ w_down, zc[:, -(CONV_W - 1):]

def trunk_layer(x, pos, attend, shift0, wkv0, conv0, lw):
    (w_in, w_out, shift_mu, w0, w2, a0, a2, g2, k_k, k_a, r_k, gn_g, gn_b,
     ln1_g, ln1_b, ln2_g, ln2_b, w_up, conv_w, conv_b, w_down) = lw
    B, T = x.shape[0], x.shape[1]
    proj = x @ w_in
    q = rope_partial(proj[..., :K_OFF].reshape(B, T, N_ATT_HEADS, HEAD_DIM), pos)
    k = rope_partial(proj[..., K_OFF:V_OFF].reshape(B, T, N_KV_HEADS, HEAD_DIM), pos)
    v = proj[..., V_OFF:ATT_END].reshape(B, T, N_KV_HEADS, HEAD_DIM)
    att = attend(q, k, v)
    rw, shift_new, wkv_new = rwkv7_mix(proj[..., ATT_END:], shift0, wkv0, shift_mu, w0, w2, a0, a2, g2,
                                       k_k, k_a, r_k, gn_g, gn_b)
    mix = jnp.concatenate([att, rw], axis=-1) @ w_out
    x1 = layer_norm(DN_ALPHA * x + mix, ln1_g, ln1_b)
    ffn, conv_new = conv_ffn(x1, conv0, w_up, conv_w, conv_b, w_down)
    y = layer_norm(DN_ALPHA * x1 + ffn, ln2_g, ln2_b)
    return y, k, v, wkv_new, shift_new, conv_new

def setup_inputs(seed: int = 0) -> dict:
    key = jax.random.key(seed)
    ks = jax.random.split(key, 32)
    f32 = jnp.float32
    nrm = lambda k, shape, s: jax.random.normal(k, shape, f32) * s
    n_pages = PAST_LEN // PAGE_SIZE
    n_used = DEC_BATCH * n_pages
    n_phys = n_used + n_used // 4
    col_scale = np.ones((IN_WIDTH,), np.float32)
    col_scale[V_OFF:ATT_END] = DN_BETA
    col_scale[ATT_END + 2 * RWKV_WIDTH:ATT_END + 3 * RWKV_WIDTH] = DN_BETA
    return {
        "x_prompt": nrm(ks[0], (BATCH, SEQ, D_MODEL), 1.0),
        "x_sample": nrm(ks[1], (DEC_BATCH, DEC_SEQ, D_MODEL), 1.0),
        "cache_k": nrm(ks[2], (DEPTH, n_phys, PAGE_SIZE, N_KV_HEADS, HEAD_DIM), 1.0),
        "cache_v": nrm(ks[3], (DEPTH, n_phys, PAGE_SIZE, N_KV_HEADS, HEAD_DIM), 1.0),
        "page_table": jax.random.permutation(ks[4], n_phys)[:n_used].reshape(DEC_BATCH, n_pages).astype(jnp.int32),
        "state_wkv": nrm(ks[5], (DEPTH, DEC_BATCH, N_RWKV_HEADS, HEAD_DIM, HEAD_DIM), 0.3),
        "state_shift": nrm(ks[6], (DEPTH, DEC_BATCH, RWKV_PROJ), 1.0),
        "state_conv": nrm(ks[7], (DEPTH, DEC_BATCH, CONV_W - 1, D_FF), 1.0),
        "w_in": nrm(ks[8], (DEPTH, D_MODEL, IN_WIDTH), D_MODEL ** -0.5) * jnp.asarray(col_scale),
        "w_out": nrm(ks[9], (DEPTH, MIX_WIDTH, D_MODEL), MIX_WIDTH ** -0.5 * DN_BETA),
        "shift_mu": jax.random.uniform(ks[10], (DEPTH, RWKV_PROJ), f32, 0.0, 1.0),
        "w0": jax.random.uniform(ks[11], (DEPTH, RWKV_WIDTH), f32, -6.0, -1.0),
        "w2": nrm(ks[12], (DEPTH, D_DECAY_LORA, RWKV_WIDTH), 0.1 * D_DECAY_LORA ** -0.5),
        "a0": nrm(ks[13], (DEPTH, RWKV_WIDTH), 0.1),
        "a2": nrm(ks[14], (DEPTH, D_AAA_LORA, RWKV_WIDTH), D_AAA_LORA ** -0.5),
        "g2": nrm(ks[15], (DEPTH, D_GATE_LORA, RWKV_WIDTH), D_GATE_LORA ** -0.5),
        "k_k": 0.85 + nrm(ks[16], (DEPTH, RWKV_WIDTH), 0.05),
        "k_a": 1.0 + nrm(ks[17], (DEPTH, RWKV_WIDTH), 0.05),
        "r_k": nrm(ks[18], (DEPTH, RWKV_WIDTH), 0.1),
        "gn_g": 1.0 + nrm(ks[19], (DEPTH, RWKV_WIDTH), 0.05),
        "gn_b": nrm(ks[20], (DEPTH, RWKV_WIDTH), 0.01),
        "ln1_g": 1.0 + nrm(ks[21], (DEPTH, D_MODEL), 0.05),
        "ln1_b": nrm(ks[22], (DEPTH, D_MODEL), 0.01),
        "ln2_g": 1.0 + nrm(ks[23], (DEPTH, D_MODEL), 0.05),
        "ln2_b": nrm(ks[24], (DEPTH, D_MODEL), 0.01),
        "w_up": nrm(ks[25], (DEPTH, D_MODEL, 2 * D_FF), D_MODEL ** -0.5),
        "conv_w": nrm(ks[26], (DEPTH, CONV_W, D_FF), CONV_W ** -0.5),
        "conv_b": nrm(ks[27], (DEPTH, D_FF), 0.01),
        "w_down": nrm(ks[28], (DEPTH, D_FF, D_MODEL), D_FF ** -0.5 * DN_BETA),
    }

def reference(x_prompt, x_sample, cache_k, cache_v, page_table, state_wkv, state_shift, state_conv,
              w_in, w_out, shift_mu, w0, w2, a0, a2, g2, k_k, k_a, r_k, gn_g, gn_b,
              ln1_g, ln1_b, ln2_g, ln2_b, w_up, conv_w, conv_b, w_down):
    B, S = x_prompt.shape[0], x_prompt.shape[1]
    T = x_sample.shape[1]
    past = page_table.shape[1] * PAGE_SIZE
    pos_p = jnp.arange(S, dtype=jnp.int32)
    pos_s = past + jnp.arange(T, dtype=jnp.int32)
    yp, ys = x_prompt, x_sample
    kp, vp, wp, zp, cp = [], [], [], [], []
    kq, vq, wq, zq, cq = [], [], [], [], []
    for l in range(DEPTH):
        lw = (w_in[l], w_out[l], shift_mu[l], w0[l], w2[l], a0[l], a2[l], g2[l], k_k[l], k_a[l], r_k[l],
              gn_g[l], gn_b[l], ln1_g[l], ln1_b[l], ln2_g[l], ln2_b[l], w_up[l], conv_w[l], conv_b[l], w_down[l])
        yp, k_l, v_l, wkv_l, z_l, c_l = trunk_layer(
            yp, pos_p, moba_prompt,
            jnp.zeros((B, RWKV_PROJ), x_prompt.dtype),
            jnp.zeros((B, N_RWKV_HEADS, HEAD_DIM, HEAD_DIM), state_wkv.dtype),
            jnp.zeros((B, CONV_W - 1, D_FF), x_prompt.dtype), lw)
        kp.append(k_l); vp.append(v_l); wp.append(wkv_l); zp.append(z_l); cp.append(c_l)
        sample_attend = functools.partial(moba_decode, cache_k=cache_k[l], cache_v=cache_v[l], page_table=page_table)
        ys, k_l, v_l, wkv_l, z_l, c_l = trunk_layer(
            ys, pos_s, sample_attend, state_shift[l], state_wkv[l], state_conv[l], lw)
        kq.append(k_l); vq.append(v_l); wq.append(wkv_l); zq.append(z_l); cq.append(c_l)
    k_prompt = jnp.stack(kp)
    v_prompt = jnp.stack(vp)
    wkv_prompt = jnp.stack(wp)
    shift_prompt = jnp.stack(zp)
    conv_prompt = jnp.stack(cp)
    k_sample = jnp.stack(kq)
    v_sample = jnp.stack(vq)
    wkv_sample = jnp.stack(wq)
    shift_sample = jnp.stack(zq)
    conv_sample = jnp.stack(cq)
    return (yp, ys, k_prompt, v_prompt, wkv_prompt, shift_prompt, conv_prompt,
            k_sample, v_sample, wkv_sample, shift_sample, conv_sample)


_drawn_inputs = setup_inputs


def setup_inputs(seed=0):
    import zlib

    import numpy as np

    out = dict(_drawn_inputs(seed))
    spreads = {}
    factors = {'cache_k': 2.746,
     'w2': 8.0,
     'gn_g': 5.784,
     'gn_b': 45.388,
     'ln1_b': 5.435,
     'ln2_b': 5.674,
     'conv_b': 8.0}
    for name, (base, spread) in spreads.items():
        noise = np.random.default_rng([zlib.crc32(name.encode()), seed]).standard_normal(out[name].shape)
        drawn = base * np.exp(spread * noise) if base else spread * noise
        out[name] = jnp.asarray(drawn.astype(out[name].dtype))
    for name, factor in factors.items():
        out[name] = (out[name] * factor).astype(out[name].dtype)
    return out
```

```python
import math
from contextlib import ExitStack

import numpy as np
import concourse.bass as bass
from concourse import mybir

F32 = mybir.dt.float32
I32 = mybir.dt.int32
ALU = mybir.AluOpType
ACT = mybir.ActivationFunctionType
AX = mybir.AxisListType.X

P = 128
D_MODEL = 2048
SEQ = 512
DEC_BATCH = 8
DEC_SEQ = 4
PAST_LEN = 4096
PAGE = 128
HD = 64
N_PAGES = PAST_LEN // PAGE
N_DEC = DEC_BATCH * DEC_SEQ
TOK = SEQ + N_DEC
HALF = TOK // 2
KT = D_MODEL // P
RW_PROJ = 3360
IN_WIDTH = 1536 + RW_PROJ
ATT_TILES = 12
IN_TILES = 39
RW_TILES = IN_TILES - ATT_TILES
LAST_W = IN_WIDTH - (IN_TILES - 1) * P
D_FF = 5632
FT = D_FF // P
SLOTS = 4
DOWN_K = FT // SLOTS
LN_EPS = 1e-5
GN_EPS = 64e-5
NEG = -1e30
ALPHA = 2.0 ** 0.25
DECAY_SCALE = -math.exp(-0.5)
CHUNK = 64
N_CHUNK = SEQ // CHUNK
PAIRS = 8
SCALE = HD ** -0.5

CONST_PARTS = [("ident", 128), ("swap", 128), ("rot", 128), ("headsum", 128), ("ones", 128),
               ("low8", 128), ("lowoff", 128), ("up8", 128), ("up", 128), ("upinc", 128),
               ("causal", 128), ("seg", 512), ("cos", TOK), ("sin", TOK), ("before", 256), ("own", 128)]
CONST_AT = {}
CONST_W = 0
for _n, _w in CONST_PARTS:
    CONST_AT[_n] = (CONST_W, _w)
    CONST_W += _w

VEC_ROWS = [[("shift_mu", 27), ("w0", 8), ("a0", 8), ("k_k", 8), ("k_a", 8), ("r_k", 8), ("gn_g", 8), ("gn_b", 8)],
            [("ln1_g", 16), ("ln1_b", 16), ("ln2_g", 16), ("ln2_b", 16)],
            [("conv0", 44), ("conv1", 44)],
            [("conv2", 44), ("conv_b", 44)]]
VEC_AT = {}
for _t, _rows in enumerate(VEC_ROWS):
    _r = 0
    for _n, _k in _rows:
        VEC_AT[_n] = _t * P + _r
        _r += _k


def constants():
    c = np.zeros((P, CONST_W), np.float32)
    part = lambda n: c[:, CONST_AT[n][0]:CONST_AT[n][0] + CONST_AT[n][1]]
    i = np.arange(P)
    part("ident")[:] = np.eye(P)
    part("swap")[i, (i + 64) % P] = 1.0
    for h in (0, 64):
        for d in range(8):
            part("rot")[h + d + 8, h + d] = -1.0
            part("rot")[h + d, h + d + 8] = 1.0
    same = (i[:, None] // 64) == (i[None, :] // 64)
    part("headsum")[:] = same
    part("ones")[:] = 1.0
    block = (i[:, None] // 8) == (i[None, :] // 8)
    part("low8")[:] = same & block & (i[:, None] > i[None, :])
    part("lowoff")[:] = same & ~block & (i[:, None] > i[None, :])
    part("up8")[:] = same & block & (i[:, None] < i[None, :])
    part("up")[:] = same & (i[:, None] < i[None, :])
    part("upinc")[:] = same & (i[:, None] <= i[None, :])
    part("causal")[:] = np.where(i[None, :] <= i[:, None], 0.0, NEG)
    part("seg")[:] = (np.arange(SEQ) % CHUNK != 0)[None, :]
    inv = np.power(np.float32(500000.0), -(np.arange(8, dtype=np.float32) * np.float32(2.0) / np.float32(16)))
    pos = np.concatenate([np.arange(SEQ), np.tile(PAST_LEN + np.arange(DEC_SEQ), DEC_BATCH)]).astype(np.float32)
    ang = pos[None, :] * inv.astype(np.float32)[:, None]
    part("cos")[:] = 1.0
    for h in (0, 8, 64, 72):
        part("cos")[h:h + 8] = np.cos(ang)
        part("sin")[h:h + 8] = np.sin(ang)
    b = np.arange(16)
    part("before")[:] = (b[None, :] < b[:, None]).astype(np.float32).reshape(1, 256)
    q_t = (i % 16) // 4
    n = np.arange(N_DEC)
    for bp in range(4):
        mine = (n[None, :] // 4 == 2 * bp + i[:, None] // 64) & (n[None, :] % 4 <= q_t[:, None])
        part("own")[:, bp * N_DEC:(bp + 1) * N_DEC] = np.where(mine, 0.0, NEG)
    return c


def hybrid_layer_kernel(nc, x_prompt, x_sample, cache_k, cache_v, page_table, state_wkv, state_shift, state_conv,
                        w_in, w_out, shift_mu, w0, w2, a0, a2, g2, k_k, k_a, r_k, gn_g, gn_b,
                        ln1_g, ln1_b, ln2_g, ln2_b, w_up, conv_w, conv_b, w_down, consts,
                        y_prompt, y_sample, k_prompt, v_prompt, wkv_prompt, shift_prompt, conv_prompt,
                        k_sample, v_sample, wkv_sample, shift_sample, conv_sample, stop_at=99):
    ctx = ExitStack()
    with ctx:
        def sb(name, shape, dt=F32):
            return ctx.enter_context(nc.sbuf_tensor(name, shape, dt))

        def sem(name):
            return ctx.enter_context(nc.semaphore(name))

        XT = sb("XT", [P, KT, TOK])
        W = sb("W", [P, SLOTS, KT * P])
        BIG = sb("BIG", [P, FT * TOK])
        C = sb("C", [P, CONST_W])
        VC = sb("VC", [P, 4 * P])
        ps = ctx.enter_context(nc.psum_tensor("ps", [P, 8, 512], F32))
        shiftT = sb("shiftT", [P, RW_TILES, DEC_BATCH])
        convT = sb("convT", [P, FT, 2 * DEC_BATCH])
        WORK = sb("WORK", [P, 5120])

        def const(name):
            a, n = CONST_AT[name]
            return C[:, a:a + n]
        ident = const("ident")
        ZT = BIG[:, 0:IN_TILES * TOK].rearrange("p (m t) -> p m t", t=TOK)
        x_tok = BIG[:, 0:5 * D_MODEL].rearrange("p (a n) -> p a n", n=D_MODEL)
        shift_tok = BIG[0:DEC_BATCH, 10240:10240 + 27 * P]
        conv_tok = BIG[0:16, 13824:13824 + D_FF]
        vec_tok = BIG[:, 19456:19456 + 4 * P].rearrange("p (a n) -> p a n", n=P)
        last_tok = WORK[0:33, 0:RW_TILES * P]

        free_areas = [[BIG, 0, ATT_TILES * TOK], [BIG, IN_TILES * TOK, FT * TOK], [W[:, :, :].rearrange("p a n -> p (a n)"), 0, SLOTS * KT * P],
                      [WORK, 0, 5120]]

        def carve(*shape):
            n = math.prod(shape)
            for area in free_areas:
                if area[2] - area[1] >= n:
                    area[1] += n
                    view = area[0][:, area[1] - n:area[1]]
                    if len(shape) > 1:
                        names = "abcd"[:len(shape)]
                        view = view.rearrange(f"p ({' '.join(names)}) -> p {' '.join(names)}", **dict(zip(names, shape)))
                    return view
            raise ValueError(f"no room for {shape}")

        HC = N_CHUNK // 2
        SC = 2
        D3 = BIG[:, 0:8 * TOK].rearrange("p (m t) -> p m t", t=TOK)
        LD, LC, AA, KK, SQ, PX, PY, PN, BON, G = [carve(TOK) for _ in range(10)]
        AB = AA
        LW = carve(3, P)
        AR = carve(HC, 2, P)
        BB, KB, VB = carve(HC, P), carve(HC, P), carve(HC, P)
        Nd, NdT, Lo, AKT, RKT, N4, P1T, P2T, P3T, M4T, GT, R2 = [[carve(SC, P) for _ in range(2)] for _ in range(12)]
        BR, NN, MM, M2, Bx, By, KV = [[carve(2 * SC, P) for _ in range(2)] for _ in range(7)]
        BR = [x.rearrange("p (c w) n -> p c w n", w=2) for x in BR]
        Bx = [x.rearrange("p (c w) n -> p c w n", w=2) for x in Bx]
        By = [x.rearrange("p (c w) n -> p c w n", w=2) for x in By]
        ST = [carve(P), carve(P)]
        WKV = carve(P)
        SVT = sb("SVT", [P, 6, P])

        wt = [W[:, u, :].rearrange("p (k n) -> p k n", n=P) for u in range(SLOTS)]
        win_v = w_in[0].rearrange("(k p) n -> p k n", p=P)

        x_in = sem("x_in")
        consts_in, small_in = sem("consts_in"), sem("small_in")
        pads_zero = sem("pads_zero")
        w_landed = [sem(f"w_landed{u}") for u in range(SLOTS)]
        w_free = [sem(f"w_free{u}") for u in range(SLOTS)]
        acc_free = sem("acc_free")
        xt_mm, xt_ev, xt_ev_b = sem("xt_mm"), sem("xt_ev"), sem("xt_ev_b")
        small_mm, small_ev = sem("small_mm"), sem("small_ev")
        last_mm, last_ev = sem("last_mm"), sem("last_ev")
        stored = sem("stored")
        n_stored = [0]
        STEPS = {"solve_dve": ["p2", "p3", "b0", "b1", "b2", "b3", "g"], "solve_pe": ["s3", "n4", "p3", "m", "m2", "m4", "b3", "g"],
                 "solve_act": ["m", "m2", "m4"]}

        def after(name, step, n, s):
            return (n - 1 - s) * len(STEPS[name]) + 2 * STEPS[name].index(step) + s + 1
        shifted, lora_act = sem("shifted"), sem("lora_act")
        names = ("lw_landed lora_mm lora_ev exp_ev ld_ready lprev_ready kk_raw sq_ready ss_mm ss_root "
                 "bonus_in bonus_mm bonus_ev ab_ready sv_mm sv_ev sv_out "
                 "solve_dve solve_pe solve_act bd_dve bd_pool bd_act tok_mm tok_ev gram_mm gram_ev s3_ev "
                 "chain_mm chain_ev o_ev o_mm "
                 "wkv_mm wkv_ev pair_pool rw_chain bd_zero")
        S = {n: sem(n) for n in names.split()}
        names = ("sv_in state_in state_out dec_o dec_o_in rec rec_half ot_mm ot_ev "
                 "gn_mu_mm gn_sq gn_var_mm gn_root gn_ev rot_mm rope_ev rope_chain kvt_mm kvt_ev swap_mm kdup_ev qsw_ev qbd_zero qbd_ev kvt_out "
                 "stat_copy sc_mm mask_ev max_ev pexp_ev pnorm_ev pt_mm pt_ev ao_mm ao_ev att_chain "
                 "page_in kt_ev_a kt_ev_d qk_mm sc_ev soft_ev pexpd_ev ptd_mm ptd_ev pv_mm oq_ev oqt_mm of_ev osw_mm dec_ev dec_chain qb_ev gate_chain gn_chain")
        S.update({n: sem(n) for n in names.split()})
        names = ("ln_mu_mm ln_sub ln_sq ln_var_mm ln_root ln_rs ln_scaled ln_ev gp_hist gp_zero gate_ev conv_chain conv_ev silu_ev h_ev "
                 "cvn_ev cn_mm cn_ev y_mm y_ev y_out")
        S.update({n: sem(n) for n in names.split()})
        page_landed = [sem(f"page_landed{j}") for j in range(8)]
        page_free = [sem(f"page_free{j}") for j in range(8)]
        shift_chain = sem("shift_chain")
        dec_vecs = nc.dram_tensor("dec_vecs", (6, N_DEC, 1024), F32).ap()
        SVT6 = sb("SVT6", [P, 6 * N_DEC])
        HB = sb("HB", [P, 16])
        dec_out = nc.dram_tensor("dec_out", (N_DEC, 1024), F32).ap()
        pages = sb("pages", [1, DEC_BATCH * N_PAGES], I32)
        eps = sb("eps", [P, 2])
        SV = WORK[:, 0:1536].rearrange("p (v t j) -> p v t j", v=6, j=HD)
        SD = WORK[:, 1536:3584].rearrange("p (i j) -> p i j", j=HD)
        OD = WORK[:, 3584:3840].rearrange("p (t i) -> p t i", i=HD)
        SA = WORK[:, 3840:3872]
        E0 = IN_TILES * TOK
        TD = BIG[:, E0:E0 + 2048].rearrange("p (i j) -> p i j", j=HD)
        o_tok = BIG[0:N_DEC, E0:E0 + 1024]
        XC = WORK[:, 3872:3872 + TOK]
        XS = WORK[:, 4416:4416 + TOK]
        F0 = 20 * TOK
        RT = BIG[:, F0:F0 + TOK]
        KVT = WORK[:, 0:2560].rearrange("p (a n) -> p a n", n=512)
        QBD = WORK[:, 2560:3072].rearrange("p (r b q) -> p r b q", r=2, b=DEC_BATCH)
        QSW = WORK[:, 3072:3328].rearrange("p (f n) -> p f n", n=N_DEC)
        KDUP = BIG[:, F0:F0 + 2048].rearrange("p (v t) -> p v t", t=SEQ)
        KC = BIG[:, F0 + 2048:F0 + 2560]
        Q2 = BIG[:, F0 + 2560:F0 + 3584].rearrange("p (f t) -> p f t", t=SEQ)
        VS = BIG[:, F0 + 3584:F0 + 3840].rearrange("p (a d) -> p a d", d=HD)
        PR = [BIG[:, F0 + 3840 + 1280 * j:F0 + 5120 + 1280 * j] for j in range(2)]
        PT = [BIG[:, F0 + 6400 + 1280 * j:F0 + 7680 + 1280 * j] for j in range(2)]
        STAT = WORK[:, 3328:3392].rearrange("p (j k) -> p j k", k=4)
        W2D = W[:, :, :].rearrange("p a n -> p (a n)")
        pg = [W2D[:, 1024 * j:1024 * (j + 1)].rearrange("p (g n) -> p g n", n=256) for j in range(8)]
        SC_W = PAST_LEN + N_DEC
        SCR = BIG[:, F0:F0 + SC_W]
        KTD = [[BIG[:, F0 + 4160 + 1024 * (2 * j + b):F0 + 5184 + 1024 * (2 * j + b)].rearrange("p (r n) -> p r n", n=512)
                for b in range(2)] for j in range(2)]
        PTD = [BIG[:, F0 + 8256 + 512 * j:F0 + 8768 + 512 * j] for j in range(2)]
        PTO = BIG[:, F0 + 9280:F0 + 9408]
        OQ = BIG[:, F0 + 9408:F0 + 9536]
        OF = BIG[:, F0 + 9536:F0 + 9664]
        DS = BIG[:, F0 + 9664:F0 + 9792]
        RK = BIG[:, E0:E0 + 512].rearrange("p (c i j) -> p c i j", c=2, j=16)
        QB = BIG[:, E0 + 512:E0 + 640].rearrange("p (r b q) -> p r b q", r=2, b=2)
        ATT = BIG[:, 0:8 * TOK].rearrange("p (f t) -> p f t", t=TOK)
        HT = BIG[:, :].rearrange("p (f t) -> p f t", t=TOK)
        GPW = SEQ + 2 + DEC_BATCH * (DEC_SEQ + 2)
        GP = [WORK[:, GPW * j:GPW * (j + 1)] for j in range(2)]
        CO = [WORK[:, 2 * GPW + (GPW - 2) * j:2 * GPW + (GPW - 2) * (j + 1)] for j in range(2)]
        co_dec = [WORK[:, 2 * GPW + (GPW - 2) * j + SEQ + 2:2 * GPW + (GPW - 2) * j + SEQ + 2 + 6 * DEC_BATCH]
                  .rearrange("p (b t) -> p b t", t=DEC_SEQ + 2)[:, :, 0:DEC_SEQ] for j in range(2)]
        CVN = WORK[:, 2244:2244 + FT * 18].rearrange("p (f n) -> p f n", n=18)
        LQ = [WORK[:, 3040 + TOK * j:3040 + TOK * (j + 1)] for j in range(2)]
        RS = WORK[:, 4128:4128 + TOK]
        Y = [BIG[:, 2048 * j:2048 * (j + 1)] for j in range(5)]
        CN = BIG[0:18, 10240:10240 + D_FF]
        ROUND_OUT = [10, 10, 10, 9]
        ROUND_UP = [r + 4 for r in ROUND_OUT]
        ROUND_DOWN = [r + 22 for r in ROUND_UP]
        wout_v = w_out[0].rearrange("(k p) n -> p k n", p=P)
        wup_v = w_up[0].rearrange("(k p) n -> p k n", p=P)
        wdown_v = w_down[0].rearrange("(k p) n -> p k n", p=P)

        ck = cache_k[0].rearrange("g p v d -> g p (v d)")
        cv = cache_v[0].rearrange("g p v d -> g p (v d)")

        def load_pages(eng, b):
            eng.wait_ge(S["page_in"], 16)
            for u in range(SLOTS):
                eng.wait_ge(w_free[u], (7 if u < 3 else 6) + 4)
            with eng.Fori(0, 4) as bp:
                for kind, cache in enumerate((ck, cv)):
                    with eng.Fori(0, 2) as r:
                        for c in range(4):
                            j = 2 * c + b
                            eng.wait_ge(page_free[j], 4 * bp + 2 * kind + r + 1)
                            for g in range(4):
                                row = eng.value_load(pages[0:1, bass.ds((2 * bp + b) * N_PAGES + r * 16 + c * 4 + g, 1)])
                                eng.dma_start(pg[j][:, g], cache[bass.ds(row, 1)].rearrange("a p n -> (a p) n")).then_inc(page_landed[j], 16)

        block = ctx.enter_context(nc.Block())

        st_v = state_wkv[0].rearrange("b h i j -> (b h) i j")
        wst_v = wkv_sample[0].rearrange("b h i j -> (b h) i j")

        @block.sync
        def _(sp):
            sp.dma_start(C[:, :], consts).then_inc(consts_in, 16)
            for a in range(4):
                sp.dma_start(x_tok[:, a], x_prompt[0, a * P:(a + 1) * P, :]).then_inc(x_in, 16)
            sp.dma_start(x_tok[0:N_DEC, 4], x_sample.rearrange("b t n -> (b t) n")).then_inc(x_in, 16)
            def load_in(tile, u, rnd, width=P):
                sp.wait_ge(w_free[u], rnd + 1)
                sp.dma_start(wt[u][:, :, 0:width], win_v[:, :, bass.ds(tile * P, width)]).then_inc(w_landed[u], 16)
            sp.wait_ge(pads_zero, 2)
            sp.dma_start(shift_tok[:, 0:RW_PROJ], state_shift[0]).then_inc(small_in, 16)
            sp.dma_start(conv_tok, state_conv[0].rearrange("b r n -> (b r) n")).then_inc(small_in, 16)
            full = 26 * P
            sp.dma_start(vec_tok[0:26, 0], shift_mu[0, 0:full].rearrange("(r n) -> r n", n=P)).then_inc(small_in, 16)
            sp.dma_start(vec_tok[26:27, 0, 0:32], shift_mu[0:1, full:RW_PROJ]).then_inc(small_in, 16)
            for name, src in (("w0", w0), ("a0", a0), ("k_k", k_k), ("k_a", k_a), ("r_k", r_k), ("gn_g", gn_g),
                              ("gn_b", gn_b), ("ln1_g", ln1_g), ("ln1_b", ln1_b), ("ln2_g", ln2_g),
                              ("ln2_b", ln2_b), ("conv_b", conv_b)):
                t, r = divmod(VEC_AT[name], P)
                n = src.shape[1] // P
                sp.dma_start(vec_tok[r:r + n, t], src[0].rearrange("(r n) -> r n", n=P)).then_inc(small_in, 16)
            for j in range(3):
                t, r = divmod(VEC_AT[f"conv{j}"], P)
                sp.dma_start(vec_tok[r:r + FT, t], conv_w[0, j].rearrange("(r n) -> r n", n=P)).then_inc(small_in, 16)
            SMALL = 19
            with sp.Fori(0, 6) as i:
                for u in range(SLOTS):
                    load_in(ATT_TILES + i * SLOTS + u, u, i)
            for u in range(3):
                load_in(ATT_TILES + 24 + u, u, 6, P if u < 2 else LAST_W)
            sp.wait_ge(last_ev, 7)
            sp.dma_start(shift_prompt[0], last_tok[0:1, 0:RW_PROJ]).then_inc(stored, 16)
            for b in range(DEC_BATCH):
                r = 1 + b * DEC_SEQ + DEC_SEQ - 1
                sp.dma_start(shift_sample[0, b:b + 1], last_tok[r:r + 1, 0:RW_PROJ]).then_inc(stored, 16)
            RWS = 9
            with sp.Fori(0, PAIRS) as p:
                sp.wait_ge(S["lora_mm"], p + 1)
                cols = bass.ds(p * P, P)
                for dst, src in ((LW[0:64, 0], w2[0, :, cols]), (LW[64:128, 0], a2[0, :, cols]),
                                 (LW[:, 1], g2[0, 0:P, cols]), (LW[0:32, 2], g2[0, P:160, cols])):
                    sp.dma_start(dst, src).then_inc(S["lw_landed"], 16)
                sp.wait_ge(S["sv_ev"], p + 1)
                sp.dma_start(dec_vecs[:, :, cols].rearrange("v t n -> t v n"), SVT[0:N_DEC]).then_inc(S["sv_out"], 16)
                sp.wait_ge(S["wkv_ev"], p + 1)
                for e in range(2):
                    sp.dma_start(wkv_prompt[0, 0, bass.ds(p * 2 + e, 1)].rearrange("h i j -> (h i) j"),
                                 WKV[e * 64:e * 64 + 64, e * 64:e * 64 + 64]).then_inc(stored, 16)
            sp.dma_start(pages[0:1, :], page_table.rearrange("(o b) n -> o (b n)", o=1)).then_inc(S["page_in"], 16)
            sp.wait_ge(S["pair_pool"], PAIRS + 1)
            for i in range(3):
                for u in range(SLOTS):
                    load_in(i * SLOTS + u, u, (7 if u < 3 else 6) + i)
                if i == 0:
                    sp.wait_ge(S["sv_out"], 16 * PAIRS + 16)
                    for v in range(6):
                        for b in range(DEC_BATCH):
                            sp.dma_start(SV[b * 16:b * 16 + 16, v], dec_vecs[v, b * DEC_SEQ:(b + 1) * DEC_SEQ].rearrange("t (h j) -> h t j", j=HD)).then_inc(S["sv_in"], 16)
                    sp.dma_start(SD, st_v[:, 0:32]).then_inc(S["state_in"], 16)
            sp.wait_ge(S["rec_half"], 1)
            sp.dma_start(wst_v[:, 0:32], SD).then_inc(S["state_out"], 16)
            sp.wait_ge(S["state_out"], 16)
            sp.dma_start(SD, st_v[:, 32:64]).then_inc(S["state_in"], 16)
            sp.wait_ge(S["rec_half"], 2)
            sp.dma_start(wst_v[:, 32:64], SD).then_inc(S["state_out"], 16)
            for b in range(DEC_BATCH):
                sp.dma_start(dec_out[b * DEC_SEQ:(b + 1) * DEC_SEQ].rearrange("t (h i) -> h t i", i=HD), OD[b * 16:b * 16 + 16]).then_inc(S["dec_o"], 16)
            sp.wait_ge(S["dec_o"], 16 * DEC_BATCH)
            sp.dma_start(o_tok, dec_out).then_inc(S["dec_o_in"], 16)
            sp.wait_ge(S["kvt_ev"], 5)
            for a in range(4):
                for dst, at in ((k_prompt, 0), (v_prompt, 256)):
                    sp.dma_start(dst[0, 0, a * P:(a + 1) * P].rearrange("t v d -> t (v d)"), KVT[:, a, at:at + 256]).then_inc(S["kvt_out"], 16)
            for dst, at in ((k_sample, 0), (v_sample, 256)):
                sp.dma_start(dst[0].rearrange("b t v d -> (b t) (v d)"), KVT[0:N_DEC, 4, at:at + 256]).then_inc(S["kvt_out"], 16)
            load_pages(sp, 0)
            for j in range(8):
                sp.wait_ge(page_free[j], 17)

            def load(u, rnd, src):
                sp.wait_ge(w_free[u], rnd + 1)
                sp.dma_start(wt[u][:, 0:src.shape[1], :], src).then_inc(w_landed[u], 16)
            with sp.Fori(0, 4) as i:
                for u in range(SLOTS):
                    load(u, ROUND_OUT[u] + i, wout_v[:, :, bass.ds((4 * i + u) * P, P)])
            with sp.Fori(0, FT // 2) as i:
                for u in range(SLOTS):
                    load(u, ROUND_UP[u] + i, wup_v[:, :, bass.ds((2 * i + u // 2) * P + (u % 2) * D_FF, P)])
            with sp.Fori(0, KT) as m:
                for u in range(SLOTS):
                    load(u, ROUND_DOWN[u] + m, wdown_v[:, u * DOWN_K:(u + 1) * DOWN_K, bass.ds(m * P, P)])
            sp.wait_ge(S["cn_ev"], 11)
            sp.dma_start(conv_prompt[0, 0], CN[0:2]).then_inc(S["kvt_out"], 16)
            sp.dma_start(conv_sample[0].rearrange("b r n -> (b r) n"), CN[2:18]).then_inc(S["kvt_out"], 16)
            for a in range(5):
                sp.wait_ge(S["y_ev"], 4 * a + 4)
                if a < 4:
                    sp.dma_start(y_prompt[0, a * P:(a + 1) * P], Y[a]).then_inc(S["y_out"], 16)
                else:
                    sp.dma_start(y_sample.rearrange("b t n -> (b t) n"), Y[4][0:N_DEC]).then_inc(S["y_out"], 16)
            sp.wait_ge(stored, 9 * 16 + 32 * PAIRS)
            sp.wait_ge(S["state_out"], 32)
            sp.wait_ge(S["kvt_out"], 192)
            sp.wait_ge(S["y_out"], 80)

        @block.tensor
        def _(pe):
            for u in range(SLOTS):
                pe.sem_inc(w_free[u], 1)
            pe.wait_ge(consts_in, 16)
            for k in range(KT):
                b0 = 2 * (k % 4)
                if k == 0:
                    pe.wait_ge(x_in, 80)
                if k >= 4:
                    pe.wait_ge(xt_ev, k - 3)
                    pe.wait_ge(xt_ev_b, k - 3)
                for a in range(4):
                    nc.tensor.transpose(ps[:, b0, a * P:(a + 1) * P], x_tok[:, a, k * P:(k + 1) * P], ident)
                nc.tensor.transpose(ps[:, b0 + 1, 0:N_DEC], x_tok[0:N_DEC, 4, k * P:(k + 1) * P],
                                    ident[0:N_DEC, 0:N_DEC]).then_inc(xt_mm, 1)
            pe.wait_ge(small_in, 19 * 16)
            pe.wait_ge(xt_ev, KT)
            pe.wait_ge(xt_ev_b, KT)
            for t in range(4):
                n = sum(k for _, k in VEC_ROWS[t])
                nc.tensor.transpose(ps[:, 0, t * P:t * P + n], vec_tok[0:n, t], ident[0:n, 0:n])
            for m in range(RW_TILES):
                nc.tensor.transpose(ps[:, 1, m * 8:m * 8 + 8], shift_tok[:, m * P:(m + 1) * P], ident[0:8, 0:8])
            for f in range(FT):
                last = nc.tensor.transpose(ps[:, 2 + f // 32, (f % 32) * 16:(f % 32) * 16 + 16],
                                           conv_tok[:, f * P:(f + 1) * P], ident[0:16, 0:16])
            last.then_inc(small_mm, 1)
            pe.wait_ge(small_ev, 4)

            def dense(u, rnd, n, acc, width=P):
                pe.wait_ge(w_landed[u], (rnd + 1) * 16)
                pe.wait_ge(acc_free, n + 1)
                for k in range(KT):
                    for h in range(2):
                        last = nc.tensor.matmul(ps[0:width, 2 * acc + h, 0:HALF], wt[u][:, k, 0:width],
                                                XT[:, k, h * HALF:(h + 1) * HALF], start=k == 0, stop=k == KT - 1)
                last.then_inc(w_free[u], 1)

            with pe.Fori(0, 6) as i:
                for u in range(SLOTS):
                    dense(u, i, i * SLOTS + u, u % 2)
            for u in range(3):
                dense(u, 6, 24 + u, u % 2, P if u < 2 else LAST_W)
            pe.wait_ge(acc_free, RW_TILES + 2)
            for m in range(RW_TILES):
                w = P if m < RW_TILES - 1 else LAST_W
                bank = 4 + (m // 4) % 4
                if m // 4 >= 4:
                    pe.wait_ge(last_ev, m // 4 - 3)
                last = nc.tensor.transpose(ps[0:33, bank, (m % 4) * P:(m % 4) * P + w],
                                           ZT[0:w, ATT_TILES + m, SEQ - 1:TOK], ident[0:w, 0:w])
                if m % 4 == 3 or m == RW_TILES - 1:
                    last.then_inc(last_mm, 1)

            pe.sem_inc(S["lora_mm"], 1)
            pe.wait_ge(shifted, 1)
            pe.wait_ge(lora_act, 3)
            pe.wait_ge(S["bd_zero"], 6)
            headsum = const("headsum")
            BOTH = range(2)

            with pe.Fori(0, PAIRS) as p:
                pe.wait_ge(S["lw_landed"], 64 * p + 64)
                pe.wait_ge(S["pair_pool"], p + 1)
                for h in BOTH:
                    half = slice(h * HALF, (h + 1) * HALF)
                    nc.tensor.matmul(ps[:, 0 + h, 0:HALF], LW[0:64, 0], ZT[0:64, 36 + 0, half], start=True, stop=True)
                    nc.tensor.matmul(ps[:, 2 + h, 0:HALF], LW[64:128, 0], ZT[64:128, 36, half], start=True, stop=True)
                    nc.tensor.matmul(ps[:, 4 + h, 0:HALF], LW[:, 1], ZT[:, 37, half], start=True, stop=False)
                    last = nc.tensor.matmul(ps[:, 4 + h, 0:HALF], LW[0:32, 2], ZT[0:32, 38, half], start=False, stop=True)
                last.then_inc(S["lora_mm"], 1)
                pe.wait_ge(S["sq_ready"], p + 1)
                for h in BOTH:
                    last = nc.tensor.matmul(ps[:, 6 + h, 0:HALF], headsum, SQ[:, h * HALF:(h + 1) * HALF], start=True, stop=True)
                last.then_inc(S["ss_mm"], 1)
                pe.wait_ge(S["bonus_in"], p + 1)
                for h in BOTH:
                    last = nc.tensor.matmul(ps[:, 6 + h, 0:HALF], headsum, BON[:, h * HALF:(h + 1) * HALF], start=True, stop=True)
                last.then_inc(S["bonus_mm"], 1)
                pe.wait_ge(S["ab_ready"], p + 1)
                pe.wait_ge(S["exp_ev"], 4 * p + 4)
                rz, kz, vz = (ZT[:, bass.ds(ATT_TILES + 8 * j + p, 1), SEQ:TOK].rearrange("p a t -> p (a t)") for j in range(3))
                for j in range(6):
                    src = SVT6[:, j * N_DEC:(j + 1) * N_DEC]
                    last = nc.tensor.transpose(ps[0:N_DEC, j // 4, (j % 4) * P:(j % 4) * P + P], src, ident)
                last.then_inc(S["sv_mm"], 1)
                pe.wait_ge(S["sv_ev"], p + 1)
                for h in BOTH:
                    hp = 2 * p + h
                    pe.wait_ge(S["bd_dve"], hp + 1)
                    pe.wait_ge(S["bd_pool"], hp + 1)
                    pe.wait_ge(S["bd_act"], hp + 1)
                    pe.wait_ge(S["bonus_ev"], p + 1)
                    pe.wait_ge(S["lora_ev"], 3 * p + 3)
                    for s in BOTH:
                        if h or s:
                            pe.wait_ge(S["tok_ev"], 3 * (4 * p + 2 * h + s))
                        if h and not s:
                            pe.wait_ge(S["chain_ev"], 8 * p + 5)
                            pe.wait_ge(S["o_ev"], 8 * p + 4)
                        for c in range(SC):
                            for j, src in enumerate((AR[:, s * SC + c, 0], BB[:, s * SC + c])):
                                nc.tensor.transpose(ps[:, 6, (j * SC + c) * P:(j * SC + c + 1) * P], src, ident)
                            for j, src in enumerate((KB[:, s * SC + c], VB[:, s * SC + c])):
                                last = nc.tensor.transpose(ps[:, 7, (j * SC + c) * P:(j * SC + c + 1) * P], src, ident)
                        last.then_inc(S["tok_mm"], 1)
                        for c in range(SC):
                            x = s * SC + c
                            nc.tensor.matmul(ps[:, 3 * s, c * 256:(c + 1) * 256], BB[:, x], AR[:, x], start=True, stop=True)
                            nc.tensor.matmul(ps[:, 3 * s + 1, c * 256:(c + 1) * 256], KB[:, x], AR[:, x], start=True, stop=True)
                            last = nc.tensor.matmul(ps[:, 3 * s + 2, c * P:(c + 1) * P], AR[:, x, 0], BB[:, x], start=True, stop=True)
                        last.then_inc(S["gram_mm"], 1)

                    def products(s, items):
                        for c in range(SC):
                            for bank, at, width, lhsT, rhs in items:
                                last = nc.tensor.matmul(ps[:, bank, at + c * width:at + (c + 1) * width], lhsT(c), rhs(c), start=True, stop=True)
                        last.then_inc(S["solve_pe"], 1)

                    for s in BOTH:
                        n = 4 * p + 2 * h + s + 1
                        pe.wait_ge(S["gram_ev"], 2 * n - 1)
                        pe.wait_ge(S["tok_ev"], 3 * n)
                        products(s, [(3 * s, 0, P, lambda c: NdT[s][:, c], lambda c: Nd[s][:, c]),
                                              (3 * s, 256, P, lambda c: Nd[s][:, c], lambda c: NdT[s][:, c]),
                                              (3 * s + 1, 0, P, lambda c: AKT[s][:, c], lambda c: KV[s][:, SC + c])])
                    for s in BOTH:
                        n = 4 * p + 2 * h + s + 1
                        pe.wait_ge(S["s3_ev"], 2 * n)
                        pe.wait_ge(S["gram_ev"], 2 * n)
                        products(s, [(3 * s + 2, 0, P, lambda c: NN[s][:, SC + c], lambda c: NN[s][:, c]),
                                              (3 * s + 2, 256, P, lambda c: NN[s][:, c], lambda c: P1T[s][:, c])])
                    for s in BOTH:
                        n = 4 * p + 2 * h + s + 1
                        pe.wait_ge(S["solve_dve"], after("solve_dve", "p2", n, s))
                        products(s, [(3 * s, 0, P, lambda c: N4[s][:, c], lambda c: P2T[s][:, c])])
                    for s in BOTH:
                        n = 4 * p + 2 * h + s + 1
                        pe.wait_ge(S["solve_dve"], after("solve_dve", "p3", n, s))
                        products(s, [(3 * s + 1, 0, P, lambda c: P3T[s][:, c], lambda c: Lo[s][:, c]),
                                             (3 * s + 1, 256, P, lambda c: Lo[s][:, c], lambda c: P3T[s][:, c]),
                                             (3 * s + 2, 0, 256, lambda c: P3T[s][:, c], lambda c: Bx[s][:, c])])
                    for s in BOTH:
                        n = 4 * p + 2 * h + s + 1
                        pe.wait_ge(S["solve_act"], after("solve_act", "m", n, s))
                        pe.wait_ge(S["solve_dve"], after("solve_dve", "b0", n, s))
                        products(s, [(3 * s, 0, P, lambda c: MM[s][:, SC + c], lambda c: MM[s][:, c]),
                                              (3 * s, 256, P, lambda c: MM[s][:, c], lambda c: MM[s][:, SC + c]),
                                              (3 * s + 1, 0, 256, lambda c: MM[s][:, SC + c], lambda c: By[s][:, c])])
                    for s in BOTH:
                        n = 4 * p + 2 * h + s + 1
                        pe.wait_ge(S["solve_act"], after("solve_act", "m2", n, s))
                        pe.wait_ge(S["solve_dve"], after("solve_dve", "b1", n, s))
                        products(s, [(3 * s, 0, P, lambda c: M2[s][:, c], lambda c: M2[s][:, SC + c]),
                                              (3 * s + 2, 0, 256, lambda c: M2[s][:, SC + c], lambda c: Bx[s][:, c])])
                    for s in BOTH:
                        n = 4 * p + 2 * h + s + 1
                        pe.wait_ge(S["solve_act"], after("solve_act", "m4", n, s))
                        pe.wait_ge(S["solve_dve"], after("solve_dve", "b2", n, s))
                        products(s, [(3 * s + 1, 0, 256, lambda c: M4T[s][:, c], lambda c: By[s][:, c])])
                    for s in BOTH:
                        n = 4 * p + 2 * h + s + 1
                        pe.wait_ge(S["solve_dve"], after("solve_dve", "b3", n, s))
                        products(s, [(3 * s + 2, 0, 256, lambda c: Bx[s][:, c, 0], lambda c: BR[s][:, c])])
                    for s in BOTH:
                        n = 4 * p + 2 * h + s + 1
                        pe.wait_ge(S["solve_dve"], after("solve_dve", "g", n, s))
                        for c in range(SC):
                            x = s * SC + c
                            g = 4 * h + x
                            state, out = ps[:, 6 + g % 2, 0:P], ps[:, (0, 1, 3, 4)[x], 0:P]
                            if g:
                                pe.wait_ge(S["chain_ev"], 8 * p + g)
                            nc.tensor.matmul(state, BR[s][:, c, 0], Bx[s][:, c, 1], start=True, stop=False)
                            nc.tensor.matmul(state, KV[s][:, c], KV[s][:, SC + c], start=False, stop=False)
                            nc.tensor.matmul(out, Bx[s][:, c, 1], BR[s][:, c, 1], start=True, stop=False)
                            nc.tensor.matmul(out, KV[s][:, SC + c], RKT[s][:, c], start=False, stop=False)
                            pe.wait_ge(S["chain_ev"], 8 * p + g + 1)
                            if g == 0:
                                pe.wait_ge(S["ld_ready"], p + 1)
                            old = ST[g % 2]
                            nc.tensor.matmul(state, GT[s][:, c], old, start=False, stop=True).then_inc(S["chain_mm"], 1)
                            nc.tensor.matmul(out, old, R2[s][:, c], start=False, stop=True).then_inc(S["o_mm"], 1)
                pe.wait_ge(S["o_ev"], 8 * p + 8)
                pe.wait_ge(S["chain_ev"], 8 * p + 9)
                nc.tensor.transpose(ps[:, 0, 0:P], ST[0], ident).then_inc(S["wkv_mm"], 1)

            pe.wait_ge(S["pair_pool"], PAIRS + 1)
            pe.wait_ge(acc_free, RW_TILES + 2)
            for i in range(3):
                for u in range(SLOTS):
                    dense(u, (7 if u < 3 else 6) + i, RW_TILES + 4 * i + u, u % 2)
            for u in range(8):
                pe.sem_inc(page_free[u], 1)
            pe.wait_ge(S["dec_o_in"], 16)
            for f in range(8):
                last = nc.tensor.transpose(ps[:, 4, f * N_DEC:(f + 1) * N_DEC], o_tok[:, f * P:(f + 1) * P], ident[0:N_DEC, 0:N_DEC])
            last.then_inc(S["ot_mm"], 1)
            pe.wait_ge(S["ot_ev"], 1)
            pe.wait_ge(acc_free, RW_TILES + ATT_TILES + 2)
            with pe.Fori(0, PAIRS) as p:
                pe.wait_ge(S["gn_ev"], p + 1)
                for h in BOTH:
                    last = nc.tensor.matmul(ps[:, h, 0:HALF], headsum, ZT[:, bass.ds(ATT_TILES + p, 1), h * HALF:(h + 1) * HALF].rearrange("p a t -> p (a t)"), start=True, stop=True)
                last.then_inc(S["gn_mu_mm"], 1)
                pe.wait_ge(S["gn_sq"], p + 1)
                for h in BOTH:
                    last = nc.tensor.matmul(ps[:, 2 + h, 0:HALF], headsum, XS[:, h * HALF:(h + 1) * HALF], start=True, stop=True)
                last.then_inc(S["gn_var_mm"], 1)
            for m in range(10):
                b0 = 4 + 2 * (m % 2)
                if m >= 2:
                    pe.wait_ge(S["rope_ev"], m - 1)
                for h in BOTH:
                    last = nc.tensor.matmul(ps[:, b0 + h, 0:HALF], const("rot"), ZT[:, m, h * HALF:(h + 1) * HALF], start=True, stop=True)
                last.then_inc(S["rot_mm"], 1)
            pe.wait_ge(S["rope_ev"], 10)
            pe.wait_ge(S["gn_ev"], PAIRS + 1)
            for a in range(5):
                n = P if a < 4 else N_DEC
                for m in range(4):
                    last = nc.tensor.transpose(ps[0:n, a, m * P:(m + 1) * P], ZT[:, 8 + m, a * P:a * P + n], ident)
                last.then_inc(S["kvt_mm"], 1)
            for m in range(2):
                last = nc.tensor.matmul(ps[:, 5 + m, :], const("swap"), ZT[:, 8 + m, 0:SEQ], start=True, stop=True)
            last.then_inc(S["swap_mm"], 1)
            nc.tensor.matmul(ps[:, 7, 0:256], const("swap"), ZT[:, 0:8, SEQ:TOK], start=True, stop=True).then_inc(S["swap_mm"], 1)

            pe.wait_ge(S["kvt_ev"], 5)
            pe.wait_ge(S["kdup_ev"], 1)
            pe.wait_ge(S["qsw_ev"], 1)
            with pe.Fori(0, 4) as v:
                pe.wait_ge(S["stat_copy"], v + 1)

                def head_scores(hd):
                    f, e = divmod(hd, 2)
                    rows = slice(e * 64, e * 64 + 64)
                    pe.wait_ge(S["pexp_ev"], 4 * (4 * v + hd) + 4)
                    for i in range(4):
                        last = nc.tensor.matmul(ps[:, i, 0:(i + 1) * P], Q2[rows, f, i * P:(i + 1) * P], KC[rows, 0:(i + 1) * P], start=True, stop=True)
                        last.then_inc(S["sc_mm"], 1)
                head_scores(0)
                for hd in range(4):
                    f, e = divmod(hd, 2)
                    rows = slice(e * 64, e * 64 + 64)
                    n = 4 * v + hd
                    if hd < 3:
                        head_scores(hd + 1)
                    pe.wait_ge(S["pnorm_ev"], n + 1)
                    for a in range(4):
                        pe.wait_ge(S["pt_ev"], 4 * n + a + 2)
                        for i in range(a, 4):
                            off = i * (i + 1) // 2 * P
                            last = nc.tensor.transpose(ps[:, 4 + a % 3, (i - a) * P:(i - a + 1) * P], PR[hd % 2][:, off + a * P:off + (a + 1) * P], ident)
                        last.then_inc(S["pt_mm"], 1)
                    if e == 0:
                        pe.wait_ge(S["ao_ev"], 2 * v + f + 1)
                    for a in range(4):
                        pe.wait_ge(S["pt_ev"], 4 * n + a + 4)
                        toff = sum(4 - x for x in range(a)) * P
                        last = nc.tensor.matmul(ps[rows, 7, a * P:512], VS[:, a], PT[hd % 2][:, toff:toff + (4 - a) * P],
                                                start=a == 0, stop=a == 3, skip_group_check=True)
                    last.then_inc(S["ao_mm"], 1)

            pe.wait_ge(S["ao_ev"], 9)
            pe.wait_ge(S["qbd_ev"], 1)
            with pe.Fori(0, 4) as bp:
                pe.wait_ge(S["qb_ev"], bp + 1)
                pe.wait_ge(S["dec_ev"], bp + 1)
                qb = lambda r, b: QB[:, r, b]

                def scores(c):
                    n = 8 * bp + c
                    if c % 2 == 0:
                        pe.wait_ge(S["kt_ev_a"], n + 1)
                    else:
                        pe.wait_ge(S["kt_ev_a"], n + 1)
                    pe.wait_ge(S["kt_ev_d"], n + 1)
                    pe.wait_ge(S["sc_ev"], 2 * n + 2)
                    for b in BOTH:
                        for r in BOTH:
                            o = 32 * (2 * b + r)
                            last = nc.tensor.matmul(ps[o:o + 32, 4 + c % 2, :], qb(r, b), KTD[c % 2][b][:, r], start=True, stop=True,
                                                    skip_group_check=True)
                    last.then_inc(S["qk_mm"], 1)
                for c in range(8):
                    n = 8 * bp + c
                    for b in BOTH:
                        j = (2 * c + b) % 8
                        pe.wait_ge(page_landed[j], 64 * (4 * bp + c // 4) + 64)
                        if b == 0:
                            if c:
                                pe.wait_ge(S["kt_ev_a"], n)
                        else:
                            if c:
                                pe.wait_ge(S["kt_ev_d"], n)
                        for r in BOTH:
                            for g in range(4):
                                last = nc.tensor.transpose(ps[:, 2 * b + r, g * P:(g + 1) * P], pg[j][:, g, r * P:(r + 1) * P], ident)
                        last.then_inc(page_free[j], 1)
                    if c:
                        scores(c - 1)
                scores(7)
                pe.wait_ge(S["sc_ev"], 16 * bp + 16)
                for b in BOTH:
                    for r in BOTH:
                        o = 32 * (2 * b + r)
                        last = nc.tensor.matmul(ps[o:o + 32, 6, 0:N_DEC], qb(r, b), ZT[:, 8 + r, SEQ:TOK], start=True, stop=True, skip_group_check=True)
                last.then_inc(S["qk_mm"], 1)
                pe.wait_ge(S["pexpd_ev"], bp + 1)
                nc.tensor.transpose(ps[0:N_DEC, 6, 0:P], SCR[:, PAST_LEN:SC_W], ident).then_inc(S["ptd_mm"], 1)

                def values(c):
                    pe.wait_ge(S["ptd_ev"], 9 * bp + c + 2)
                    for b in BOTH:
                        j = (2 * c + b) % 8
                        pe.wait_ge(page_landed[j], 64 * (4 * bp + 2 + c // 4) + 64)
                        for r in BOTH:
                            o = 32 * (2 * b + r)
                            for g in range(4):
                                last = nc.tensor.matmul(ps[o:o + 32, 7, 0:P], PTD[c % 2][:, g * P + o:g * P + o + 32],
                                                        pg[j][:, g, r * P:(r + 1) * P], start=(c == 0 and g == 0), stop=False, skip_group_check=True)
                        last.then_inc(page_free[j], 1)
                for c in range(8):
                    if c >= 2:
                        pe.wait_ge(S["ptd_ev"], 9 * bp + c)
                    for g in range(4):
                        last = nc.tensor.transpose(ps[:, 4 + c % 2, g * P:(g + 1) * P], SCR[:, (4 * c + g) * P:(4 * c + g + 1) * P], ident)
                    last.then_inc(S["ptd_mm"], 1)
                    if c:
                        values(c - 1)
                values(7)
                for b in BOTH:
                    for r in BOTH:
                        o = 32 * (2 * b + r)
                        last = nc.tensor.matmul(ps[o:o + 32, 7, 0:P], PTO[0:N_DEC, o:o + 32], KVT[0:N_DEC, 4, 256 + r * P:256 + (r + 1) * P],
                                                start=False, stop=True, skip_group_check=True)
                last.then_inc(S["pv_mm"], 1)
                pe.wait_ge(S["oq_ev"], bp + 1)
                nc.tensor.transpose(ps[:, 0, 0:P], OQ, ident).then_inc(S["oqt_mm"], 1)
                pe.wait_ge(S["of_ev"], bp + 1)
                nc.tensor.matmul(ps[:, 1, 0:P], const("swap"), OF, start=True, stop=True).then_inc(S["osw_mm"], 1)

            pe.wait_ge(S["dec_ev"], 5)
            with pe.Fori(0, 4) as i:
                for u in range(SLOTS):
                    pe.wait_ge(w_landed[u], (ROUND_OUT[u] + i + 1) * 16)
                    pe.wait_ge(acc_free, IN_TILES + 4 * i + u + 1)
                    for k in range(KT):
                        for h in range(2):
                            last = nc.tensor.matmul(ps[:, 2 * (u % 2) + h, 0:HALF], wt[u][:, k], ZT[:, k if k < 8 else k + 4, h * HALF:(h + 1) * HALF],
                                                    start=k == 0, stop=k == KT - 1)
                    last.then_inc(w_free[u], 1)

            def layer_norm(which):
                for k in range(KT):
                    for h in range(2):
                        last = nc.tensor.matmul(ps[:, 4 + h, 0:HALF], const("ones"), XT[:, k, h * HALF:(h + 1) * HALF], start=k == 0, stop=k == KT - 1)
                last.then_inc(S["ln_mu_mm"], 1)
                for k in range(KT):
                    pe.wait_ge(S["ln_sq"], KT * which + k + 1)
                    for h in range(2):
                        last = nc.tensor.matmul(ps[:, 6 + h, 0:HALF], const("ones"), LQ[k % 2][:, h * HALF:(h + 1) * HALF], start=k == 0, stop=k == KT - 1)
                    last.then_inc(S["ln_var_mm"], 1)
            pe.wait_ge(acc_free, IN_TILES + KT + 2)
            layer_norm(0)
            pe.wait_ge(S["ln_root"], 1)

            def up_tile(u, rnd, f, b0, normed=False):
                pe.wait_ge(w_landed[u], (rnd + 1) * 16)
                pe.wait_ge(S["h_ev" if u % 2 else "gate_ev"], f + 1)
                for k in range(KT):
                    if normed:
                        pe.wait_ge(S["ln_ev"], k + 1)
                    for h in range(2):
                        last = nc.tensor.matmul(ps[:, b0 + 2 * (u % 2) + h, 0:HALF], wt[u][:, k], XT[:, k, h * HALF:(h + 1) * HALF],
                                                start=k == 0, stop=k == KT - 1)
                last.then_inc(w_free[u], 1)
            for u in range(SLOTS):
                up_tile(u, ROUND_UP[u], u // 2, 4 * (u // 2), u == 0)
            with pe.Fori(1, FT // 2) as i:
                for u in range(SLOTS):
                    up_tile(u, ROUND_UP[u] + i, 2 * i + u // 2, 4 * (u // 2))
            pe.wait_ge(S["h_ev"], FT + 2)
            with pe.Fori(0, KT // 2) as i:
                for m in range(2):
                    pe.wait_ge(acc_free, IN_TILES + KT + 2 * i + m + 1)
                    for u in range(SLOTS):
                        pe.wait_ge(w_landed[u], (ROUND_DOWN[u] + 2 * i + m + 1) * 16)
                        for k in range(DOWN_K):
                            for h in range(2):
                                last = nc.tensor.matmul(ps[:, 2 * m + h, 0:HALF], wt[u][:, k], HT[:, u * DOWN_K + k, h * HALF:(h + 1) * HALF],
                                                        start=u == 0 and k == 0, stop=u == SLOTS - 1 and k == DOWN_K - 1)
                        last.then_inc(w_free[u], 1)
            for g in range(11):
                if g >= 4:
                    pe.wait_ge(S["cn_ev"], g - 3)
                if g == 0:
                    pe.wait_ge(acc_free, IN_TILES + 2 * KT + 2)
                    pe.wait_ge(S["cvn_ev"], FT + 2)
                for j in range(4):
                    last = nc.tensor.transpose(ps[0:18, g % 4, j * P:(j + 1) * P], CVN[:, 4 * g + j], ident)
                last.then_inc(S["cn_mm"], 1)
            layer_norm(1)
            for a in range(5):
                n = P if a < 4 else N_DEC
                for q in range(4):
                    if a == 0:
                        pe.wait_ge(S["ln_ev"], KT + 4 * q + 4)
                        pe.wait_ge(S["cn_ev"], 11)
                    else:
                        pe.wait_ge(S["y_ev"], 4 * a - 3 + q)
                    for j in range(4):
                        last = nc.tensor.transpose(ps[0:n, q, j * P:(j + 1) * P], XT[:, 4 * q + j, a * P:a * P + n], ident)
                    last.then_inc(S["y_mm"], 1)

        @block.scalar
        def _(act):
            for k in range(KT):
                act.wait_ge(xt_mm, k + 1)
                nc.scalar.activation(XT[:, k, 0:SEQ], ps[:, 2 * (k % 4), :], ACT.Copy).then_inc(xt_ev, 1)
            act.sem_inc(acc_free, 2)

            def evac(u, rnd, tile, acc, width=P):
                act.wait_ge(w_free[u], rnd + 2)
                nc.scalar.activation(ZT[0:width, bass.ds(tile, 1), :].rearrange("p a (h t) -> p (a h) t", h=2),
                                     ps[0:width, 2 * acc:2 * acc + 2, 0:HALF], ACT.Copy).then_inc(acc_free, 1)
            with act.Fori(0, 6) as i:
                for u in range(SLOTS):
                    evac(u, i, ATT_TILES + i * SLOTS + u, u % 2)
            for u in range(3):
                evac(u, 6, ATT_TILES + 24 + u, u % 2, P if u < 2 else LAST_W)

            act.wait_ge(shifted, 1)
            nc.scalar.activation(ZT[0:64, 36, :], ZT[0:64, 36, :], ACT.Tanh).then_inc(lora_act, 1)
            nc.scalar.activation(ZT[:, 37, :], ZT[:, 37, :], ACT.Sigmoid).then_inc(lora_act, 1)
            nc.scalar.activation(ZT[0:32, 38, :], ZT[0:32, 38, :], ACT.Sigmoid).then_inc(lora_act, 1)
            BOTH = range(2)
            two = lambda x: x.rearrange("p (h t) -> p h t", h=2)
            with act.Fori(0, PAIRS) as p:
                act.wait_ge(S["pair_pool"], p + 1)
                act.wait_ge(S["lora_mm"], p + 2)
                nc.scalar.activation(two(LD), ps[:, 0:2, 0:HALF], ACT.Tanh, bias=HB[:, bass.ds(p, 1)], scale=0.5).then_inc(S["lora_ev"], 1)
                nc.scalar.activation(two(AA), ps[:, 2:4, 0:HALF], ACT.Tanh, bias=HB[:, bass.ds(8 + p, 1)], scale=0.5).then_inc(S["lora_ev"], 1)
                nc.scalar.activation(two(G), ps[:, 4:6, 0:HALF], ACT.Copy).then_inc(S["lora_ev"], 1)
                act.wait_ge(S["kk_raw"], p + 1)
                nc.scalar.activation(SQ, KK, ACT.Square).then_inc(S["sq_ready"], 1)
                act.wait_ge(S["lprev_ready"], p + 1)
                nc.scalar.activation(PX[:, 0:SEQ], LC[:, 0:SEQ], ACT.Exp).then_inc(S["exp_ev"], 1)
                nc.scalar.activation(PN[:, 0:SEQ], LC[:, 0:SEQ], ACT.Exp, scale=-1.0).then_inc(S["exp_ev"], 1)
                nc.scalar.activation(PY[:, 0:SEQ], PY[:, 0:SEQ], ACT.Exp).then_inc(S["exp_ev"], 1)
                nc.scalar.activation(SVT6[:, 5 * N_DEC:6 * N_DEC], LD[:, SEQ:TOK], ACT.Exp).then_inc(S["exp_ev"], 1)
                act.wait_ge(S["ss_mm"], p + 1)
                nc.scalar.activation(two(SQ), ps[:, 6:8, 0:HALF], ACT.Sqrt).then_inc(S["ss_root"], 1)
                act.wait_ge(S["sv_mm"], p + 1)
                act.wait_ge(S["sv_out"], 16 * p + 16)
                sv = SVT[0:N_DEC].rearrange("p a n -> p (a n)")
                nc.scalar.activation(sv[:, 0:512], ps[0:N_DEC, 0, :], ACT.Copy)
                nc.scalar.activation(sv[:, 512:768], ps[0:N_DEC, 1, 0:256], ACT.Copy).then_inc(S["sv_ev"], 1)
                for h in BOTH:
                    hp = 2 * p + h
                    if h:
                        act.wait_ge(S["gram_mm"], 4 * p + 2)
                    for e in BOTH:
                        rows = slice(e * 64, e * 64 + 64)
                        v = ZT[rows, bass.ds(ATT_TILES + 16 + p, 1), h * 256:(h + 1) * 256].rearrange("p a (c t) -> p (a c) t", t=CHUNK)
                        last = nc.scalar.activation(VB[rows, :, e * 64:e * 64 + 64], v, ACT.Copy)
                    last.then_inc(S["bd_act"], 1)
                    for s in BOTH:
                        n = 4 * p + 2 * h + s + 1
                        act.wait_ge(S["tok_mm"], n)
                        if h and not s:
                            act.wait_ge(S["o_mm"], 8 * p + 4)
                            act.wait_ge(S["solve_dve"], after("solve_dve", "g", 4 * p + 2, 1))
                        nc.scalar.activation(Bx[s][:, :, 0], ps[:, 6, 0:256].rearrange("p (c n) -> p c n", n=P), ACT.Copy).then_inc(S["tok_ev"], 1)
                        nc.scalar.activation(BR[s][:, :, 0], ps[:, 6, 256:512].rearrange("p (c n) -> p c n", n=P), ACT.Copy).then_inc(S["tok_ev"], 1)
                        nc.scalar.activation(KV[s], ps[:, 7, :].rearrange("p (c n) -> p c n", n=P), ACT.Copy).then_inc(S["tok_ev"], 1)
                    for s in BOTH:
                        act.wait_ge(S["solve_pe"], after("solve_pe", "s3", 4 * p + 2 * h + s + 1, s))
                        nc.scalar.activation(NN[s], ps[:, 3 * s, :].rearrange("p (c n) -> p c n", n=P), ACT.Copy).then_inc(S["s3_ev"], 1)
                        nc.scalar.activation(Bx[s][:, :, 1], ps[:, 3 * s + 1, 0:256].rearrange("p (c n) -> p c n", n=P), ACT.Copy).then_inc(S["s3_ev"], 1)
                    for step, dst, bank, width in (("m", MM, 1, 512), ("m2", M2, 0, 512), ("m4", M4T, 0, 256)):
                        for s in BOTH:
                            act.wait_ge(S["solve_pe"], after("solve_pe", step, 4 * p + 2 * h + s + 1, s))
                            nc.scalar.activation(dst[s], ps[:, 3 * s + bank, 0:width].rearrange("p (c n) -> p c n", n=P), ACT.Copy).then_inc(S["solve_act"], 1)
                    for x in range(HC):
                        act.wait_ge(S["o_mm"], 8 * p + 4 * h + x + 1)
                        for e in BOTH:
                            rows = slice(e * 64, e * 64 + 64)
                            t0 = (4 * h + x) * CHUNK
                            last = nc.scalar.activation(ZT[rows, bass.ds(ATT_TILES + p, 1), t0:t0 + CHUNK].rearrange("p a t -> p (a t)"),
                                                        ps[rows, (0, 1, 3, 4)[x], e * 64:e * 64 + 64], ACT.Copy)
                        last.then_inc(S["o_ev"], 1)
                act.wait_ge(S["wkv_mm"], p + 1)
                act.wait_ge(stored, 9 * 16 + 32 * p)
                nc.scalar.activation(WKV, ps[:, 0, 0:P], ACT.Copy).then_inc(S["wkv_ev"], 1)

            for i in range(3):
                for u in range(SLOTS):
                    evac(u, (7 if u < 3 else 6) + i, 4 * i + u, u % 2)
            with act.Fori(0, PAIRS) as p:
                act.wait_ge(S["gn_mu_mm"], p + 1)
                act.wait_ge(S["gn_chain"], 4 * p + 1)
                nc.scalar.activation(XS, XC, ACT.Square).then_inc(S["gn_sq"], 1)
                act.wait_ge(S["gn_var_mm"], p + 1)
                nc.scalar.activation(two(XS), ps[:, 2:4, 0:HALF], ACT.Sqrt, bias=eps[:, 0:1], scale=1.0 / HD).then_inc(S["gn_root"], 1)
            for a in range(5):
                n = P if a < 4 else N_DEC
                act.wait_ge(S["kvt_mm"], a + 1)
                nc.scalar.activation(KVT[0:n, a], ps[0:n, a, :], ACT.Copy).then_inc(S["kvt_ev"], 1)
            act.wait_ge(S["swap_mm"], 2)
            nc.scalar.activation(QSW.rearrange("p f n -> p (f n)"), ps[:, 7, 0:256], ACT.Copy).then_inc(S["qsw_ev"], 1)
            act.sem_inc(S["pexp_ev"], 4)
            act.sem_inc(S["pt_ev"], 3)
            with act.Fori(0, 4) as v:

                def exps(hd):
                    act.wait_ge(S["max_ev"], 4 * v + hd + 1)
                    for i in range(4):
                        off = i * (i + 1) // 2 * P
                        nc.scalar.activation(PR[hd % 2][:, off:off + (i + 1) * P], ps[:, i, 0:(i + 1) * P], ACT.Exp,
                                             bias=STAT[:, 4 + hd % 2, i:i + 1], scale=SCALE, accum_out=STAT[:, 6 + hd % 2, i:i + 1]).then_inc(S["pexp_ev"], 1)
                exps(0)
                for hd in range(4):
                    n = 4 * v + hd
                    if hd < 3:
                        exps(hd + 1)
                    for a in range(4):
                        act.wait_ge(S["pt_mm"], 4 * n + a + 1)
                        toff = sum(4 - x for x in range(a)) * P
                        nc.scalar.activation(PT[hd % 2][:, toff:toff + (4 - a) * P], ps[:, 4 + a % 3, 0:(4 - a) * P], ACT.Copy).then_inc(S["pt_ev"], 1)
            act.sem_inc(S["sc_ev"], 4)
            with act.Fori(0, 4) as bp:
                def score_copy(c):
                    n = 8 * bp + c
                    act.wait_ge(S["qk_mm"], 9 * bp + c + 1)
                    for k in BOTH:
                        nc.scalar.activation(SCR[:, (2 * c + k) * 256:(2 * c + k + 1) * 256], ps[:, 4 + c % 2, k * 256:(k + 1) * 256], ACT.Copy,
                                             accum_out=DS[:, 2 * c + k:2 * c + k + 1]).then_inc(S["sc_ev"], 1)
                act.wait_ge(S["dec_ev"], bp + 1)
                for c in range(8):
                    j = (2 * c) % 8
                    act.wait_ge(page_free[j], 4 * bp + c // 4 + 2)
                    if c >= 2:
                        act.wait_ge(S["qk_mm"], 9 * bp + c - 1)
                    nc.scalar.activation(KTD[c % 2][0], ps[:, 0:2, :], ACT.Copy).then_inc(S["kt_ev_a"], 1)
                    if c:
                        score_copy(c - 1)
                score_copy(7)
                act.wait_ge(S["soft_ev"], bp + 1)
                nc.scalar.activation(SCR[:, :], SCR[:, :], ACT.Exp, bias=DS[:, 40:41], scale=SCALE, accum_out=DS[:, 41:42]).then_inc(S["pexpd_ev"], 1)
                act.wait_ge(S["ptd_mm"], 9 * bp + 1)
                nc.scalar.activation(PTO[0:N_DEC], ps[0:N_DEC, 6, 0:P], ACT.Copy).then_inc(S["ptd_ev"], 1)
                for c in range(8):
                    act.wait_ge(S["ptd_mm"], 9 * bp + c + 2)
                    if c >= 2:
                        act.wait_ge(page_free[(2 * c - 3) % 8], 4 * bp + 2 + (c - 2) // 4 + 2)
                    nc.scalar.activation(PTD[c % 2], ps[:, 4 + c % 2, :], ACT.Copy).then_inc(S["ptd_ev"], 1)
                act.wait_ge(S["oqt_mm"], bp + 1)
                nc.scalar.activation(OF, ps[:, 0, 0:P], ACT.Copy).then_inc(S["of_ev"], 1)

            def layer_norm(which):
                for k in range(KT):
                    act.wait_ge(S["ln_sub"], KT * which + k + 1)
                    if k >= 2:
                        act.wait_ge(S["ln_var_mm"], KT * which + k - 1)
                    nc.scalar.activation(LQ[k % 2], XT[:, k, :], ACT.Square).then_inc(S["ln_sq"], 1)
                act.wait_ge(S["ln_var_mm"], KT * which + KT)
                nc.scalar.activation(two(RS), ps[:, 6:8, 0:HALF], ACT.Sqrt, bias=eps[:, 1:2], scale=1.0 / D_MODEL).then_inc(S["ln_root"], 1)
                for k in range(KT):
                    g, b = (VC[:, VEC_AT[f"ln{which + 1}_{x}"] + k:VEC_AT[f"ln{which + 1}_{x}"] + k + 1] for x in "gb")
                    act.wait_ge(S["ln_scaled"], KT * which + k + 1)
                    nc.scalar.activation(XT[:, k, :], XT[:, k, :], ACT.Identity, scale=g, bias=b).then_inc(S["ln_ev"], 1)
            layer_norm(0)
            act.sem_inc(S["gate_ev"], 2)
            act.wait_ge(S["gp_zero"], 1)
            with act.Fori(0, FT // 2) as i:
                for j in range(2):
                    f = 2 * i + j
                    act.wait_ge(w_free[2 * j], ROUND_UP[2 * j] + i + 2)
                    act.wait_ge(S["conv_ev"], f + 1)
                    act.wait_ge(S["cvn_ev"], f + 1)
                    b0 = 4 * j
                    nc.scalar.activation(GP[j][:, 2:2 + HALF], ps[:, b0, 0:HALF], ACT.Copy)
                    nc.scalar.activation(GP[j][:, 2 + HALF:2 + SEQ], ps[:, b0 + 1, 0:SEQ - HALF], ACT.Copy)
                    dec = GP[j][:, SEQ + 2:GPW].rearrange("p (b t) -> p b t", t=DEC_SEQ + 2)
                    nc.scalar.activation(dec[:, :, 2:], ps[:, b0 + 1, SEQ - HALF:HALF].rearrange("p (b t) -> p b t", t=DEC_SEQ), ACT.Copy).then_inc(S["gate_ev"], 1)
                    act.wait_ge(S["conv_ev"], f + 3)
                    nc.scalar.activation(CO[j], CO[j], ACT.Silu).then_inc(S["silu_ev"], 1)
            layer_norm(1)
            for a in range(5):
                n = P if a < 4 else N_DEC
                for q in range(4):
                    act.wait_ge(S["y_mm"], 4 * a + q + 1)
                    nc.scalar.activation(Y[a][0:n, q * 512:(q + 1) * 512], ps[0:n, q, :], ACT.Copy).then_inc(S["y_ev"], 1)

        @block.vector
        def _(dve):
            for k in range(KT):
                dve.wait_ge(xt_mm, k + 1)
                nc.vector.tensor_copy(XT[:, k, SEQ:TOK], ps[:, 2 * (k % 4) + 1, 0:N_DEC]).then_inc(xt_ev_b, 1)
            dve.wait_ge(small_mm, 1)
            for t in range(4):
                n = sum(k for _, k in VEC_ROWS[t])
                l = nc.vector.tensor_copy(VC[:, t * P:t * P + n], ps[:, 0, t * P:t * P + n])
            l.then_inc(small_ev, 1)
            nc.vector.tensor_copy(shiftT[:, :, :].rearrange("p m b -> p (m b)"), ps[:, 1, 0:RW_TILES * 8]).then_inc(small_ev, 1)
            cv = convT[:, :, :].rearrange("p m b -> p (m b)")
            nc.vector.tensor_copy(cv[:, 0:512], ps[:, 2, :]).then_inc(small_ev, 1)
            nc.vector.tensor_copy(cv[:, 512:FT * 16], ps[:, 3, 0:FT * 16 - 512]).then_inc(small_ev, 1)
            for g in range(7):
                dve.wait_ge(last_mm, g + 1)
                n = 512 if g < 6 else 2 * P + LAST_W
                nc.vector.tensor_copy(last_tok[:, g * 512:g * 512 + n], ps[0:33, 4 + g % 4, 0:n]).then_inc(last_ev, 1)

            link_n = [0]

            def link(ins):
                link_n[0] += 1
                ins.then_inc(shift_chain, 1)
                dve.wait_ge(shift_chain, link_n[0])
            l = nc.vector.tensor_scalar(HB[:, :], VC[:, VEC_AT["w0"]:VEC_AT["w0"] + 16], 0.5, None, ALU.mult)
            for m0, m1, rows in ((0, 8, P), (8, 16, P), (16, 24, P), (24, 26, P), (26, 27, LAST_W)):
                n = m1 - m0
                z = ZT[0:rows, ATT_TILES + m0:ATT_TILES + m1, :]
                d = D3[0:rows, 0:n, :]
                zs, ds = (x[:, :, SEQ:TOK].rearrange("p m (b t) -> p m b t", t=DEC_SEQ) for x in (z, d))
                nc.vector.tensor_tensor(d[:, :, 1:SEQ], z[:, :, 0:SEQ - 1], z[:, :, 1:SEQ], ALU.subtract)
                nc.vector.tensor_scalar(d[:, :, 0], z[:, :, 0], -1.0, None, ALU.mult)
                for m in range(n):
                    nc.vector.tensor_tensor(ds[:, m, :, 1:DEC_SEQ], zs[:, m, :, 0:DEC_SEQ - 1], zs[:, m, :, 1:DEC_SEQ], ALU.subtract)
                link(nc.vector.tensor_tensor(ds[:, :, :, 0], shiftT[0:rows, m0:m1, :], zs[:, :, :, 0], ALU.subtract))
                for m in range(n):
                    mu = VC[0:rows, VEC_AT["shift_mu"] + m0 + m:VEC_AT["shift_mu"] + m0 + m + 1]
                    l = nc.vector.scalar_tensor_tensor(out=z[:, m], in0=d[:, m], scalar=mu, in1=z[:, m], op0=ALU.mult, op1=ALU.add)
                link(l)
            nc.vector.memset(ST[0], 0.0).then_inc(shifted, 1)
            for x in (AR, BB, KB, VB):
                l = nc.vector.memset(x, 0.0)
                l.then_inc(S["bd_zero"], 1)
            nc.vector.memset(ST[1], 0.0).then_inc(S["bd_zero"], 1)
            dve.sem_inc(S["chain_ev"], 1)
            dve.wait_ge(stored, 9 * 16)
            dve.sem_inc(S["bd_zero"], 1)

            K = 9
            BOTH = range(2)
            seg = const("seg")
            masks = {n: const(n) for n in ("low8", "lowoff", "up8", "up", "upinc")}
            wide = lambda m: masks[m].rearrange("p (a n) -> p a n", a=1).to_broadcast([P, SC, P])
            two = lambda x: x.rearrange("p (h t) -> p h t", h=2)
            with dve.Fori(0, PAIRS) as p:
                count = [0]

                def link(ins):
                    count[0] += 1
                    ins.then_inc(S["rw_chain"], 1)
                    dve.wait_ge(S["rw_chain"], K * p + count[0])
                vec = lambda name: VC[:, bass.ds(VEC_AT[name] + p, 1)]
                tile = lambda j: ZT[:, bass.ds(ATT_TILES + 8 * j + p, 1), :].rearrange("p a t -> p (a t)")
                rz, kz, vz = tile(0), tile(1), tile(2)
                dve.wait_ge(S["pair_pool"], p + 1)
                nc.vector.tensor_scalar(KK, kz, vec("k_k"), None, ALU.mult).then_inc(S["kk_raw"], 1)
                dve.wait_ge(S["lora_ev"], 3 * p + 2)
                link(nc.vector.tensor_scalar(LD, LD, 0.5 * DECAY_SCALE, 0.5 * DECAY_SCALE, ALU.mult, ALU.add))
                link(nc.vector.tensor_tensor_scan(LC[:, 0:SEQ], seg, LD[:, 0:SEQ], 0.0, ALU.mult, ALU.add))
                nc.vector.tensor_tensor(PY[:, 0:SEQ], LC[:, 0:SEQ], LD[:, 0:SEQ], ALU.subtract).then_inc(S["lprev_ready"], 1)
                link(nc.vector.tensor_scalar(AA, AA, 0.5, 0.5, ALU.mult, ALU.add))
                link(nc.vector.tensor_scalar(BON, AA, -1.0, vec("k_a"), ALU.add, ALU.mult))
                link(nc.vector.scalar_tensor_tensor(out=kz, in0=BON, scalar=1.0, in1=kz, op0=ALU.add, op1=ALU.mult))
                dve.wait_ge(S["ss_root"], p + 1)
                link(nc.vector.tensor_scalar(SQ, SQ, 1e-12, None, ALU.max))
                link(nc.vector.reciprocal(SQ, SQ))
                link(nc.vector.tensor_tensor(KK, KK, SQ, ALU.mult))
                nc.vector.scalar_tensor_tensor(out=BON, in0=rz, scalar=vec("r_k"), in1=kz, op0=ALU.mult, op1=ALU.mult).then_inc(S["bonus_in"], 1)
                link(nc.vector.tensor_tensor(AB, KK, AA, ALU.mult))
                for j, x in enumerate((rz, kz, vz, KK, AB)):
                    l = nc.vector.tensor_copy(SVT6[:, j * N_DEC:(j + 1) * N_DEC], x[:, SEQ:TOK])
                l.then_inc(S["ab_ready"], 1)
                dve.wait_ge(S["bonus_mm"], p + 1)
                nc.vector.tensor_tensor(two(BON), ps[:, 6:8, 0:HALF], two(vz), ALU.mult).then_inc(S["bonus_ev"], 1)
                dve.wait_ge(S["exp_ev"], 4 * p + 4)
                for h in BOTH:
                    hp = 2 * p + h
                    if h:
                        dve.wait_ge(S["gram_mm"], 4 * p + 2)
                    for e in BOTH:
                        rows = slice(e * 64, e * 64 + 64)
                        cut = lambda x: x[rows, h * 256:(h + 1) * 256].rearrange("p (c t) -> p c t", t=CHUNK)
                        nc.vector.scalar_tensor_tensor(out=AR[rows, :, 0, e * 64:e * 64 + 64], in0=cut(KK), scalar=-1.0,
                                                       in1=cut(PY), op0=ALU.mult, op1=ALU.mult)
                        l = nc.vector.tensor_tensor(BB[rows, :, e * 64:e * 64 + 64], cut(AB), cut(PN), ALU.mult)
                    l.then_inc(S["bd_dve"], 1)
                    three = lambda x: x.rearrange("p (c n) -> p c n", n=P)
                    for s in BOTH:
                        n = 4 * p + 2 * h + s + 1
                        dve.wait_ge(S["gram_mm"], n)
                        if h and not s:
                            dve.wait_ge(S["o_mm"], 8 * p + 4)
                        bank0 = ps[:, 3 * s, :].rearrange("p (c w n) -> p c w n", w=2, n=P)
                        bank1 = ps[:, 3 * s + 1, :].rearrange("p (c w n) -> p c w n", w=2, n=P)
                        bank2 = three(ps[:, 3 * s + 2, 0:256])
                        nc.vector.tensor_tensor(NdT[s], bank0[:, :, 0], wide("up8"), ALU.mult)
                        nc.vector.tensor_tensor(BR[s][:, :, 1], bank0[:, :, 1], wide("upinc"), ALU.mult)
                        nc.vector.tensor_tensor(AKT[s], bank1[:, :, 0], wide("up"), ALU.mult)
                        nc.vector.tensor_tensor(RKT[s], bank1[:, :, 1], wide("upinc"), ALU.mult)
                        nc.vector.tensor_tensor(Nd[s], bank2, wide("low8"), ALU.mult)
                        nc.vector.tensor_tensor(Lo[s], bank2, wide("lowoff"), ALU.mult).then_inc(S["gram_ev"], 1)
                        dve.wait_ge(S["gram_ev"], 2 * n - 1)
                        l = nc.vector.tensor_tensor(P1T[s], NdT[s], ident.rearrange("p (a n) -> p a n", a=1).to_broadcast([P, SC, P]), ALU.add)
                        l.then_inc(S["gram_ev"], 1)
                    for s in BOTH:
                        n = 4 * p + 2 * h + s + 1
                        dve.wait_ge(S["solve_pe"], after("solve_pe", "n4", n, s))
                        dve.wait_ge(S["gram_ev"], 2 * n)
                        nc.vector.tensor_copy(N4[s], three(ps[:, 3 * s + 2, 0:256]))
                        nc.vector.tensor_tensor(P2T[s], three(ps[:, 3 * s + 2, 256:512]), P1T[s], ALU.add).then_inc(S["solve_dve"], 1)
                    for s in BOTH:
                        n = 4 * p + 2 * h + s + 1
                        dve.wait_ge(S["solve_pe"], after("solve_pe", "p3", n, s))
                        dve.wait_ge(S["solve_dve"], after("solve_dve", "p2", n, s))
                        nc.vector.tensor_tensor(P3T[s], three(ps[:, 3 * s, 0:256]), P2T[s], ALU.add).then_inc(S["solve_dve"], 1)
                    four = lambda x: x.rearrange("p (c w n) -> p c w n", w=2, n=P)
                    for s in BOTH:
                        n = 4 * p + 2 * h + s + 1
                        dve.wait_ge(S["solve_pe"], after("solve_pe", "m", n, s))
                        nc.vector.tensor_copy(By[s], four(ps[:, 3 * s + 2, :])).then_inc(S["solve_dve"], 1)
                    for s in BOTH:
                        n = 4 * p + 2 * h + s + 1
                        dve.wait_ge(S["solve_pe"], after("solve_pe", "m2", n, s))
                        dve.wait_ge(S["solve_dve"], after("solve_dve", "b0", n, s))
                        nc.vector.tensor_tensor(Bx[s], four(ps[:, 3 * s + 1, :]), By[s], ALU.add).then_inc(S["solve_dve"], 1)
                    for s in BOTH:
                        n = 4 * p + 2 * h + s + 1
                        dve.wait_ge(S["solve_pe"], after("solve_pe", "m4", n, s))
                        dve.wait_ge(S["solve_dve"], after("solve_dve", "b1", n, s))
                        nc.vector.tensor_tensor(By[s], four(ps[:, 3 * s + 2, :]), Bx[s], ALU.add).then_inc(S["solve_dve"], 1)
                    for s in BOTH:
                        n = 4 * p + 2 * h + s + 1
                        dve.wait_ge(S["solve_pe"], after("solve_pe", "b3", n, s))
                        dve.wait_ge(S["solve_dve"], after("solve_dve", "b2", n, s))
                        nc.vector.tensor_tensor(Bx[s], four(ps[:, 3 * s + 1, :]), By[s], ALU.add).then_inc(S["solve_dve"], 1)
                    for s in BOTH:
                        n = 4 * p + 2 * h + s + 1
                        dve.wait_ge(S["solve_pe"], after("solve_pe", "g", n, s))
                        b = four(ps[:, 3 * s + 2, :])
                        dve.wait_ge(S["bd_pool"], hp + 1)
                        nc.vector.tensor_tensor(GT[s], b[:, :, 0], ident.rearrange("p (a n) -> p a n", a=1).to_broadcast([P, SC, P]), ALU.add)
                        nc.vector.tensor_tensor(R2[s], b[:, :, 1], AR[:, s * SC:(s + 1) * SC, 1], ALU.add).then_inc(S["solve_dve"], 1)
                    for x in range(HC):
                        dve.wait_ge(S["chain_mm"], 8 * p + 4 * h + x + 1)
                        if h or x:
                            dve.wait_ge(S["o_mm"], 8 * p + 4 * h + x)
                        end = (4 * h + x + 1) * CHUNK - 1
                        nc.vector.tensor_scalar(ST[(4 * h + x + 1) % 2], ps[:, 6 + x % 2, 0:P], PX[:, end:end + 1], None,
                                                ALU.mult).then_inc(S["chain_ev"], 1)
                dve.wait_ge(S["wkv_mm"], p + 1)
                nc.vector.memset(ST[0], 0.0).then_inc(S["ld_ready"], 1)
                assert count[0] == 9, count

            rc = [0]

            def step(ins):
                rc[0] += 1
                ins.then_inc(S["rec"], 1)
                dve.wait_ge(S["rec"], rc[0])
            cols = lambda x, n: x.rearrange("p (a j) -> p a j", a=1).to_broadcast([P, n, HD])
            rows_of = lambda x: x.rearrange("p (i a) -> p i a", a=1).to_broadcast([P, 32, HD])
            nc.vector.memset(eps[:, 0:1], GN_EPS)
            nc.vector.memset(eps[:, 1:2], LN_EPS).then_inc(S["rec"], 1)
            rc[0] += 1
            dve.wait_ge(S["sv_in"], 16 * 6 * DEC_BATCH)
            for half in range(2):
                dve.wait_ge(S["state_in"], 16 * half + 16)
                for t in range(DEC_SEQ):
                    r, k, v, kk, ab, w = (SV[:, j, t] for j in range(6))
                    step(nc.vector.tensor_tensor(TD, SD, cols(kk, 32), ALU.mult))
                    nc.vector.tensor_reduce(SA, TD, AX, ALU.add).then_inc(S["rec"], 1)
                    rc[0] += 1
                    step(nc.vector.tensor_tensor(SD, SD, cols(w, 32), ALU.mult))
                    step(nc.vector.tensor_tensor(TD, rows_of(SA), cols(ab, 32), ALU.mult))
                    step(nc.vector.tensor_tensor(SD, SD, TD, ALU.subtract))
                    step(nc.vector.tensor_tensor(TD, rows_of(v[:, half * 32:half * 32 + 32]), cols(k, 32), ALU.mult))
                    step(nc.vector.tensor_tensor(SD, SD, TD, ALU.add))
                    step(nc.vector.tensor_tensor(TD, SD, cols(r, 32), ALU.mult))
                    step(nc.vector.tensor_reduce(OD[:, t, half * 32:half * 32 + 32], TD, AX, ALU.add))
                dve.sem_inc(S["rec_half"], 1)
            dve.wait_ge(S["ot_mm"], 1)
            nc.vector.tensor_copy(ZT[:, ATT_TILES:ATT_TILES + 8, SEQ:TOK], ps[:, 4, 0:256].rearrange("p (f n) -> p f n", n=N_DEC)).then_inc(S["ot_ev"], 1)
            dve.sem_inc(S["gn_ev"], 1)
            with dve.Fori(0, PAIRS) as p:
                o, gate, bonus = (ZT[:, bass.ds(ATT_TILES + 8 * j + p, 1), :].rearrange("p a t -> p (a t)") for j in range(3))
                dve.wait_ge(S["gn_mu_mm"], p + 1)
                nc.vector.scalar_tensor_tensor(out=two(XC), in0=ps[:, 0:2, 0:HALF], scalar=-1.0 / HD, in1=two(o), op0=ALU.mult, op1=ALU.add).then_inc(S["gn_chain"], 1)
                dve.wait_ge(S["gn_root"], p + 1)
                nc.vector.reciprocal(XS, XS).then_inc(S["gn_chain"], 1)
                dve.wait_ge(S["gn_chain"], 4 * p + 2)
                nc.vector.tensor_tensor(XC, XC, XS, ALU.mult).then_inc(S["gn_chain"], 1)
                dve.wait_ge(S["gn_chain"], 4 * p + 3)
                nc.vector.tensor_scalar(XC, XC, VC[:, bass.ds(VEC_AT["gn_g"] + p, 1)], VC[:, bass.ds(VEC_AT["gn_b"] + p, 1)], ALU.mult, ALU.add).then_inc(S["gn_chain"], 1)
                dve.wait_ge(S["gn_chain"], 4 * p + 4)
                nc.vector.tensor_tensor(XC, XC, bonus, ALU.add).then_inc(S["gate_chain"], 1)
                dve.wait_ge(S["gate_chain"], p + 1)
                nc.vector.tensor_tensor(o, XC, gate, ALU.mult).then_inc(S["gn_ev"], 1)
            dve.wait_ge(S["gn_ev"], PAIRS + 1)
            for m in range(10):
                b0 = 4 + 2 * (m % 2)
                dve.wait_ge(S["rot_mm"], m + 1)
                nc.vector.tensor_tensor(two(RT), ps[:, b0:b0 + 2, 0:HALF], two(const("sin")), ALU.mult)
                nc.vector.tensor_tensor(ZT[:, m, :], ZT[:, m, :], const("cos"), ALU.mult).then_inc(S["rope_chain"], 1)
                dve.wait_ge(S["rope_chain"], m + 1)
                nc.vector.tensor_tensor(ZT[:, m, :], ZT[:, m, :], RT, ALU.add).then_inc(S["rope_ev"], 1)
                dve.wait_ge(S["rope_ev"], m + 1)
            dve.wait_ge(S["swap_mm"], 1)
            for kv in range(4):
                m, own = divmod(kv, 2)
                for e in range(2):
                    rows = slice(e * 64, e * 64 + 64)
                    src = ZT[rows, 8 + m, 0:SEQ] if e == own else ps[rows, 5 + m, :]
                    l = nc.vector.tensor_copy(KDUP[rows, kv], src)
            l.then_inc(S["kdup_ev"], 1)
            nc.vector.memset(QBD, 0.0).then_inc(S["qbd_zero"], 1)
            dve.wait_ge(S["qbd_zero"], 1)
            dve.wait_ge(S["qsw_ev"], 1)
            for pair in range(2):
                for kv2 in range(2):
                    rows = slice(kv2 * 64, kv2 * 64 + 64)
                    for g in range(4):
                        f = (2 * pair + kv2) * 2 + g // 2
                        src = ZT[rows, f, SEQ:TOK] if g % 2 == kv2 else QSW[rows, f]
                        dst = QBD[rows, pair, :, kv2 * 16:kv2 * 16 + 16].rearrange("p b (t g) -> p b t g", g=4)[:, :, :, g]
                        l = nc.vector.tensor_copy(dst, src.rearrange("p (b t) -> p b t", t=DEC_SEQ))
            l.then_inc(S["qbd_ev"], 1)
            dve.wait_ge(S["kvt_out"], 160)
            dve.sem_inc(S["ao_ev"], 1)
            with dve.Fori(0, 4) as v:
                for hd in range(4):
                    f, e = divmod(hd, 2)
                    n = 4 * v + hd
                    b = hd % 2
                    dve.wait_ge(S["sc_mm"], 4 * n + 4)
                    for i in range(4):
                        diag = ps[:, i, i * P:(i + 1) * P]
                        l = nc.vector.tensor_tensor(diag, diag, const("causal"), ALU.add)
                    l.then_inc(S["mask_ev"], 1)
                    dve.wait_ge(S["mask_ev"], n + 1)
                    for i in range(4):
                        l = nc.vector.tensor_reduce(STAT[:, 2 + b, i:i + 1], ps[:, i, 0:(i + 1) * P], AX, ALU.max)
                    l.then_inc(S["att_chain"], 1)
                    dve.wait_ge(S["att_chain"], 2 * n + 1)
                    nc.vector.tensor_scalar(STAT[:, 4 + b], STAT[:, 2 + b], -SCALE, None, ALU.mult).then_inc(S["max_ev"], 1)
                    dve.wait_ge(S["pexp_ev"], 4 * n + 8)
                    nc.vector.reciprocal(STAT[:, 8 + b], STAT[:, 6 + b]).then_inc(S["att_chain"], 1)
                    dve.wait_ge(S["att_chain"], 2 * n + 2)
                    for i in range(4):
                        off = i * (i + 1) // 2 * P
                        x = PR[b][:, off:off + (i + 1) * P]
                        l = nc.vector.tensor_scalar(x, x, STAT[:, 8 + b, i:i + 1], None, ALU.mult)
                    l.then_inc(S["pnorm_ev"], 1)
                    if hd >= 2:
                        if hd == 3:
                            dve.wait_ge(S["ao_mm"], n + 1)
                            tile = 2 * v + 1
                        else:
                            dve.wait_ge(S["ao_mm"], n)
                            tile = 2 * v
                        nc.vector.tensor_copy(ZT[:, bass.ds(tile, 1), 0:SEQ].rearrange("p a t -> p (a t)"), ps[:, 7, :]).then_inc(S["ao_ev"], 1)
            dve.sem_inc(S["dec_ev"], 1)
            dve.wait_ge(S["ao_ev"], 9)
            with dve.Fori(0, 4) as bp:
                if True:
                    nc.vector.tensor_copy(QB, QBD[:, :, bass.ds(2 * bp, 2), :]).then_inc(S["qb_ev"], 1)
                for c in range(8):
                    j = (2 * c + 1) % 8
                    dve.wait_ge(page_free[j], 4 * bp + c // 4 + 2)
                    if c >= 2:
                        dve.wait_ge(S["qk_mm"], 9 * bp + c - 1)
                    nc.vector.tensor_copy(KTD[c % 2][1], ps[:, 2:4, :]).then_inc(S["kt_ev_d"], 1)
                dve.wait_ge(S["qk_mm"], 9 * bp + 9)
                dve.wait_ge(S["sc_ev"], 16 * bp + 20)
                own = C[:, bass.ds(CONST_AT["own"][0] + bp * N_DEC, N_DEC)]
                dc = [0]
                KD = 8

                def link(ins):
                    dc[0] += 1
                    ins.then_inc(S["dec_chain"], 1)
                    dve.wait_ge(S["dec_chain"], KD * bp + dc[0])
                nc.vector.tensor_tensor(SCR[:, PAST_LEN:SC_W], ps[:, 6, 0:N_DEC], own, ALU.add)
                gates = DS[:, 0:16]
                g_i = gates.rearrange("p (i a) -> p i a", a=1).to_broadcast([P, 16, 16])
                g_j = gates.rearrange("p (a j) -> p a j", a=1).to_broadcast([P, 16, 16])
                before = const("before").rearrange("p (i j) -> p i j", j=16)
                nc.vector.tensor_tensor(RK[:, 0], g_j, g_i, ALU.is_gt)
                link(nc.vector.tensor_tensor(RK[:, 1], g_j, g_i, ALU.is_ge))
                link(nc.vector.tensor_tensor(RK[:, 1], RK[:, 1], before, ALU.mult))
                link(nc.vector.tensor_tensor(RK[:, 0], RK[:, 0], RK[:, 1], ALU.max))
                link(nc.vector.tensor_reduce(DS[:, 16:32], RK[:, 0], AX, ALU.add))
                link(nc.vector.tensor_scalar(DS[:, 16:32], DS[:, 16:32], 2.5, NEG, ALU.is_gt, ALU.mult))
                blocks = SCR[:, 0:PAST_LEN].rearrange("p (n k) -> p n k", k=256)
                link(nc.vector.tensor_tensor(blocks, blocks, DS[:, 16:32].rearrange("p (n a) -> p n a", a=1).to_broadcast([P, 16, 256]), ALU.add))
                link(nc.vector.tensor_reduce(DS[:, 39:40], SCR[:, :], AX, ALU.max))
                nc.vector.tensor_scalar(DS[:, 40:41], DS[:, 39:40], -SCALE, None, ALU.mult).then_inc(S["soft_ev"], 1)
                dve.wait_ge(S["pexpd_ev"], bp + 1)
                link(nc.vector.reciprocal(DS[:, 42:43], DS[:, 41:42]))
                dve.wait_ge(S["pv_mm"], bp + 1)
                nc.vector.tensor_scalar(OQ, ps[:, 7, 0:P], DS[:, 42:43], None, ALU.mult).then_inc(S["oq_ev"], 1)
                dve.wait_ge(S["osw_mm"], bp + 1)
                cols_of = lambda x: x.rearrange("p (b r v t g) -> p b r v t g", b=2, r=2, v=2, t=4)
                for r in range(2):
                    for kv2 in range(2):
                        for g in range(4):
                            f = (2 * r + kv2) * 2 + g // 2
                            e = g % 2
                            rows = slice(e * 64, e * 64 + 64)
                            src = (OF if e == kv2 else ps[:, 1, 0:P])[rows]
                            src = cols_of(src)[:, :, r, kv2, :, g]
                            dst = ZT[rows, f:f + 1, bass.ds(SEQ + 8 * bp, 8)].rearrange("p a (b t) -> p (a b) t", t=DEC_SEQ)
                            l = nc.vector.tensor_copy(dst, src)
                l.then_inc(S["dec_ev"], 1)
                assert dc[0] == 8, dc
                dve.wait_ge(S["dec_ev"], bp + 2)
            with dve.Fori(0, 4) as i:
                for u in range(SLOTS):
                    dve.wait_ge(w_free[u], ROUND_OUT[u] + i + 2)
                    x = XT[:, bass.ds(4 * i + u, 1), :].rearrange("p a (h t) -> p (a h) t", h=2)
                    nc.vector.scalar_tensor_tensor(out=x, in0=x, scalar=ALPHA, in1=ps[:, 2 * (u % 2):2 * (u % 2) + 2, 0:HALF],
                                                   op0=ALU.mult, op1=ALU.add).then_inc(acc_free, 1)

            def layer_norm(which):
                dve.wait_ge(S["ln_mu_mm"], which + 1)
                for k in range(KT):
                    nc.vector.scalar_tensor_tensor(out=two(XT[:, k, :]), in0=ps[:, 4:6, 0:HALF], scalar=-1.0 / D_MODEL, in1=two(XT[:, k, :]),
                                                   op0=ALU.mult, op1=ALU.add).then_inc(S["ln_sub"], 1)
                dve.wait_ge(S["ln_root"], which + 1)
                nc.vector.reciprocal(RS, RS).then_inc(S["ln_rs"], 1)
                dve.wait_ge(S["ln_rs"], which + 1)
                for k in range(KT):
                    nc.vector.tensor_tensor(XT[:, k, :], XT[:, k, :], RS, ALU.mult).then_inc(S["ln_scaled"], 1)
            dve.wait_ge(acc_free, IN_TILES + KT + 2)
            layer_norm(0)
            dve.sem_inc(S["conv_ev"], 2)
            dve.sem_inc(S["h_ev"], 2)
            with dve.Fori(0, FT // 2) as i:
                for j in range(2):
                    f = 2 * i + j
                    taps = [VC[:, bass.ds(VEC_AT[f"conv{x}"] + f, 1)] for x in range(3)]
                    bias = VC[:, bass.ds(VEC_AT["conv_b"] + f, 1)]
                    dve.wait_ge(S["gate_ev"], f + 3)
                    dve.wait_ge(S["gp_hist"], f + 1)
                    dve.wait_ge(S["h_ev"], f + 1)
                    nc.vector.tensor_scalar(CO[j], GP[j][:, 2:GPW], taps[2], bias, ALU.mult, ALU.add).then_inc(S["conv_chain"], 1)
                    dve.wait_ge(S["conv_chain"], 2 * f + 1)
                    nc.vector.scalar_tensor_tensor(out=CO[j], in0=GP[j][:, 1:GPW - 1], scalar=taps[1], in1=CO[j], op0=ALU.mult, op1=ALU.add).then_inc(S["conv_chain"], 1)
                    dve.wait_ge(S["conv_chain"], 2 * f + 2)
                    nc.vector.scalar_tensor_tensor(out=CO[j], in0=GP[j][:, 0:GPW - 2], scalar=taps[0], in1=CO[j], op0=ALU.mult, op1=ALU.add).then_inc(S["conv_ev"], 1)
                    dve.wait_ge(S["silu_ev"], f + 1)
                    dve.wait_ge(w_free[2 * j + 1], ROUND_UP[2 * j + 1] + i + 2)
                    b0 = 4 * j + 2
                    ht = HT[:, bass.ds(f, 1), :].rearrange("p a t -> p (a t)")
                    nc.vector.tensor_tensor(ht[:, 0:HALF], CO[j][:, 0:HALF], ps[:, b0, 0:HALF], ALU.mult)
                    nc.vector.tensor_tensor(ht[:, HALF:SEQ], CO[j][:, HALF:SEQ], ps[:, b0 + 1, 0:SEQ - HALF], ALU.mult)
                    if True:
                        nc.vector.tensor_tensor(ht[:, SEQ:TOK].rearrange("p (b t) -> p b t", t=DEC_SEQ),
                                                co_dec[j], ps[:, b0 + 1, SEQ - HALF:HALF].rearrange("p (b t) -> p b t", t=DEC_SEQ), ALU.mult).then_inc(S["h_ev"], 1)
            with dve.Fori(0, KT // 2) as i:
                for m in range(2):
                    dve.wait_ge(w_free[3], ROUND_DOWN[3] + 2 * i + m + 2)
                    x = XT[:, bass.ds(2 * i + m, 1), :].rearrange("p a (h t) -> p (a h) t", h=2)
                    nc.vector.scalar_tensor_tensor(out=x, in0=x, scalar=ALPHA, in1=ps[:, 2 * m:2 * m + 2, 0:HALF],
                                                   op0=ALU.mult, op1=ALU.add).then_inc(acc_free, 1)
            for g in range(11):
                dve.wait_ge(S["cn_mm"], g + 1)
                nc.vector.tensor_copy(CN[:, g * 512:(g + 1) * 512], ps[0:18, g % 4, :]).then_inc(S["cn_ev"], 1)
            dve.wait_ge(acc_free, IN_TILES + 2 * KT + 2)
            layer_norm(1)

        @block.gpsimd
        def _(pool):
            nc.gpsimd.memset(shift_tok, 0.0).then_inc(pads_zero, 1)
            pool.wait_ge(pads_zero, 1)
            nc.gpsimd.memset(vec_tok, 0.0).then_inc(pads_zero, 1)

            BOTH = range(2)
            pool.sem_inc(S["pair_pool"], 1)
            pool.sem_inc(S["sv_out"], 16)
            pool.sem_inc(S["ld_ready"], 1)
            pool.wait_ge(S["bd_zero"], 6)
            with pool.Fori(0, PAIRS) as p:
                pool.wait_ge(S["exp_ev"], 4 * p + 4)
                pool.wait_ge(S["ab_ready"], p + 1)
                for h in BOTH:
                    if h:
                        pool.wait_ge(S["solve_dve"], after("solve_dve", "g", 4 * p + 2, 1))
                    for e in BOTH:
                        rows = slice(e * 64, e * 64 + 64)
                        cut = lambda x: x[rows, h * 256:(h + 1) * 256].rearrange("p (c t) -> p c t", t=CHUNK)
                        zcut = lambda j: ZT[rows, bass.ds(ATT_TILES + 8 * j + p, 1), h * 256:(h + 1) * 256].rearrange("p a (c t) -> p (a c) t", t=CHUNK)
                        nc.gpsimd.tensor_tensor(KB[rows, :, e * 64:e * 64 + 64], zcut(1), cut(PN), ALU.mult)
                        l = nc.gpsimd.tensor_tensor(AR[rows, :, 1, e * 64:e * 64 + 64], zcut(0), cut(PX), ALU.mult)
                    l.then_inc(S["bd_pool"], 1)
                pool.wait_ge(S["bd_act"], 2 * p + 2)
                pool.wait_ge(S["bonus_ev"], p + 1)
                pool.wait_ge(S["bd_pool"], 2 * p + 2)
                pool.wait_ge(S["lora_ev"], 3 * p + 3)
                pool.wait_ge(S["chain_ev"], 8 * p + 9)
                pool.wait_ge(S["wkv_ev"], p + 1)
                pool.wait_ge(S["ld_ready"], p + 2)
                pool.wait_ge(S["o_ev"], 8 * p + 8)
                for j, x in ((2, BON), (1, G)):
                    l = nc.gpsimd.tensor_copy(ZT[:, bass.ds(ATT_TILES + 8 * j + p, 1), :].rearrange("p a t -> p (a t)"), x)
                l.then_inc(S["pair_pool"], 1)
            pool.wait_ge(S["kvt_ev"], 5)
            pool.wait_ge(S["kdup_ev"], 1)
            pool.wait_ge(S["rope_ev"], 10)
            with pool.Fori(0, 4) as v:
                pool.wait_ge(S["ao_ev"], 2 * v + 1)
                nc.gpsimd.tensor_copy(KC, KDUP[:, bass.ds(v, 1)].rearrange("p a t -> p (a t)"))
                nc.gpsimd.tensor_copy(Q2, ZT[:, bass.ds(2 * v, 2), 0:SEQ])
                nc.gpsimd.tensor_copy(VS, KVT[:, 0:4, bass.ds(256 + v * HD, HD)]).then_inc(S["stat_copy"], 1)
            load_pages(pool, 1)
            pool.wait_ge(S["dec_ev"], 5)
            pool.sem_inc(S["cvn_ev"], 2)
            nc.gpsimd.memset(GP[0][:, 0:2], 0.0)
            nc.gpsimd.memset(GP[1][:, 0:2], 0.0).then_inc(S["gp_zero"], 1)
            with pool.Fori(0, FT // 2) as i:
                for j in range(2):
                    f = 2 * i + j
                    dec = GP[j][:, SEQ + 2:GPW].rearrange("p (b t) -> p b t", t=DEC_SEQ + 2)
                    pool.wait_ge(S["conv_ev"], f + 1)
                    nc.gpsimd.tensor_copy(dec[:, :, 0:2], convT[:, bass.ds(f, 1), :].rearrange("p a (b r) -> p (a b) r", r=2)).then_inc(S["gp_hist"], 1)
                    pool.wait_ge(S["gate_ev"], f + 3)
                    nc.gpsimd.tensor_copy(CVN[:, bass.ds(f, 1), 0:2].rearrange("p a n -> p (a n)"), GP[j][:, SEQ:SEQ + 2])
                    nc.gpsimd.tensor_copy(CVN[:, bass.ds(f, 1), 2:18].rearrange("p a (b r) -> p (a b) r", r=2), dec[:, :, DEC_SEQ:]).then_inc(S["cvn_ev"], 1)


_INS = ["x_prompt", "x_sample", "cache_k", "cache_v", "page_table", "state_wkv", "state_shift", "state_conv",
        "w_in", "w_out", "shift_mu", "w0", "w2", "a0", "a2", "g2", "k_k", "k_a", "r_k", "gn_g", "gn_b",
        "ln1_g", "ln1_b", "ln2_g", "ln2_b", "w_up", "conv_w", "conv_b", "w_down"]
_OUTS = [(1, SEQ, D_MODEL), (DEC_BATCH, DEC_SEQ, D_MODEL), (1, 1, SEQ, 4, HD), (1, 1, SEQ, 4, HD),
         (1, 1, 16, HD, HD), (1, 1, RW_PROJ), (1, 1, 2, D_FF), (1, DEC_BATCH, DEC_SEQ, 4, HD),
         (1, DEC_BATCH, DEC_SEQ, 4, HD), (1, DEC_BATCH, 16, HD, HD), (1, DEC_BATCH, RW_PROJ), (1, DEC_BATCH, 2, D_FF)]


def kernel(**inputs):
    import numpy as _np
    import concourse.bacc as _bacc
    from concourse import mybir as _mybir
    from concourse.bass_utils import run_bass_kernel_spmd as _run

    nc = _bacc.Bacc("TRN2", target_bir_lowering=False, num_devices=1)
    arrays, args = {}, []
    given = [(name, _np.ascontiguousarray(inputs[name])) for name in _INS] + [("consts", constants())]
    for name, a in given:
        arrays[f"in_{name}_dram"] = a
        args.append(nc.dram_tensor(f"in_{name}_dram", a.shape, _mybir.dt.from_np(a.dtype), kind="ExternalInput").ap())
    for i, shape in enumerate(_OUTS):
        args.append(nc.dram_tensor(f"out_{i}_dram", shape, F32, kind="ExternalOutput").ap())
    hybrid_layer_kernel(nc, *args)
    r = _run(nc, [arrays], core_ids=[0])
    return tuple(r.results[0][f"out_{i}_dram"] for i in range(len(_OUTS)))
```

```python
import math
from contextlib import ExitStack

import numpy as np
import concourse.bass as bass
from concourse import mybir

F32 = mybir.dt.float32
I32 = mybir.dt.int32
ALU = mybir.AluOpType
ACT = mybir.ActivationFunctionType
AX = mybir.AxisListType.X

P = 128
D_MODEL = 2048
SEQ = 512
DEC_BATCH = 8
DEC_SEQ = 4
PAST_LEN = 4096
PAGE = 128
HD = 64
N_PAGES = PAST_LEN // PAGE
N_DEC = DEC_BATCH * DEC_SEQ
TOK = SEQ + N_DEC
HALF = TOK // 2
KT = D_MODEL // P
RW_PROJ = 3360
IN_WIDTH = 1536 + RW_PROJ
ATT_TILES = 12
IN_TILES = 39
RW_TILES = IN_TILES - ATT_TILES
LAST_W = IN_WIDTH - (IN_TILES - 1) * P
D_FF = 5632
FT = D_FF // P
SLOTS = 4
DOWN_K = FT // SLOTS
LN_EPS = 1e-5
GN_EPS = 64e-5
NEG = -1e30
ALPHA = 2.0 ** 0.25
DECAY_SCALE = -math.exp(-0.5)
CHUNK = 64
ATT_ORDER = [8, 9, 10, 11] + list(range(8))
ROPE_TILES = [m for m in ATT_ORDER if m not in (10, 11)]
N_CHUNK = SEQ // CHUNK
PAIRS = 8
SCALE = HD ** -0.5

CONST_PARTS = [("ident", 128), ("swap", 128), ("rot", 128), ("headsum", 128), ("ones", 128),
               ("low8", 128), ("lowoff", 128), ("up8", 128), ("up", 128), ("upinc", 128),
               ("causal", 128), ("seg", 512), ("cos", TOK), ("sin", TOK), ("before", 256), ("own", 128)]
CONST_AT = {}
CONST_W = 0
for _n, _w in CONST_PARTS:
    CONST_AT[_n] = (CONST_W, _w)
    CONST_W += _w

VEC_ROWS = [[("shift_mu", 27), ("w0", 8), ("a0", 8), ("k_k", 8), ("k_a", 8), ("r_k", 8), ("gn_g", 8), ("gn_b", 8)],
            [("ln1_g", 16), ("ln1_b", 16), ("ln2_g", 16), ("ln2_b", 16)],
            [("conv0", 44), ("conv1", 44)],
            [("conv2", 44), ("conv_b", 44)]]
VEC_AT = {}
for _t, _rows in enumerate(VEC_ROWS):
    _r = 0
    for _n, _k in _rows:
        VEC_AT[_n] = _t * P + _r
        _r += _k


def constants():
    c = np.zeros((P, CONST_W), np.float32)
    part = lambda n: c[:, CONST_AT[n][0]:CONST_AT[n][0] + CONST_AT[n][1]]
    i = np.arange(P)
    part("ident")[:] = np.eye(P)
    part("swap")[i, (i + 64) % P] = 1.0
    for h in (0, 64):
        for d in range(8):
            part("rot")[h + d + 8, h + d] = -1.0
            part("rot")[h + d, h + d + 8] = 1.0
    same = (i[:, None] // 64) == (i[None, :] // 64)
    part("headsum")[:] = same
    part("ones")[:] = 1.0
    block = (i[:, None] // 8) == (i[None, :] // 8)
    part("low8")[:] = same & block & (i[:, None] > i[None, :])
    part("lowoff")[:] = same & ~block & (i[:, None] > i[None, :])
    part("up8")[:] = same & block & (i[:, None] < i[None, :])
    part("up")[:] = same & (i[:, None] < i[None, :])
    part("upinc")[:] = same & (i[:, None] <= i[None, :])
    part("causal")[:] = np.where(i[None, :] <= i[:, None], 0.0, NEG)
    part("seg")[:] = (np.arange(SEQ) % CHUNK != 0)[None, :]
    inv = np.power(np.float32(500000.0), -(np.arange(8, dtype=np.float32) * np.float32(2.0) / np.float32(16)))
    pos = np.concatenate([np.arange(SEQ), np.tile(PAST_LEN + np.arange(DEC_SEQ), DEC_BATCH)]).astype(np.float32)
    ang = pos[None, :] * inv.astype(np.float32)[:, None]
    part("cos")[:] = 1.0
    for h in (0, 8, 64, 72):
        part("cos")[h:h + 8] = np.cos(ang)
        part("sin")[h:h + 8] = np.sin(ang)
    b = np.arange(16)
    part("before")[:] = (b[None, :] < b[:, None]).astype(np.float32).reshape(1, 256)
    q_t = (i % 16) // 4
    n = np.arange(N_DEC)
    for bp in range(4):
        mine = (n[None, :] // 4 == 2 * bp + i[:, None] // 64) & (n[None, :] % 4 <= q_t[:, None])
        part("own")[:, bp * N_DEC:(bp + 1) * N_DEC] = np.where(mine, 0.0, NEG)
    return c


def hybrid_layer_kernel(nc, x_prompt, x_sample, cache_k, cache_v, page_table, state_wkv, state_shift, state_conv,
                        w_in, w_out, shift_mu, w0, w2, a0, a2, g2, k_k, k_a, r_k, gn_g, gn_b,
                        ln1_g, ln1_b, ln2_g, ln2_b, w_up, conv_w, conv_b, w_down, consts,
                        y_prompt, y_sample, k_prompt, v_prompt, wkv_prompt, shift_prompt, conv_prompt,
                        k_sample, v_sample, wkv_sample, shift_sample, conv_sample, stop_at=99):
    ctx = ExitStack()
    with ctx:
        def sb(name, shape, dt=F32):
            return ctx.enter_context(nc.sbuf_tensor(name, shape, dt))

        def sem(name):
            return ctx.enter_context(nc.semaphore(name))

        XT = sb("XT", [P, KT, TOK])
        W = sb("W", [P, SLOTS, KT * P])
        BIG = sb("BIG", [P, FT * TOK])
        C = sb("C", [P, CONST_W])
        VC = sb("VC", [P, 4 * P])
        ps = ctx.enter_context(nc.psum_tensor("ps", [P, 8, 512], F32))
        shiftT = sb("shiftT", [P, RW_TILES, DEC_BATCH])
        convT = sb("convT", [P, FT, 2 * DEC_BATCH])
        WORK = sb("WORK", [P, 5120])

        def const(name):
            a, n = CONST_AT[name]
            return C[:, a:a + n]
        ident = const("ident")
        ZT = BIG[:, 0:IN_TILES * TOK].rearrange("p (m t) -> p m t", t=TOK)
        x_tok = BIG[:, 0:5 * D_MODEL].rearrange("p (a n) -> p a n", n=D_MODEL)
        shift_tok = BIG[0:DEC_BATCH, 10240:10240 + 27 * P]
        conv_tok = BIG[0:16, 13824:13824 + D_FF]
        vec_tok = BIG[:, 19456:19456 + 4 * P].rearrange("p (a n) -> p a n", n=P)
        last_tok = WORK[0:33, 0:RW_TILES * P]

        free_areas = [[BIG, 0, ATT_TILES * TOK], [BIG, IN_TILES * TOK, FT * TOK], [W[:, :, :].rearrange("p a n -> p (a n)"), 0, SLOTS * KT * P],
                      [WORK, 0, 5120]]

        def carve(*shape):
            n = math.prod(shape)
            for area in free_areas:
                if area[2] - area[1] >= n:
                    area[1] += n
                    view = area[0][:, area[1] - n:area[1]]
                    if len(shape) > 1:
                        names = "abcd"[:len(shape)]
                        view = view.rearrange(f"p ({' '.join(names)}) -> p {' '.join(names)}", **dict(zip(names, shape)))
                    return view
            raise ValueError(f"no room for {shape}")

        HC = N_CHUNK // 2
        SC = 2
        D3 = BIG[:, 0:8 * TOK].rearrange("p (m t) -> p m t", t=TOK)
        LD, LC, AA, KK, SQ, PX, PY, PN, BON, G = [carve(TOK) for _ in range(10)]
        AB = AA
        LW = carve(3, P)
        AR = carve(HC, 2, P)
        BB, KB, VB = carve(HC, P), carve(HC, P), carve(HC, P)
        Nd, NdT, Lo, AKT, RKT, N4, P1T, P2T, P3T, M4T, GT, R2 = [[carve(SC, P) for _ in range(2)] for _ in range(12)]
        BR, NN, MM, M2, Bx, By, KV = [[carve(2 * SC, P) for _ in range(2)] for _ in range(7)]
        BR = [x.rearrange("p (c w) n -> p c w n", w=2) for x in BR]
        Bx = [x.rearrange("p (c w) n -> p c w n", w=2) for x in Bx]
        By = [x.rearrange("p (c w) n -> p c w n", w=2) for x in By]
        ST = [carve(P), carve(P)]
        WKV = carve(P)
        SVT = sb("SVT", [P, 6, P])

        wt = [W[:, u, :].rearrange("p (k n) -> p k n", n=P) for u in range(SLOTS)]
        win_v = w_in[0].rearrange("(k p) n -> p k n", p=P)

        x_in = sem("x_in")
        consts_in, small_in = sem("consts_in"), sem("small_in")
        pads_zero = sem("pads_zero")
        w_landed = [sem(f"w_landed{u}") for u in range(SLOTS)]
        w_free = [sem(f"w_free{u}") for u in range(SLOTS)]
        acc_free = sem("acc_free")
        xt_mm, xt_ev, xt_ev_b = sem("xt_mm"), sem("xt_ev"), sem("xt_ev_b")
        small_mm, small_ev = sem("small_mm"), sem("small_ev")
        last_mm, last_ev = sem("last_mm"), sem("last_ev")
        stored = sem("stored")
        n_stored = [0]
        STEPS = {"solve_dve": ["p2", "p3", "b0", "b1", "b2", "b3", "g"], "solve_pe": ["s3", "n4", "p3", "m", "m2", "m4", "b3", "g"],
                 "solve_act": ["m", "m2", "m4"]}

        def after(name, step, n, s):
            return (n - 1 - s) * len(STEPS[name]) + 2 * STEPS[name].index(step) + s + 1
        shifted, lora_act = sem("shifted"), sem("lora_act")
        names = ("lw_landed lora_mm lora_ev exp_ev ld_ready lprev_ready kk_raw sq_ready ss_mm ss_max ss_root "
                 "bonus_in bonus_mm bonus_ev ab_ready sv_mm sv_ev sv_out "
                 "solve_dve solve_pe solve_act bd_dve bd_pool bd_act tok_mm tok_ev gram_mm gram_ev s3_ev "
                 "chain_mm chain_ev o_ev o_mm "
                 "wkv_mm wkv_ev pair_pool rw_chain bd_zero")
        S = {n: sem(n) for n in names.split()}
        names = ("sv_in state_in state_out dec_o dec_o_in rec rec_half ot_mm ot_ev "
                 "gn_mu_mm gn_sq gn_var_mm gn_root gn_ev rot_mm rope_ev rope_chain kvt_mm kvt_ev swap_mm kdup_ev qsw_ev qbd_zero qbd_ev kvt_out "
                 "stat_copy sc_mm max_ev pexp_ev pnorm_ev pt_mm pt_ev ao_mm ao_ev att_chain "
                 "page_in kt_ev_a kt_ev_d qk_mm sc_ev soft_ev pexpd_ev ptd_mm ptd_ev pv_mm oq_ev oqt_mm of_ev osw_mm dec_ev dec_chain qb_ev gn_chain")
        S.update({n: sem(n) for n in names.split()})
        names = ("ln_mu_mm ln_sub ln_sq ln_var_mm ln_root ln_rs ln_scaled ln_ev gp_hist gp_zero gate_ev conv_chain conv_ev silu_ev h_ev "
                 "cvn_ev cn_mm cn_ev y_mm y_ev y_out")
        S.update({n: sem(n) for n in names.split()})
        page_landed = [sem(f"page_landed{j}") for j in range(8)]
        page_free = [sem(f"page_free{j}") for j in range(8)]
        shift_chain = sem("shift_chain")
        dec_vecs = nc.dram_tensor("dec_vecs", (6, N_DEC, 1024), F32).ap()
        SVT6 = sb("SVT6", [P, 6 * N_DEC])
        HB = sb("HB", [P, 16])
        dec_out = nc.dram_tensor("dec_out", (N_DEC, 1024), F32).ap()
        pages = sb("pages", [1, DEC_BATCH * N_PAGES], I32)
        eps = sb("eps", [P, 2])
        SV = WORK[:, 0:1536].rearrange("p (v t j) -> p v t j", v=6, j=HD)
        SD = WORK[:, 1536:3584].rearrange("p (i j) -> p i j", j=HD)
        OD = WORK[:, 3584:3840].rearrange("p (t i) -> p t i", i=HD)
        SA = WORK[:, 3840:3872]
        E0 = IN_TILES * TOK
        TD = BIG[:, E0:E0 + 2048].rearrange("p (i j) -> p i j", j=HD)
        o_tok = BIG[0:N_DEC, E0:E0 + 1024]
        XC = [WORK[:, 3872 + SEQ * j:3872 + SEQ * (j + 1)] for j in range(2)]
        SVF = SVT[:, :, :].rearrange("p a n -> p (a n)")
        XS = SVF[:, 0:SEQ]
        XC8 = WORK[:, 3872:3872 + 256]
        XS8 = SVF[:, 0:256]
        F0 = 20 * TOK
        RT = BIG[:, E0 + 2048:E0 + 2048 + TOK]
        KVT = WORK[:, 0:2560].rearrange("p (a n) -> p a n", n=512)
        QBD = WORK[:, 2560:3072].rearrange("p (r b q) -> p r b q", r=2, b=DEC_BATCH)
        QSW = WORK[:, 3072:3328].rearrange("p (f n) -> p f n", n=N_DEC)
        KDUP = BIG[:, F0:F0 + 2048].rearrange("p (v t) -> p v t", t=SEQ)
        OPS = [F0 + 2048, F0 + 8960]
        KC = [BIG[:, o:o + 512] for o in OPS]
        Q2 = [BIG[:, o + 512:o + 1536].rearrange("p (f t) -> p f t", t=SEQ) for o in OPS]
        VS = [BIG[:, o + 1536:o + 1792].rearrange("p (a d) -> p a d", d=HD) for o in OPS]
        BLOCKS = (3, 2, 1, 0)
        PR = [BIG[:, F0 + 3840 + 1280 * j:F0 + 5120 + 1280 * j] for j in range(2)]
        PT = [BIG[:, F0 + 6400 + 1280 * j:F0 + 7680 + 1280 * j] for j in range(2)]
        STAT = WORK[:, 3328:3392].rearrange("p (j k) -> p j k", k=4)
        W2D = W[:, :, :].rearrange("p a n -> p (a n)")
        pg = [W2D[:, 1024 * j:1024 * (j + 1)].rearrange("p (g n) -> p g n", n=256) for j in range(8)]
        SC_W = PAST_LEN + N_DEC
        SCR = BIG[:, F0:F0 + SC_W]
        KTD = [[BIG[:, F0 + 4160 + 1024 * (2 * j + b):F0 + 5184 + 1024 * (2 * j + b)].rearrange("p (r n) -> p r n", n=512)
                for b in range(2)] for j in range(2)]
        PTD = [BIG[:, F0 + 8256 + 512 * j:F0 + 8768 + 512 * j] for j in range(2)]
        PTO = BIG[:, F0 + 9280:F0 + 9408]
        OQ = BIG[:, F0 + 9408:F0 + 9536]
        OF = BIG[:, F0 + 9536:F0 + 9664]
        DS = BIG[:, F0 + 9664:F0 + 9792]
        RK = BIG[:, E0:E0 + 512].rearrange("p (c i j) -> p c i j", c=2, j=16)
        QB = BIG[:, E0 + 512:E0 + 640].rearrange("p (r b q) -> p r b q", r=2, b=2)
        ATT = BIG[:, 0:8 * TOK].rearrange("p (f t) -> p f t", t=TOK)
        HT = BIG[:, :].rearrange("p (f t) -> p f t", t=TOK)
        GPW = SEQ + 2 + DEC_BATCH * (DEC_SEQ + 2)
        GP = [WORK[:, GPW * j:GPW * (j + 1)] for j in range(2)]
        CO = [WORK[:, 2 * GPW + (GPW - 2) * j:2 * GPW + (GPW - 2) * (j + 1)] for j in range(2)]
        co_dec = [WORK[:, 2 * GPW + (GPW - 2) * j + SEQ + 2:2 * GPW + (GPW - 2) * j + SEQ + 2 + 6 * DEC_BATCH]
                  .rearrange("p (b t) -> p b t", t=DEC_SEQ + 2)[:, :, 0:DEC_SEQ] for j in range(2)]
        CVN = WORK[:, 2244:2244 + FT * 18].rearrange("p (f n) -> p f n", n=18)
        LQ = [WORK[:, 3040 + TOK * j:3040 + TOK * (j + 1)] for j in range(2)]
        RS = WORK[:, 4128:4128 + TOK]
        Y = [BIG[:, 2048 * j:2048 * (j + 1)] for j in range(5)]
        CN = BIG[0:18, 10240:10240 + D_FF]
        ROUND_OUT = [10, 10, 10, 9]
        ROUND_UP = [r + 4 for r in ROUND_OUT]
        ROUND_DOWN = [r + 22 for r in ROUND_UP]
        wout_v = w_out[0].rearrange("(k p) n -> p k n", p=P)
        wup_v = w_up[0].rearrange("(k p) n -> p k n", p=P)
        wdown_v = w_down[0].rearrange("(k p) n -> p k n", p=P)

        ck = cache_k[0].rearrange("g p v d -> g p (v d)")
        cv = cache_v[0].rearrange("g p v d -> g p (v d)")

        def load_pages(eng, b):
            eng.wait_ge(S["page_in"], 16)
            for u in range(SLOTS):
                eng.wait_ge(w_free[u], (7 if u < 3 else 6) + 4)
            with eng.Fori(0, 4) as bp:
                for kind, cache in enumerate((ck, cv)):
                    with eng.Fori(0, 2) as r:
                        for c in range(4):
                            j = 2 * c + b
                            eng.wait_ge(page_free[j], 4 * bp + 2 * kind + r + 1)
                            for g in range(4):
                                row = eng.value_load(pages[0:1, bass.ds((2 * bp + b) * N_PAGES + r * 16 + c * 4 + g, 1)])
                                eng.dma_start(pg[j][:, g], cache[bass.ds(row, 1)].rearrange("a p n -> (a p) n")).then_inc(page_landed[j], 16)

        block = ctx.enter_context(nc.Block())

        st_v = state_wkv[0].rearrange("b h i j -> (b h) i j")
        wst_v = wkv_sample[0].rearrange("b h i j -> (b h) i j")

        @block.sync
        def _(sp):
            sp.dma_start(C[:, :], consts).then_inc(consts_in, 16)
            for a in range(4):
                sp.dma_start(x_tok[:, a], x_prompt[0, a * P:(a + 1) * P, :]).then_inc(x_in, 16)
            sp.dma_start(x_tok[0:N_DEC, 4], x_sample.rearrange("b t n -> (b t) n")).then_inc(x_in, 16)
            def load_in(tile, u, rnd, width=P):
                sp.wait_ge(w_free[u], rnd + 1)
                sp.dma_start(wt[u][:, :, 0:width], win_v[:, :, bass.ds(tile * P, width)]).then_inc(w_landed[u], 16)
            sp.wait_ge(pads_zero, 2)
            sp.dma_start(shift_tok[:, 0:RW_PROJ], state_shift[0]).then_inc(small_in, 16)
            sp.dma_start(conv_tok, state_conv[0].rearrange("b r n -> (b r) n")).then_inc(small_in, 16)
            full = 26 * P
            sp.dma_start(vec_tok[0:26, 0], shift_mu[0, 0:full].rearrange("(r n) -> r n", n=P)).then_inc(small_in, 16)
            sp.dma_start(vec_tok[26:27, 0, 0:32], shift_mu[0:1, full:RW_PROJ]).then_inc(small_in, 16)
            for name, src in (("w0", w0), ("a0", a0), ("k_k", k_k), ("k_a", k_a), ("r_k", r_k), ("gn_g", gn_g),
                              ("gn_b", gn_b), ("ln1_g", ln1_g), ("ln1_b", ln1_b), ("ln2_g", ln2_g),
                              ("ln2_b", ln2_b), ("conv_b", conv_b)):
                t, r = divmod(VEC_AT[name], P)
                n = src.shape[1] // P
                sp.dma_start(vec_tok[r:r + n, t], src[0].rearrange("(r n) -> r n", n=P)).then_inc(small_in, 16)
            for j in range(3):
                t, r = divmod(VEC_AT[f"conv{j}"], P)
                sp.dma_start(vec_tok[r:r + FT, t], conv_w[0, j].rearrange("(r n) -> r n", n=P)).then_inc(small_in, 16)
            SMALL = 19
            with sp.Fori(0, 6) as i:
                for u in range(SLOTS):
                    load_in(ATT_TILES + i * SLOTS + u, u, i)
            for u in range(3):
                load_in(ATT_TILES + 24 + u, u, 6, P if u < 2 else LAST_W)
            sp.wait_ge(last_ev, 7)
            sp.dma_start(shift_prompt[0], last_tok[0:1, 0:RW_PROJ]).then_inc(stored, 16)
            for b in range(DEC_BATCH):
                r = 1 + b * DEC_SEQ + DEC_SEQ - 1
                sp.dma_start(shift_sample[0, b:b + 1], last_tok[r:r + 1, 0:RW_PROJ]).then_inc(stored, 16)
            with sp.Fori(0, PAIRS) as p:
                cols = bass.ds(p * P, P)
                sp.wait_ge(S["sv_ev"], p + 1)
                sp.dma_start(dec_vecs[:, :, cols].rearrange("v t n -> t v n"), SVT[0:N_DEC]).then_inc(S["sv_out"], 16)
                sp.wait_ge(S["wkv_ev"], p + 1)
                for e in range(2):
                    sp.dma_start(wkv_prompt[0, 0, bass.ds(p * 2 + e, 1)].rearrange("h i j -> (h i) j"),
                                 WKV[e * 64:e * 64 + 64, e * 64:e * 64 + 64]).then_inc(stored, 16)
            sp.dma_start(pages[0:1, :], page_table.rearrange("(o b) n -> o (b n)", o=1)).then_inc(S["page_in"], 16)
            sp.wait_ge(S["pair_pool"], PAIRS + 1)
            sp.wait_ge(S["ld_ready"], PAIRS + 1)
            for i in range(3):
                for u in range(SLOTS):
                    load_in(ATT_ORDER[i * SLOTS + u], u, (7 if u < 3 else 6) + i)
                if i == 0:
                    sp.wait_ge(S["sv_out"], 16 * PAIRS + 16)
                    for v in range(6):
                        for b in range(DEC_BATCH):
                            sp.dma_start(SV[b * 16:b * 16 + 16, v], dec_vecs[v, b * DEC_SEQ:(b + 1) * DEC_SEQ].rearrange("t (h j) -> h t j", j=HD)).then_inc(S["sv_in"], 16)
            sp.wait_ge(S["kvt_ev"], 5)
            for a in range(4):
                for dst, at in ((k_prompt, 0), (v_prompt, 256)):
                    sp.dma_start(dst[0, 0, a * P:(a + 1) * P].rearrange("t v d -> t (v d)"), KVT[:, a, at:at + 256]).then_inc(S["kvt_out"], 16)
            for dst, at in ((k_sample, 0), (v_sample, 256)):
                sp.dma_start(dst[0].rearrange("b t v d -> (b t) (v d)"), KVT[0:N_DEC, 4, at:at + 256]).then_inc(S["kvt_out"], 16)
            load_pages(sp, 0)
            for j in range(8):
                sp.wait_ge(page_free[j], 17)

            def load(u, rnd, src):
                sp.wait_ge(w_free[u], rnd + 1)
                sp.dma_start(wt[u][:, 0:src.shape[1], :], src).then_inc(w_landed[u], 16)
            with sp.Fori(0, 4) as i:
                for u in range(SLOTS):
                    load(u, ROUND_OUT[u] + i, wout_v[:, :, bass.ds((4 * i + u) * P, P)])
            with sp.Fori(0, FT // 2) as i:
                for u in range(SLOTS):
                    load(u, ROUND_UP[u] + i, wup_v[:, :, bass.ds((2 * i + u // 2) * P + (u % 2) * D_FF, P)])
            with sp.Fori(0, KT) as m:
                for u in range(SLOTS):
                    load(u, ROUND_DOWN[u] + m, wdown_v[:, u * DOWN_K:(u + 1) * DOWN_K, bass.ds(m * P, P)])
            sp.wait_ge(S["cn_ev"], 11)
            sp.dma_start(conv_prompt[0, 0], CN[0:2]).then_inc(S["kvt_out"], 16)
            sp.dma_start(conv_sample[0].rearrange("b r n -> (b r) n"), CN[2:18]).then_inc(S["kvt_out"], 16)
            for a in range(5):
                sp.wait_ge(S["y_ev"], 4 * a + 4)
                if a < 4:
                    sp.dma_start(y_prompt[0, a * P:(a + 1) * P], Y[a]).then_inc(S["y_out"], 16)
                else:
                    sp.dma_start(y_sample.rearrange("b t n -> (b t) n"), Y[4][0:N_DEC]).then_inc(S["y_out"], 16)
            sp.wait_ge(stored, 9 * 16 + 32 * PAIRS)
            sp.wait_ge(S["state_out"], 32)
            sp.wait_ge(S["kvt_out"], 192)
            sp.wait_ge(S["y_out"], 80)

        @block.tensor
        def _(pe):
            for u in range(SLOTS):
                pe.sem_inc(w_free[u], 1)
            pe.wait_ge(consts_in, 16)
            for k in range(KT):
                b0 = 2 * (k % 4)
                if k == 0:
                    pe.wait_ge(x_in, 80)
                if k >= 4:
                    pe.wait_ge(xt_ev, k - 3)
                    pe.wait_ge(xt_ev_b, k - 3)
                for a in range(4):
                    nc.tensor.transpose(ps[:, b0, a * P:(a + 1) * P], x_tok[:, a, k * P:(k + 1) * P], ident)
                nc.tensor.transpose(ps[:, b0 + 1, 0:N_DEC], x_tok[0:N_DEC, 4, k * P:(k + 1) * P],
                                    ident[0:N_DEC, 0:N_DEC]).then_inc(xt_mm, 1)
            pe.wait_ge(small_in, 19 * 16)
            pe.wait_ge(xt_ev, KT)
            pe.wait_ge(xt_ev_b, KT)
            for t in range(4):
                n = sum(k for _, k in VEC_ROWS[t])
                nc.tensor.transpose(ps[:, 0, t * P:t * P + n], vec_tok[0:n, t], ident[0:n, 0:n])
            for m in range(RW_TILES):
                nc.tensor.transpose(ps[:, 1, m * 8:m * 8 + 8], shift_tok[:, m * P:(m + 1) * P], ident[0:8, 0:8])
            for f in range(FT):
                last = nc.tensor.transpose(ps[:, 2 + f // 32, (f % 32) * 16:(f % 32) * 16 + 16],
                                           conv_tok[:, f * P:(f + 1) * P], ident[0:16, 0:16])
            last.then_inc(small_mm, 1)
            pe.wait_ge(small_ev, 4)

            def dense(u, rnd, n, acc, width=P):
                pe.wait_ge(w_landed[u], (rnd + 1) * 16)
                pe.wait_ge(acc_free, n + 1)
                for k in range(KT):
                    for h in range(2):
                        last = nc.tensor.matmul(ps[0:width, 2 * acc + h, 0:HALF], wt[u][:, k, 0:width],
                                                XT[:, k, h * HALF:(h + 1) * HALF], start=k == 0, stop=k == KT - 1)
                last.then_inc(w_free[u], 1)

            with pe.Fori(0, 6) as i:
                for u in range(SLOTS):
                    dense(u, i, i * SLOTS + u, u % 2)
            for u in range(3):
                dense(u, 6, 24 + u, u % 2, P if u < 2 else LAST_W)
            pe.wait_ge(acc_free, RW_TILES + 2)
            for m in range(RW_TILES):
                w = P if m < RW_TILES - 1 else LAST_W
                bank = 4 + (m // 4) % 4
                if m // 4 >= 4:
                    pe.wait_ge(last_ev, m // 4 - 3)
                last = nc.tensor.transpose(ps[0:33, bank, (m % 4) * P:(m % 4) * P + w],
                                           ZT[0:w, ATT_TILES + m, SEQ - 1:TOK], ident[0:w, 0:w])
                if m % 4 == 3 or m == RW_TILES - 1:
                    last.then_inc(last_mm, 1)

            pe.sem_inc(S["lora_mm"], 1)
            pe.wait_ge(shifted, 1)
            pe.wait_ge(lora_act, 3)
            pe.wait_ge(S["bd_zero"], 6)
            headsum = const("headsum")
            BOTH = range(2)

            with pe.Fori(0, PAIRS) as p:
                pe.wait_ge(S["lw_landed"], 64 * p + 64)
                halves = [slice(h * HALF, (h + 1) * HALF) for h in BOTH]
                for h in BOTH:
                    last = nc.tensor.matmul(ps[:, 0 + h, 0:HALF], LW[0:64, 0], ZT[0:64, 36, halves[h]], start=True, stop=True)
                last.then_inc(S["lora_mm"], 1)
                for h in BOTH:
                    last = nc.tensor.matmul(ps[:, 2 + h, 0:HALF], LW[64:128, 0], ZT[64:128, 36, halves[h]], start=True, stop=True)
                last.then_inc(S["lora_mm"], 1)
                pe.wait_ge(S["sq_ready"], p + 1)
                for h in BOTH:
                    last = nc.tensor.matmul(ps[:, 6 + h, 0:HALF], headsum, SQ[:, halves[h]], start=True, stop=True)
                last.then_inc(S["ss_mm"], 1)
                for h in BOTH:
                    nc.tensor.matmul(ps[:, 4 + h, 0:HALF], LW[:, 1], ZT[:, 37, halves[h]], start=True, stop=False)
                    last = nc.tensor.matmul(ps[:, 4 + h, 0:HALF], LW[0:32, 2], ZT[0:32, 38, halves[h]], start=False, stop=True)
                last.then_inc(S["lora_mm"], 1)
                pe.wait_ge(S["bonus_in"], p + 1)
                for h in BOTH:
                    last = nc.tensor.matmul(ps[:, 6 + h, 0:HALF], headsum, BON[:, h * HALF:(h + 1) * HALF], start=True, stop=True)
                last.then_inc(S["bonus_mm"], 1)
                pe.wait_ge(S["ab_ready"], p + 1)
                pe.wait_ge(S["exp_ev"], 4 * p + 4)
                rz, kz, vz = (ZT[:, bass.ds(ATT_TILES + 8 * j + p, 1), SEQ:TOK].rearrange("p a t -> p (a t)") for j in range(3))
                for j in range(6):
                    src = SVT6[:, j * N_DEC:(j + 1) * N_DEC]
                    last = nc.tensor.transpose(ps[0:N_DEC, j // 4, (j % 4) * P:(j % 4) * P + P], src, ident)
                last.then_inc(S["sv_mm"], 1)
                pe.wait_ge(S["sv_ev"], p + 1)
                for h in BOTH:
                    hp = 2 * p + h
                    pe.wait_ge(S["bd_dve"], hp + 1)
                    pe.wait_ge(S["bd_pool"], hp + 1)
                    pe.wait_ge(S["bd_act"], hp + 1)
                    pe.wait_ge(S["bonus_ev"], p + 1)
                    pe.wait_ge(S["lora_ev"], 3 * p + 3)
                    for s in BOTH:
                        if h or s:
                            pe.wait_ge(S["tok_ev"], 3 * (4 * p + 2 * h + s))
                        if h and not s:
                            pe.wait_ge(S["chain_ev"], 8 * p + 5)
                            pe.wait_ge(S["o_ev"], 8 * p + 4)
                        for c in range(SC):
                            for j, src in enumerate((AR[:, s * SC + c, 0], BB[:, s * SC + c])):
                                nc.tensor.transpose(ps[:, 6, (j * SC + c) * P:(j * SC + c + 1) * P], src, ident)
                            for j, src in enumerate((KB[:, s * SC + c], VB[:, s * SC + c])):
                                last = nc.tensor.transpose(ps[:, 7, (j * SC + c) * P:(j * SC + c + 1) * P], src, ident)
                        last.then_inc(S["tok_mm"], 1)
                        for c in range(SC):
                            x = s * SC + c
                            nc.tensor.matmul(ps[:, 3 * s, c * 256:(c + 1) * 256], BB[:, x], AR[:, x], start=True, stop=True)
                            nc.tensor.matmul(ps[:, 3 * s + 1, c * 256:(c + 1) * 256], KB[:, x], AR[:, x], start=True, stop=True)
                            last = nc.tensor.matmul(ps[:, 3 * s + 2, c * P:(c + 1) * P], AR[:, x, 0], BB[:, x], start=True, stop=True)
                        last.then_inc(S["gram_mm"], 1)

                    def products(s, items):
                        for c in range(SC):
                            for bank, at, width, lhsT, rhs in items:
                                last = nc.tensor.matmul(ps[:, bank, at + c * width:at + (c + 1) * width], lhsT(c), rhs(c), start=True, stop=True)
                        last.then_inc(S["solve_pe"], 1)

                    for s in BOTH:
                        n = 4 * p + 2 * h + s + 1
                        pe.wait_ge(S["gram_ev"], 2 * n - 1)
                        pe.wait_ge(S["tok_ev"], 3 * n)
                        products(s, [(3 * s, 0, P, lambda c: NdT[s][:, c], lambda c: Nd[s][:, c]),
                                              (3 * s, 256, P, lambda c: Nd[s][:, c], lambda c: NdT[s][:, c]),
                                              (3 * s + 1, 0, P, lambda c: AKT[s][:, c], lambda c: KV[s][:, SC + c])])
                    for s in BOTH:
                        n = 4 * p + 2 * h + s + 1
                        pe.wait_ge(S["s3_ev"], 2 * n)
                        pe.wait_ge(S["gram_ev"], 2 * n)
                        products(s, [(3 * s + 2, 0, P, lambda c: NN[s][:, SC + c], lambda c: NN[s][:, c]),
                                              (3 * s + 2, 256, P, lambda c: NN[s][:, c], lambda c: P1T[s][:, c])])
                    for s in BOTH:
                        n = 4 * p + 2 * h + s + 1
                        pe.wait_ge(S["solve_dve"], after("solve_dve", "p2", n, s))
                        products(s, [(3 * s, 0, P, lambda c: N4[s][:, c], lambda c: P2T[s][:, c])])
                    for s in BOTH:
                        n = 4 * p + 2 * h + s + 1
                        pe.wait_ge(S["solve_dve"], after("solve_dve", "p3", n, s))
                        products(s, [(3 * s + 1, 0, P, lambda c: P3T[s][:, c], lambda c: Lo[s][:, c]),
                                             (3 * s + 1, 256, P, lambda c: Lo[s][:, c], lambda c: P3T[s][:, c]),
                                             (3 * s + 2, 0, 256, lambda c: P3T[s][:, c], lambda c: Bx[s][:, c])])
                    for s in BOTH:
                        n = 4 * p + 2 * h + s + 1
                        pe.wait_ge(S["solve_act"], after("solve_act", "m", n, s))
                        pe.wait_ge(S["solve_dve"], after("solve_dve", "b0", n, s))
                        products(s, [(3 * s, 0, P, lambda c: MM[s][:, SC + c], lambda c: MM[s][:, c]),
                                              (3 * s, 256, P, lambda c: MM[s][:, c], lambda c: MM[s][:, SC + c]),
                                              (3 * s + 1, 0, 256, lambda c: MM[s][:, SC + c], lambda c: By[s][:, c])])
                    for s in BOTH:
                        n = 4 * p + 2 * h + s + 1
                        pe.wait_ge(S["solve_act"], after("solve_act", "m2", n, s))
                        pe.wait_ge(S["solve_dve"], after("solve_dve", "b1", n, s))
                        products(s, [(3 * s, 0, P, lambda c: M2[s][:, c], lambda c: M2[s][:, SC + c]),
                                              (3 * s + 2, 0, 256, lambda c: M2[s][:, SC + c], lambda c: Bx[s][:, c])])
                    for s in BOTH:
                        n = 4 * p + 2 * h + s + 1
                        pe.wait_ge(S["solve_act"], after("solve_act", "m4", n, s))
                        pe.wait_ge(S["solve_dve"], after("solve_dve", "b2", n, s))
                        products(s, [(3 * s + 1, 0, 256, lambda c: M4T[s][:, c], lambda c: By[s][:, c])])
                    for s in BOTH:
                        n = 4 * p + 2 * h + s + 1
                        pe.wait_ge(S["solve_dve"], after("solve_dve", "b3", n, s))
                        products(s, [(3 * s + 2, 0, 256, lambda c: Bx[s][:, c, 0], lambda c: BR[s][:, c])])
                    for s in BOTH:
                        n = 4 * p + 2 * h + s + 1
                        pe.wait_ge(S["solve_dve"], after("solve_dve", "g", n, s))
                        for c in range(SC):
                            x = s * SC + c
                            g = 4 * h + x
                            state, out = ps[:, 6 + g % 2, 0:P], ps[:, (0, 1, 3, 4)[x], 0:P]
                            if g:
                                pe.wait_ge(S["chain_ev"], 8 * p + g)
                            nc.tensor.matmul(state, BR[s][:, c, 0], Bx[s][:, c, 1], start=True, stop=False)
                            nc.tensor.matmul(state, KV[s][:, c], KV[s][:, SC + c], start=False, stop=False)
                            nc.tensor.matmul(out, Bx[s][:, c, 1], BR[s][:, c, 1], start=True, stop=False)
                            nc.tensor.matmul(out, KV[s][:, SC + c], RKT[s][:, c], start=False, stop=False)
                            pe.wait_ge(S["chain_ev"], 8 * p + g + 1)
                            if g == 0:
                                pe.wait_ge(S["ld_ready"], p + 1)
                            old = ST[g % 2]
                            nc.tensor.matmul(state, GT[s][:, c], old, start=False, stop=True).then_inc(S["chain_mm"], 1)
                            nc.tensor.matmul(out, old, R2[s][:, c], start=False, stop=True).then_inc(S["o_mm"], 1)
                pe.wait_ge(S["chain_ev"], 8 * p + 9)
                nc.tensor.transpose(ps[:, 6, 0:P], ST[0], ident).then_inc(S["wkv_mm"], 1)
                pe.wait_ge(S["o_ev"], 8 * p + 8)

            pe.wait_ge(S["pair_pool"], PAIRS + 1)
            pe.wait_ge(S["ld_ready"], PAIRS + 1)
            pe.wait_ge(S["wkv_ev"], PAIRS)
            pe.wait_ge(acc_free, RW_TILES + 2)
            def rotate(r):
                if r:
                    pe.wait_ge(S["rope_ev"], r)
                for h in BOTH:
                    last = nc.tensor.matmul(ps[:, 4 + h, 0:HALF], const("rot"), ZT[:, ROPE_TILES[r], h * HALF:(h + 1) * HALF], start=True, stop=True)
                last.then_inc(S["rot_mm"], 1)
            for t in range(ATT_TILES):
                u = t % SLOTS
                dense(u, (7 if u < 3 else 6) + t // SLOTS, RW_TILES + t, u % 2)
                if t and ATT_ORDER[t - 1] in ROPE_TILES:
                    pe.wait_ge(acc_free, RW_TILES + t + 2)
                    rotate(ROPE_TILES.index(ATT_ORDER[t - 1]))
                if 1 <= t <= PAIRS:
                    pe.wait_ge(S["gn_sq"], t)
                    if t > 1:
                        pe.wait_ge(S["gn_root"], 2 * t - 3)
                    nc.tensor.matmul(ps[:, 7, :], headsum, XS, start=True, stop=True).then_inc(S["gn_var_mm"], 1)
                if t < PAIRS:
                    nc.tensor.matmul(ps[:, 6, :], headsum, ZT[:, ATT_TILES + t, 0:SEQ], start=True, stop=True).then_inc(S["gn_mu_mm"], 1)
            for u in range(8):
                pe.sem_inc(page_free[u], 1)
            pe.wait_ge(acc_free, RW_TILES + ATT_TILES + 2)
            rotate(len(ROPE_TILES) - 1)
            pe.wait_ge(S["dec_o_in"], 16)
            pe.wait_ge(S["rope_ev"], 10)
            for f in range(8):
                last = nc.tensor.transpose(ps[:, 4, f * N_DEC:(f + 1) * N_DEC], o_tok[:, f * P:(f + 1) * P], ident[0:N_DEC, 0:N_DEC])
            last.then_inc(S["ot_mm"], 1)
            pe.wait_ge(S["ot_ev"], 1)
            nc.tensor.matmul(ps[:, 6, 0:256], headsum, ZT[:, ATT_TILES:ATT_TILES + 8, SEQ:TOK], start=True, stop=True).then_inc(S["gn_mu_mm"], 1)
            for a in range(5):
                n = P if a < 4 else N_DEC
                if a == 4:
                    pe.wait_ge(S["ot_ev"], 1)
                for m in range(4):
                    last = nc.tensor.transpose(ps[0:n, a, m * P:(m + 1) * P], ZT[:, 8 + m, a * P:a * P + n], ident)
                last.then_inc(S["kvt_mm"], 1)
            pe.wait_ge(S["gn_sq"], PAIRS + 1)
            nc.tensor.matmul(ps[:, 7, 0:256], headsum, XS8, start=True, stop=True).then_inc(S["gn_var_mm"], 1)
            pe.wait_ge(S["gn_root"], 2 * PAIRS + 1)
            pe.wait_ge(S["gn_chain"], 4 * PAIRS + 1)
            for m in range(2):
                last = nc.tensor.matmul(ps[:, 5 + m, :], const("swap"), ZT[:, 8 + m, 0:SEQ], start=True, stop=True)
            last.then_inc(S["swap_mm"], 1)
            nc.tensor.matmul(ps[:, 7, 0:256], const("swap"), ZT[:, 0:8, SEQ:TOK], start=True, stop=True).then_inc(S["swap_mm"], 1)

            pe.wait_ge(S["kvt_ev"], 5)
            pe.wait_ge(S["kdup_ev"], 1)
            pe.wait_ge(S["qsw_ev"], 1)
            with pe.Fori(0, 2) as v:

                def head_scores(hd):
                    f, e = divmod(hd % 4, 2)
                    n = 8 * v + hd
                    j = hd // 4
                    rows = slice(e * 64, e * 64 + 64)
                    if hd % 4 == 0:
                        pe.wait_ge(S["stat_copy"], 2 * v + j + 1)
                    for k, i in enumerate(BLOCKS):
                        pe.wait_ge(S["pexp_ev"], 4 * n + k + 1)
                        nc.tensor.matmul(ps[:, i, 0:(i + 1) * P], Q2[j][rows, f, i * P:(i + 1) * P], KC[j][rows, 0:(i + 1) * P],
                                         start=True, stop=False, skip_group_check=True)
                        nc.tensor.matmul(ps[:, i, i * P:(i + 1) * P], ident, const("causal"),
                                         start=False, stop=True, skip_group_check=True).then_inc(S["sc_mm"], 1)
                head_scores(0)
                for hd in range(8):
                    e = hd % 2
                    j = hd // 4
                    rows = slice(e * 64, e * 64 + 64)
                    n = 8 * v + hd
                    if hd < 7:
                        head_scores(hd + 1)
                    pe.wait_ge(S["pnorm_ev"], n + 1)
                    for a in range(4):
                        pe.wait_ge(S["pt_ev"], 4 * n + a + 2)
                        for i in range(a, 4):
                            off = i * (i + 1) // 2 * P
                            last = nc.tensor.transpose(ps[:, 4 + a % 3, (i - a) * P:(i - a + 1) * P], PR[hd % 2][:, off + a * P:off + (a + 1) * P], ident)
                        last.then_inc(S["pt_mm"], 1)
                    if e == 0:
                        pe.wait_ge(S["ao_ev"], 4 * v + hd // 2 + 1)
                    for a in range(4):
                        pe.wait_ge(S["pt_ev"], 4 * n + a + 4)
                        toff = sum(4 - x for x in range(a)) * P
                        last = nc.tensor.matmul(ps[rows, 7, a * P:512], VS[j][:, a], PT[hd % 2][:, toff:toff + (4 - a) * P],
                                                start=a == 0, stop=a == 3, skip_group_check=True)
                    last.then_inc(S["ao_mm"], 1)

            pe.wait_ge(S["ao_ev"], 9)
            pe.wait_ge(S["qbd_ev"], 1)
            with pe.Fori(0, 4) as bp:
                pe.wait_ge(S["qb_ev"], bp + 1)
                pe.wait_ge(S["dec_ev"], bp + 1)
                qb = lambda r, b: QB[:, r, b]

                def scores(c):
                    n = 8 * bp + c
                    pe.wait_ge(S["kt_ev_a"], n + 1)
                    pe.wait_ge(S["kt_ev_d"], n + 1)
                    pe.wait_ge(S["sc_ev"], 2 * n + 2)
                    for b in BOTH:
                        for r in BOTH:
                            o = 32 * (2 * b + r)
                            last = nc.tensor.matmul(ps[o:o + 32, 4 + c % 2, :], qb(r, b), KTD[c % 2][b][:, r], start=True, stop=True,
                                                    skip_group_check=True)
                    last.then_inc(S["qk_mm"], 1)
                for c in range(8):
                    n = 8 * bp + c
                    for b in BOTH:
                        j = (2 * c + b) % 8
                        pe.wait_ge(page_landed[j], 64 * (4 * bp + c // 4) + 64)
                        if b == 0:
                            if c:
                                pe.wait_ge(S["kt_ev_a"], n)
                        else:
                            if c:
                                pe.wait_ge(S["kt_ev_d"], n)
                        for r in BOTH:
                            for g in range(4):
                                last = nc.tensor.transpose(ps[:, 2 * b + r, g * P:(g + 1) * P], pg[j][:, g, r * P:(r + 1) * P], ident)
                        last.then_inc(page_free[j], 1)
                    if c:
                        scores(c - 1)
                scores(7)
                pe.wait_ge(S["sc_ev"], 16 * bp + 16)
                for b in BOTH:
                    for r in BOTH:
                        o = 32 * (2 * b + r)
                        last = nc.tensor.matmul(ps[o:o + 32, 6, 0:N_DEC], qb(r, b), ZT[:, 8 + r, SEQ:TOK], start=True, stop=True, skip_group_check=True)
                last.then_inc(S["qk_mm"], 1)
                pe.wait_ge(S["pexpd_ev"], bp + 1)
                nc.tensor.transpose(ps[0:N_DEC, 6, 0:P], SCR[:, PAST_LEN:SC_W], ident).then_inc(S["ptd_mm"], 1)

                def values(c):
                    pe.wait_ge(S["ptd_ev"], 9 * bp + c + 2)
                    for b in BOTH:
                        j = (2 * c + b) % 8
                        pe.wait_ge(page_landed[j], 64 * (4 * bp + 2 + c // 4) + 64)
                        for r in BOTH:
                            o = 32 * (2 * b + r)
                            for g in range(4):
                                last = nc.tensor.matmul(ps[o:o + 32, 7, 0:P], PTD[c % 2][:, g * P + o:g * P + o + 32],
                                                        pg[j][:, g, r * P:(r + 1) * P], start=(c == 0 and g == 0), stop=False, skip_group_check=True)
                        last.then_inc(page_free[j], 1)
                for c in range(8):
                    if c >= 2:
                        pe.wait_ge(S["ptd_ev"], 9 * bp + c)
                    for g in range(4):
                        last = nc.tensor.transpose(ps[:, 4 + c % 2, g * P:(g + 1) * P], SCR[:, (4 * c + g) * P:(4 * c + g + 1) * P], ident)
                    last.then_inc(S["ptd_mm"], 1)
                    if c:
                        values(c - 1)
                values(7)
                for b in BOTH:
                    for r in BOTH:
                        o = 32 * (2 * b + r)
                        last = nc.tensor.matmul(ps[o:o + 32, 7, 0:P], PTO[0:N_DEC, o:o + 32], KVT[0:N_DEC, 4, 256 + r * P:256 + (r + 1) * P],
                                                start=False, stop=True, skip_group_check=True)
                last.then_inc(S["pv_mm"], 1)
                pe.wait_ge(S["oq_ev"], bp + 1)
                nc.tensor.transpose(ps[:, 0, 0:P], OQ, ident).then_inc(S["oqt_mm"], 1)
                pe.wait_ge(S["of_ev"], bp + 1)
                nc.tensor.matmul(ps[:, 1, 0:P], const("swap"), OF, start=True, stop=True).then_inc(S["osw_mm"], 1)

            pe.wait_ge(S["dec_ev"], 5)
            with pe.Fori(0, 4) as i:
                for u in range(SLOTS):
                    pe.wait_ge(w_landed[u], (ROUND_OUT[u] + i + 1) * 16)
                    pe.wait_ge(acc_free, IN_TILES + 4 * i + u + 1)
                    for k in range(KT):
                        for h in range(2):
                            last = nc.tensor.matmul(ps[:, 2 * (u % 2) + h, 0:HALF], wt[u][:, k], ZT[:, k if k < 8 else k + 4, h * HALF:(h + 1) * HALF],
                                                    start=k == 0, stop=k == KT - 1)
                    last.then_inc(w_free[u], 1)

            def layer_norm(which):
                for k in range(KT):
                    for h in range(2):
                        last = nc.tensor.matmul(ps[:, 4 + h, 0:HALF], const("ones"), XT[:, k, h * HALF:(h + 1) * HALF], start=k == 0, stop=k == KT - 1)
                last.then_inc(S["ln_mu_mm"], 1)
                for k in range(KT):
                    pe.wait_ge(S["ln_sq"], KT * which + k + 1)
                    for h in range(2):
                        last = nc.tensor.matmul(ps[:, 6 + h, 0:HALF], const("ones"), LQ[k % 2][:, h * HALF:(h + 1) * HALF], start=k == 0, stop=k == KT - 1)
                    last.then_inc(S["ln_var_mm"], 1)
            pe.wait_ge(acc_free, IN_TILES + KT + 2)
            layer_norm(0)
            pe.wait_ge(S["ln_root"], 1)

            def up_tile(u, rnd, f, b0, normed=False):
                pe.wait_ge(w_landed[u], (rnd + 1) * 16)
                pe.wait_ge(S["h_ev" if u % 2 else "gate_ev"], f + 1)
                for k in range(KT):
                    if normed:
                        pe.wait_ge(S["ln_ev"], k + 1)
                    for h in range(2):
                        last = nc.tensor.matmul(ps[:, b0 + 2 * (u % 2) + h, 0:HALF], wt[u][:, k], XT[:, k, h * HALF:(h + 1) * HALF],
                                                start=k == 0, stop=k == KT - 1)
                last.then_inc(w_free[u], 1)
            for u in range(SLOTS):
                up_tile(u, ROUND_UP[u], u // 2, 4 * (u // 2), u == 0)
            with pe.Fori(1, FT // 2) as i:
                for u in range(SLOTS):
                    up_tile(u, ROUND_UP[u] + i, 2 * i + u // 2, 4 * (u // 2))
            pe.wait_ge(S["h_ev"], FT + 2)
            with pe.Fori(0, KT // 2) as i:
                for m in range(2):
                    pe.wait_ge(acc_free, IN_TILES + KT + 2 * i + m + 1)
                    for u in range(SLOTS):
                        pe.wait_ge(w_landed[u], (ROUND_DOWN[u] + 2 * i + m + 1) * 16)
                        for k in range(DOWN_K):
                            for h in range(2):
                                last = nc.tensor.matmul(ps[:, 2 * m + h, 0:HALF], wt[u][:, k], HT[:, u * DOWN_K + k, h * HALF:(h + 1) * HALF],
                                                        start=u == 0 and k == 0, stop=u == SLOTS - 1 and k == DOWN_K - 1)
                        last.then_inc(w_free[u], 1)
            for g in range(11):
                if g >= 4:
                    pe.wait_ge(S["cn_ev"], g - 3)
                if g == 0:
                    pe.wait_ge(acc_free, IN_TILES + 2 * KT + 2)
                    pe.wait_ge(S["cvn_ev"], FT + 2)
                for j in range(4):
                    last = nc.tensor.transpose(ps[0:18, g % 4, j * P:(j + 1) * P], CVN[:, 4 * g + j], ident)
                last.then_inc(S["cn_mm"], 1)
            layer_norm(1)
            for a in range(5):
                n = P if a < 4 else N_DEC
                for q in range(4):
                    if a == 0:
                        pe.wait_ge(S["ln_ev"], KT + 4 * q + 4)
                        pe.wait_ge(S["cn_ev"], 11)
                    else:
                        pe.wait_ge(S["y_ev"], 4 * a - 3 + q)
                    for j in range(4):
                        last = nc.tensor.transpose(ps[0:n, q, j * P:(j + 1) * P], XT[:, 4 * q + j, a * P:a * P + n], ident)
                    last.then_inc(S["y_mm"], 1)

        @block.scalar
        def _(act):
            for k in range(KT):
                act.wait_ge(xt_mm, k + 1)
                nc.scalar.activation(XT[:, k, 0:SEQ], ps[:, 2 * (k % 4), :], ACT.Copy).then_inc(xt_ev, 1)
            act.sem_inc(acc_free, 2)

            def evac(u, rnd, tile, acc, width=P):
                act.wait_ge(w_free[u], rnd + 2)
                nc.scalar.activation(ZT[0:width, bass.ds(tile, 1), :].rearrange("p a (h t) -> p (a h) t", h=2),
                                     ps[0:width, 2 * acc:2 * acc + 2, 0:HALF], ACT.Copy).then_inc(acc_free, 1)
            with act.Fori(0, 6) as i:
                for u in range(SLOTS):
                    evac(u, i, ATT_TILES + i * SLOTS + u, u % 2)
            for u in range(3):
                evac(u, 6, ATT_TILES + 24 + u, u % 2, P if u < 2 else LAST_W)

            act.wait_ge(shifted, 1)
            nc.scalar.activation(ZT[0:64, 36, :], ZT[0:64, 36, :], ACT.Tanh).then_inc(lora_act, 1)
            nc.scalar.activation(ZT[:, 37, :], ZT[:, 37, :], ACT.Sigmoid).then_inc(lora_act, 1)
            nc.scalar.activation(ZT[0:32, 38, :], ZT[0:32, 38, :], ACT.Sigmoid).then_inc(lora_act, 1)
            BOTH = range(2)
            two = lambda x: x.rearrange("p (h t) -> p h t", h=2)
            with act.Fori(0, PAIRS) as p:
                act.wait_ge(S["kk_raw"], p + 1)
                nc.scalar.activation(SQ, KK, ACT.Square).then_inc(S["sq_ready"], 1)
                act.wait_ge(S["lora_mm"], 3 * p + 2)
                nc.scalar.activation(two(LD), ps[:, 0:2, 0:HALF], ACT.Tanh, bias=HB[:, bass.ds(p, 1)], scale=0.5).then_inc(S["lora_ev"], 1)
                act.wait_ge(S["lora_mm"], 3 * p + 3)
                nc.scalar.activation(two(AA), ps[:, 2:4, 0:HALF], ACT.Tanh, bias=HB[:, bass.ds(8 + p, 1)], scale=0.5).then_inc(S["lora_ev"], 1)
                act.wait_ge(S["ss_max"], p + 1)
                nc.scalar.activation(SQ, SQ, ACT.Ln).then_inc(S["ss_root"], 1)
                act.wait_ge(S["ss_root"], 2 * p + 1)
                nc.scalar.activation(SQ, SQ, ACT.Exp, scale=-0.5).then_inc(S["ss_root"], 1)
                act.wait_ge(S["lprev_ready"], p + 1)
                nc.scalar.activation(PY[:, 0:SEQ], PY[:, 0:SEQ], ACT.Exp).then_inc(S["exp_ev"], 1)
                nc.scalar.activation(PN[:, 0:SEQ], LC[:, 0:SEQ], ACT.Exp, scale=-1.0).then_inc(S["exp_ev"], 1)
                nc.scalar.activation(PX[:, 0:SEQ], LC[:, 0:SEQ], ACT.Exp).then_inc(S["exp_ev"], 1)
                nc.scalar.activation(SVT6[:, 5 * N_DEC:6 * N_DEC], LD[:, SEQ:TOK], ACT.Exp).then_inc(S["exp_ev"], 1)
                act.wait_ge(S["lora_mm"], 3 * p + 4)
                act.wait_ge(S["pair_pool"], p + 1)
                nc.scalar.activation(two(G), ps[:, 4:6, 0:HALF], ACT.Copy).then_inc(S["lora_ev"], 1)
                act.wait_ge(S["sv_mm"], p + 1)
                act.wait_ge(S["sv_out"], 16 * p + 16)
                sv = SVT[0:N_DEC].rearrange("p a n -> p (a n)")
                nc.scalar.activation(sv[:, 0:512], ps[0:N_DEC, 0, :], ACT.Copy)
                nc.scalar.activation(sv[:, 512:768], ps[0:N_DEC, 1, 0:256], ACT.Copy).then_inc(S["sv_ev"], 1)
                for h in BOTH:
                    hp = 2 * p + h
                    if h:
                        act.wait_ge(S["gram_mm"], 4 * p + 2)
                    for e in BOTH:
                        rows = slice(e * 64, e * 64 + 64)
                        v = ZT[rows, bass.ds(ATT_TILES + 16 + p, 1), h * 256:(h + 1) * 256].rearrange("p a (c t) -> p (a c) t", t=CHUNK)
                        last = nc.scalar.activation(VB[rows, :, e * 64:e * 64 + 64], v, ACT.Copy)
                    last.then_inc(S["bd_act"], 1)
                    for s in BOTH:
                        n = 4 * p + 2 * h + s + 1
                        act.wait_ge(S["tok_mm"], n)
                        if h and not s:
                            act.wait_ge(S["o_mm"], 8 * p + 4)
                            act.wait_ge(S["solve_dve"], after("solve_dve", "g", 4 * p + 2, 1))
                        nc.scalar.activation(Bx[s][:, :, 0], ps[:, 6, 0:256].rearrange("p (c n) -> p c n", n=P), ACT.Copy).then_inc(S["tok_ev"], 1)
                        nc.scalar.activation(BR[s][:, :, 0], ps[:, 6, 256:512].rearrange("p (c n) -> p c n", n=P), ACT.Copy).then_inc(S["tok_ev"], 1)
                        nc.scalar.activation(KV[s], ps[:, 7, :].rearrange("p (c n) -> p c n", n=P), ACT.Copy).then_inc(S["tok_ev"], 1)
                    for s in BOTH:
                        act.wait_ge(S["solve_pe"], after("solve_pe", "s3", 4 * p + 2 * h + s + 1, s))
                        nc.scalar.activation(NN[s], ps[:, 3 * s, :].rearrange("p (c n) -> p c n", n=P), ACT.Copy).then_inc(S["s3_ev"], 1)
                        nc.scalar.activation(Bx[s][:, :, 1], ps[:, 3 * s + 1, 0:256].rearrange("p (c n) -> p c n", n=P), ACT.Copy).then_inc(S["s3_ev"], 1)
                    for step, dst, bank, width in (("m", MM, 1, 512), ("m2", M2, 0, 512), ("m4", M4T, 0, 256)):
                        for s in BOTH:
                            act.wait_ge(S["solve_pe"], after("solve_pe", step, 4 * p + 2 * h + s + 1, s))
                            nc.scalar.activation(dst[s], ps[:, 3 * s + bank, 0:width].rearrange("p (c n) -> p c n", n=P), ACT.Copy).then_inc(S["solve_act"], 1)
                    for x in range(HC):
                        act.wait_ge(S["o_mm"], 8 * p + 4 * h + x + 1)
                        for e in BOTH:
                            rows = slice(e * 64, e * 64 + 64)
                            t0 = (4 * h + x) * CHUNK
                            last = nc.scalar.activation(ZT[rows, bass.ds(ATT_TILES + p, 1), t0:t0 + CHUNK].rearrange("p a t -> p (a t)"),
                                                        ps[rows, (0, 1, 3, 4)[x], e * 64:e * 64 + 64], ACT.Copy)
                        last.then_inc(S["o_ev"], 1)
                act.wait_ge(S["wkv_mm"], p + 1)
                act.wait_ge(stored, 9 * 16 + 32 * p)
                nc.scalar.activation(WKV, ps[:, 6, 0:P], ACT.Copy).then_inc(S["wkv_ev"], 1)

            def group_norm(t):
                if 1 <= t <= PAIRS:
                    act.wait_ge(S["gn_var_mm"], t)
                    nc.scalar.activation(XS, ps[:, 7, :], ACT.Ln, bias=eps[:, 0:1], scale=1.0 / HD).then_inc(S["gn_root"], 1)
                    act.wait_ge(S["gn_root"], 2 * t - 1)
                    nc.scalar.activation(XS, XS, ACT.Exp, scale=-0.5).then_inc(S["gn_root"], 1)
                if t < PAIRS:
                    act.wait_ge(S["gn_chain"], 4 * t + 1)
                    nc.scalar.activation(XS, XC[t % 2], ACT.Square).then_inc(S["gn_sq"], 1)
            for i in range(3):
                for u in range(SLOTS):
                    evac(u, (7 if u < 3 else 6) + i, ATT_ORDER[4 * i + u], u % 2)
                    group_norm(4 * i + u)
            act.wait_ge(S["gn_chain"], 4 * PAIRS + 1)
            nc.scalar.activation(XS8, XC8, ACT.Square).then_inc(S["gn_sq"], 1)
            act.wait_ge(S["gn_var_mm"], PAIRS + 1)
            nc.scalar.activation(XS8, ps[:, 7, 0:256], ACT.Ln, bias=eps[:, 0:1], scale=1.0 / HD).then_inc(S["gn_root"], 1)
            act.wait_ge(S["gn_root"], 2 * PAIRS + 1)
            nc.scalar.activation(XS8, XS8, ACT.Exp, scale=-0.5).then_inc(S["gn_root"], 1)
            for a in range(5):
                n = P if a < 4 else N_DEC
                act.wait_ge(S["kvt_mm"], a + 1)
                nc.scalar.activation(KVT[0:n, a], ps[0:n, a, :], ACT.Copy).then_inc(S["kvt_ev"], 1)
            act.wait_ge(S["swap_mm"], 2)
            nc.scalar.activation(QSW.rearrange("p f n -> p (f n)"), ps[:, 7, 0:256], ACT.Copy).then_inc(S["qsw_ev"], 1)
            act.sem_inc(S["pexp_ev"], 4)
            act.sem_inc(S["pt_ev"], 3)
            with act.Fori(0, 2) as v:

                def exps(hd):
                    for k, i in enumerate(BLOCKS):
                        act.wait_ge(S["max_ev"], 4 * (8 * v + hd) + k + 1)
                        off = i * (i + 1) // 2 * P
                        nc.scalar.activation(PR[hd % 2][:, off:off + (i + 1) * P], ps[:, i, 0:(i + 1) * P], ACT.Exp,
                                             bias=STAT[:, 4 + hd % 2, i:i + 1], scale=SCALE, accum_out=STAT[:, 6 + hd % 2, i:i + 1]).then_inc(S["pexp_ev"], 1)
                exps(0)
                for hd in range(8):
                    n = 8 * v + hd
                    if hd < 7:
                        exps(hd + 1)
                    for a in range(4):
                        act.wait_ge(S["pt_mm"], 4 * n + a + 1)
                        toff = sum(4 - x for x in range(a)) * P
                        nc.scalar.activation(PT[hd % 2][:, toff:toff + (4 - a) * P], ps[:, 4 + a % 3, 0:(4 - a) * P], ACT.Copy).then_inc(S["pt_ev"], 1)
            act.sem_inc(S["sc_ev"], 4)
            with act.Fori(0, 4) as bp:
                def score_copy(c):
                    n = 8 * bp + c
                    act.wait_ge(S["qk_mm"], 9 * bp + c + 1)
                    for k in BOTH:
                        nc.scalar.activation(SCR[:, (2 * c + k) * 256:(2 * c + k + 1) * 256], ps[:, 4 + c % 2, k * 256:(k + 1) * 256], ACT.Copy,
                                             accum_out=DS[:, 2 * c + k:2 * c + k + 1]).then_inc(S["sc_ev"], 1)
                act.wait_ge(S["dec_ev"], bp + 1)
                for c in range(8):
                    j = (2 * c) % 8
                    act.wait_ge(page_free[j], 4 * bp + c // 4 + 2)
                    if c >= 2:
                        act.wait_ge(S["qk_mm"], 9 * bp + c - 1)
                    nc.scalar.activation(KTD[c % 2][0], ps[:, 0:2, :], ACT.Copy).then_inc(S["kt_ev_a"], 1)
                    if c:
                        score_copy(c - 1)
                score_copy(7)
                act.wait_ge(S["soft_ev"], bp + 1)
                nc.scalar.activation(SCR[:, :], SCR[:, :], ACT.Exp, bias=DS[:, 40:41], scale=SCALE, accum_out=DS[:, 41:42]).then_inc(S["pexpd_ev"], 1)
                act.wait_ge(S["ptd_mm"], 9 * bp + 1)
                nc.scalar.activation(PTO[0:N_DEC], ps[0:N_DEC, 6, 0:P], ACT.Copy).then_inc(S["ptd_ev"], 1)
                for c in range(8):
                    act.wait_ge(S["ptd_mm"], 9 * bp + c + 2)
                    if c >= 2:
                        act.wait_ge(page_free[(2 * c - 3) % 8], 4 * bp + 2 + (c - 2) // 4 + 2)
                    nc.scalar.activation(PTD[c % 2], ps[:, 4 + c % 2, :], ACT.Copy).then_inc(S["ptd_ev"], 1)
                act.wait_ge(S["oqt_mm"], bp + 1)
                nc.scalar.activation(OF, ps[:, 0, 0:P], ACT.Copy).then_inc(S["of_ev"], 1)

            def layer_norm(which):
                for k in range(KT):
                    act.wait_ge(S["ln_sub"], KT * which + k + 1)
                    if k >= 2:
                        act.wait_ge(S["ln_var_mm"], KT * which + k - 1)
                    nc.scalar.activation(LQ[k % 2], XT[:, k, :], ACT.Square).then_inc(S["ln_sq"], 1)
                act.wait_ge(S["ln_var_mm"], KT * which + KT)
                nc.scalar.activation(two(RS), ps[:, 6:8, 0:HALF], ACT.Sqrt, bias=eps[:, 1:2], scale=1.0 / D_MODEL).then_inc(S["ln_root"], 1)
                for k in range(KT):
                    g, b = (VC[:, VEC_AT[f"ln{which + 1}_{x}"] + k:VEC_AT[f"ln{which + 1}_{x}"] + k + 1] for x in "gb")
                    act.wait_ge(S["ln_scaled"], KT * which + k + 1)
                    nc.scalar.activation(XT[:, k, :], XT[:, k, :], ACT.Identity, scale=g, bias=b).then_inc(S["ln_ev"], 1)
            layer_norm(0)
            act.sem_inc(S["gate_ev"], 2)
            act.wait_ge(S["gp_zero"], 1)
            with act.Fori(0, FT // 2) as i:
                for j in range(2):
                    f = 2 * i + j
                    act.wait_ge(w_free[2 * j], ROUND_UP[2 * j] + i + 2)
                    act.wait_ge(S["conv_ev"], f + 1)
                    act.wait_ge(S["cvn_ev"], f + 1)
                    b0 = 4 * j
                    nc.scalar.activation(GP[j][:, 2:2 + HALF], ps[:, b0, 0:HALF], ACT.Copy)
                    nc.scalar.activation(GP[j][:, 2 + HALF:2 + SEQ], ps[:, b0 + 1, 0:SEQ - HALF], ACT.Copy)
                    dec = GP[j][:, SEQ + 2:GPW].rearrange("p (b t) -> p b t", t=DEC_SEQ + 2)
                    nc.scalar.activation(dec[:, :, 2:], ps[:, b0 + 1, SEQ - HALF:HALF].rearrange("p (b t) -> p b t", t=DEC_SEQ), ACT.Copy).then_inc(S["gate_ev"], 1)
                    act.wait_ge(S["conv_ev"], f + 3)
                    nc.scalar.activation(CO[j], CO[j], ACT.Silu).then_inc(S["silu_ev"], 1)
            layer_norm(1)
            for a in range(5):
                n = P if a < 4 else N_DEC
                for q in range(4):
                    act.wait_ge(S["y_mm"], 4 * a + q + 1)
                    nc.scalar.activation(Y[a][0:n, q * 512:(q + 1) * 512], ps[0:n, q, :], ACT.Copy).then_inc(S["y_ev"], 1)

        @block.vector
        def _(dve):
            for k in range(KT):
                dve.wait_ge(xt_mm, k + 1)
                nc.vector.tensor_copy(XT[:, k, SEQ:TOK], ps[:, 2 * (k % 4) + 1, 0:N_DEC]).then_inc(xt_ev_b, 1)
            dve.wait_ge(small_mm, 1)
            for t in range(4):
                n = sum(k for _, k in VEC_ROWS[t])
                l = nc.vector.tensor_copy(VC[:, t * P:t * P + n], ps[:, 0, t * P:t * P + n])
            l.then_inc(small_ev, 1)
            nc.vector.tensor_copy(shiftT[:, :, :].rearrange("p m b -> p (m b)"), ps[:, 1, 0:RW_TILES * 8]).then_inc(small_ev, 1)
            cv = convT[:, :, :].rearrange("p m b -> p (m b)")
            nc.vector.tensor_copy(cv[:, 0:512], ps[:, 2, :]).then_inc(small_ev, 1)
            nc.vector.tensor_copy(cv[:, 512:FT * 16], ps[:, 3, 0:FT * 16 - 512]).then_inc(small_ev, 1)
            for g in range(7):
                dve.wait_ge(last_mm, g + 1)
                n = 512 if g < 6 else 2 * P + LAST_W
                nc.vector.tensor_copy(last_tok[:, g * 512:g * 512 + n], ps[0:33, 4 + g % 4, 0:n]).then_inc(last_ev, 1)

            link_n = [0]

            def link(ins):
                link_n[0] += 1
                ins.then_inc(shift_chain, 1)
                dve.wait_ge(shift_chain, link_n[0])
            l = nc.vector.tensor_scalar(HB[:, :], VC[:, VEC_AT["w0"]:VEC_AT["w0"] + 16], 0.5, None, ALU.mult)
            for m0, m1, rows in ((0, 8, P), (8, 16, P), (16, 24, P), (24, 26, P), (26, 27, LAST_W)):
                n = m1 - m0
                z = ZT[0:rows, ATT_TILES + m0:ATT_TILES + m1, :]
                d = D3[0:rows, 0:n, :]
                zs, ds = (x[:, :, SEQ:TOK].rearrange("p m (b t) -> p m b t", t=DEC_SEQ) for x in (z, d))
                nc.vector.tensor_tensor(d[:, :, 1:SEQ], z[:, :, 0:SEQ - 1], z[:, :, 1:SEQ], ALU.subtract)
                nc.vector.tensor_scalar(d[:, :, 0], z[:, :, 0], -1.0, None, ALU.mult)
                for m in range(n):
                    nc.vector.tensor_tensor(ds[:, m, :, 1:DEC_SEQ], zs[:, m, :, 0:DEC_SEQ - 1], zs[:, m, :, 1:DEC_SEQ], ALU.subtract)
                link(nc.vector.tensor_tensor(ds[:, :, :, 0], shiftT[0:rows, m0:m1, :], zs[:, :, :, 0], ALU.subtract))
                for m in range(n):
                    mu = VC[0:rows, VEC_AT["shift_mu"] + m0 + m:VEC_AT["shift_mu"] + m0 + m + 1]
                    l = nc.vector.scalar_tensor_tensor(out=z[:, m], in0=d[:, m], scalar=mu, in1=z[:, m], op0=ALU.mult, op1=ALU.add)
                link(l)
            nc.vector.memset(ST[0], 0.0).then_inc(shifted, 1)
            for x in (AR, BB, KB, VB):
                l = nc.vector.memset(x, 0.0)
                l.then_inc(S["bd_zero"], 1)
            nc.vector.memset(ST[1], 0.0).then_inc(S["bd_zero"], 1)
            dve.sem_inc(S["chain_ev"], 1)
            dve.wait_ge(stored, 9 * 16)
            dve.sem_inc(S["bd_zero"], 1)

            K = 7
            BOTH = range(2)
            seg = const("seg")
            masks = {n: const(n) for n in ("low8", "lowoff", "up8", "up", "upinc")}
            wide = lambda m: masks[m].rearrange("p (a n) -> p a n", a=1).to_broadcast([P, SC, P])
            two = lambda x: x.rearrange("p (h t) -> p h t", h=2)
            with dve.Fori(0, PAIRS) as p:
                count = [0]

                def link(ins):
                    count[0] += 1
                    ins.then_inc(S["rw_chain"], 1)
                    dve.wait_ge(S["rw_chain"], K * p + count[0])
                vec = lambda name: VC[:, bass.ds(VEC_AT[name] + p, 1)]
                tile = lambda j: ZT[:, bass.ds(ATT_TILES + 8 * j + p, 1), :].rearrange("p a t -> p (a t)")
                rz, kz, vz = tile(0), tile(1), tile(2)
                dve.wait_ge(S["pair_pool"], p + 1)
                nc.vector.tensor_scalar(KK, kz, vec("k_k"), None, ALU.mult).then_inc(S["kk_raw"], 1)
                dve.wait_ge(S["lora_ev"], 3 * p + 1)
                link(nc.vector.tensor_scalar(LD, LD, 0.5 * DECAY_SCALE, 0.5 * DECAY_SCALE, ALU.mult, ALU.add))
                link(nc.vector.tensor_tensor_scan(LC[:, 0:SEQ], seg, LD[:, 0:SEQ], 0.0, ALU.mult, ALU.add))
                nc.vector.tensor_tensor(PY[:, 0:SEQ], LC[:, 0:SEQ], LD[:, 0:SEQ], ALU.subtract).then_inc(S["lprev_ready"], 1)
                dve.wait_ge(S["ss_mm"], p + 1)
                nc.vector.tensor_scalar(two(SQ), ps[:, 6:8, 0:HALF], 1e-24, None, ALU.max).then_inc(S["ss_max"], 1)
                dve.wait_ge(S["lora_ev"], 3 * p + 2)
                link(nc.vector.tensor_scalar(AA, AA, 0.5, 0.5, ALU.mult, ALU.add))
                link(nc.vector.tensor_scalar(BON, AA, -1.0, vec("k_a"), ALU.add, ALU.mult))
                link(nc.vector.scalar_tensor_tensor(out=kz, in0=BON, scalar=1.0, in1=kz, op0=ALU.add, op1=ALU.mult))
                nc.vector.scalar_tensor_tensor(out=BON, in0=rz, scalar=vec("r_k"), in1=kz, op0=ALU.mult, op1=ALU.mult).then_inc(S["bonus_in"], 1)
                dve.wait_ge(S["ss_root"], 2 * p + 2)
                link(nc.vector.tensor_tensor(KK, KK, SQ, ALU.mult))
                link(nc.vector.tensor_tensor(AB, KK, AA, ALU.mult))
                for j, x in enumerate((rz, kz, vz, KK, AB)):
                    l = nc.vector.tensor_copy(SVT6[:, j * N_DEC:(j + 1) * N_DEC], x[:, SEQ:TOK])
                l.then_inc(S["ab_ready"], 1)
                dve.wait_ge(S["bonus_mm"], p + 1)
                nc.vector.tensor_tensor(two(BON), ps[:, 6:8, 0:HALF], two(vz), ALU.mult).then_inc(S["bonus_ev"], 1)
                dve.wait_ge(S["exp_ev"], 4 * p + 4)
                for h in BOTH:
                    hp = 2 * p + h
                    if h:
                        dve.wait_ge(S["gram_mm"], 4 * p + 2)
                    for e in BOTH:
                        rows = slice(e * 64, e * 64 + 64)
                        cut = lambda x: x[rows, h * 256:(h + 1) * 256].rearrange("p (c t) -> p c t", t=CHUNK)
                        nc.vector.scalar_tensor_tensor(out=AR[rows, :, 0, e * 64:e * 64 + 64], in0=cut(KK), scalar=-1.0,
                                                       in1=cut(PY), op0=ALU.mult, op1=ALU.mult)
                        l = nc.vector.tensor_tensor(BB[rows, :, e * 64:e * 64 + 64], cut(AB), cut(PN), ALU.mult)
                    l.then_inc(S["bd_dve"], 1)
                    three = lambda x: x.rearrange("p (c n) -> p c n", n=P)
                    for s in BOTH:
                        n = 4 * p + 2 * h + s + 1
                        dve.wait_ge(S["gram_mm"], n)
                        if h and not s:
                            dve.wait_ge(S["o_mm"], 8 * p + 4)
                        bank0 = ps[:, 3 * s, :].rearrange("p (c w n) -> p c w n", w=2, n=P)
                        bank1 = ps[:, 3 * s + 1, :].rearrange("p (c w n) -> p c w n", w=2, n=P)
                        bank2 = three(ps[:, 3 * s + 2, 0:256])
                        nc.vector.tensor_tensor(NdT[s], bank0[:, :, 0], wide("up8"), ALU.mult)
                        nc.vector.tensor_tensor(BR[s][:, :, 1], bank0[:, :, 1], wide("upinc"), ALU.mult)
                        nc.vector.tensor_tensor(AKT[s], bank1[:, :, 0], wide("up"), ALU.mult)
                        nc.vector.tensor_tensor(RKT[s], bank1[:, :, 1], wide("upinc"), ALU.mult)
                        nc.vector.tensor_tensor(Nd[s], bank2, wide("low8"), ALU.mult)
                        nc.vector.tensor_tensor(Lo[s], bank2, wide("lowoff"), ALU.mult).then_inc(S["gram_ev"], 1)
                        dve.wait_ge(S["gram_ev"], 2 * n - 1)
                        l = nc.vector.tensor_tensor(P1T[s], NdT[s], ident.rearrange("p (a n) -> p a n", a=1).to_broadcast([P, SC, P]), ALU.add)
                        l.then_inc(S["gram_ev"], 1)
                    for s in BOTH:
                        n = 4 * p + 2 * h + s + 1
                        dve.wait_ge(S["solve_pe"], after("solve_pe", "n4", n, s))
                        dve.wait_ge(S["gram_ev"], 2 * n)
                        nc.vector.tensor_copy(N4[s], three(ps[:, 3 * s + 2, 0:256]))
                        nc.vector.tensor_tensor(P2T[s], three(ps[:, 3 * s + 2, 256:512]), P1T[s], ALU.add).then_inc(S["solve_dve"], 1)
                    for s in BOTH:
                        n = 4 * p + 2 * h + s + 1
                        dve.wait_ge(S["solve_pe"], after("solve_pe", "p3", n, s))
                        dve.wait_ge(S["solve_dve"], after("solve_dve", "p2", n, s))
                        nc.vector.tensor_tensor(P3T[s], three(ps[:, 3 * s, 0:256]), P2T[s], ALU.add).then_inc(S["solve_dve"], 1)
                    four = lambda x: x.rearrange("p (c w n) -> p c w n", w=2, n=P)
                    for s in BOTH:
                        n = 4 * p + 2 * h + s + 1
                        dve.wait_ge(S["solve_pe"], after("solve_pe", "m", n, s))
                        nc.vector.tensor_copy(By[s], four(ps[:, 3 * s + 2, :])).then_inc(S["solve_dve"], 1)
                    for s in BOTH:
                        n = 4 * p + 2 * h + s + 1
                        dve.wait_ge(S["solve_pe"], after("solve_pe", "m2", n, s))
                        dve.wait_ge(S["solve_dve"], after("solve_dve", "b0", n, s))
                        nc.vector.tensor_tensor(Bx[s], four(ps[:, 3 * s + 1, :]), By[s], ALU.add).then_inc(S["solve_dve"], 1)
                    for s in BOTH:
                        n = 4 * p + 2 * h + s + 1
                        dve.wait_ge(S["solve_pe"], after("solve_pe", "m4", n, s))
                        dve.wait_ge(S["solve_dve"], after("solve_dve", "b1", n, s))
                        nc.vector.tensor_tensor(By[s], four(ps[:, 3 * s + 2, :]), Bx[s], ALU.add).then_inc(S["solve_dve"], 1)
                    for s in BOTH:
                        n = 4 * p + 2 * h + s + 1
                        dve.wait_ge(S["solve_pe"], after("solve_pe", "b3", n, s))
                        dve.wait_ge(S["solve_dve"], after("solve_dve", "b2", n, s))
                        nc.vector.tensor_tensor(Bx[s], four(ps[:, 3 * s + 1, :]), By[s], ALU.add).then_inc(S["solve_dve"], 1)
                    for s in BOTH:
                        n = 4 * p + 2 * h + s + 1
                        dve.wait_ge(S["solve_pe"], after("solve_pe", "g", n, s))
                        b = four(ps[:, 3 * s + 2, :])
                        dve.wait_ge(S["bd_pool"], hp + 1)
                        nc.vector.tensor_tensor(GT[s], b[:, :, 0], ident.rearrange("p (a n) -> p a n", a=1).to_broadcast([P, SC, P]), ALU.add)
                        nc.vector.tensor_tensor(R2[s], b[:, :, 1], AR[:, s * SC:(s + 1) * SC, 1], ALU.add).then_inc(S["solve_dve"], 1)
                    for x in range(HC):
                        dve.wait_ge(S["chain_mm"], 8 * p + 4 * h + x + 1)
                        if h or x:
                            dve.wait_ge(S["o_mm"], 8 * p + 4 * h + x)
                        end = (4 * h + x + 1) * CHUNK - 1
                        nc.vector.tensor_scalar(ST[(4 * h + x + 1) % 2], ps[:, 6 + x % 2, 0:P], PX[:, end:end + 1], None,
                                                ALU.mult).then_inc(S["chain_ev"], 1)
                dve.wait_ge(S["wkv_mm"], p + 1)
                nc.vector.memset(ST[0], 0.0).then_inc(S["ld_ready"], 1)
                assert count[0] == K, count

            rc = [0]

            def step(ins):
                rc[0] += 1
                ins.then_inc(S["rec"], 1)
                dve.wait_ge(S["rec"], rc[0])
            cols = lambda x, n: x.rearrange("p (a j) -> p a j", a=1).to_broadcast([P, n, HD])
            rows_of = lambda x: x.rearrange("p (i a) -> p i a", a=1).to_broadcast([P, 32, HD])
            nc.vector.memset(eps[:, 0:1], GN_EPS)
            nc.vector.memset(eps[:, 1:2], LN_EPS).then_inc(S["rec"], 1)
            rc[0] += 1
            def recurrence():
                dve.wait_ge(S["sv_in"], 16 * 6 * DEC_BATCH)
                for half in range(2):
                    dve.wait_ge(S["state_in"], 16 * half + 16)
                    for t in range(DEC_SEQ):
                        r, k, v, kk, ab, w = (SV[:, j, t] for j in range(6))
                        yield step(nc.vector.tensor_tensor(TD, SD, cols(kk, 32), ALU.mult))
                        nc.vector.tensor_reduce(SA, TD, AX, ALU.add).then_inc(S["rec"], 1)
                        rc[0] += 1
                        yield
                        yield step(nc.vector.tensor_tensor(SD, SD, cols(w, 32), ALU.mult))
                        yield step(nc.vector.tensor_tensor(TD, rows_of(SA), cols(ab, 32), ALU.mult))
                        yield step(nc.vector.tensor_tensor(SD, SD, TD, ALU.subtract))
                        yield step(nc.vector.tensor_tensor(TD, rows_of(v[:, half * 32:half * 32 + 32]), cols(k, 32), ALU.mult))
                        yield step(nc.vector.tensor_tensor(SD, SD, TD, ALU.add))
                        yield step(nc.vector.tensor_tensor(TD, SD, cols(r, 32), ALU.mult))
                        yield step(nc.vector.tensor_reduce(OD[:, t, half * 32:half * 32 + 32], TD, AX, ALU.add))
                    dve.sem_inc(S["rec_half"], 1)
            steps = recurrence()

            def recur(n):
                for _ in range(n):
                    next(steps, None)

            def rotate(r):
                m = ROPE_TILES[r]
                dve.wait_ge(S["rot_mm"], r + 1)
                nc.vector.tensor_tensor(two(RT), ps[:, 4:6, 0:HALF], two(const("sin")), ALU.mult)
                nc.vector.tensor_tensor(ZT[:, m, :], ZT[:, m, :], const("cos"), ALU.mult).then_inc(S["rope_chain"], 1)
                dve.wait_ge(S["rope_chain"], r + 1)
                nc.vector.tensor_tensor(ZT[:, m, :], ZT[:, m, :], RT, ALU.add).then_inc(S["rope_ev"], 1)
                dve.wait_ge(S["rope_ev"], r + 1)

            def norm_end(p):
                o, gate, bonus = (ZT[:, ATT_TILES + 8 * j + p, 0:SEQ] for j in range(3))
                x = XC[p % 2]
                dve.wait_ge(S["gn_root"], 2 * p + 2)
                nc.vector.tensor_tensor(x, x, XS, ALU.mult).then_inc(S["gn_chain"], 1)
                dve.wait_ge(S["gn_chain"], 4 * p + 2)
                nc.vector.tensor_scalar(x, x, VC[:, VEC_AT["gn_g"] + p:VEC_AT["gn_g"] + p + 1], VC[:, VEC_AT["gn_b"] + p:VEC_AT["gn_b"] + p + 1],
                                        ALU.mult, ALU.add).then_inc(S["gn_chain"], 1)
                dve.wait_ge(S["gn_chain"], 4 * p + 3)
                nc.vector.tensor_tensor(x, x, bonus, ALU.add).then_inc(S["gn_chain"], 1)
                dve.wait_ge(S["gn_chain"], 4 * p + 4)
                nc.vector.tensor_tensor(o, x, gate, ALU.mult).then_inc(S["gn_ev"], 1)
            for t in range(ATT_TILES):
                recur(3)
                if t and ATT_ORDER[t - 1] in ROPE_TILES:
                    rotate(ROPE_TILES.index(ATT_ORDER[t - 1]))
                if 1 <= t <= PAIRS:
                    norm_end(t - 1)
                if t < PAIRS:
                    dve.wait_ge(S["gn_mu_mm"], t + 1)
                    nc.vector.scalar_tensor_tensor(out=XC[t % 2], in0=ps[:, 6, :], scalar=-1.0 / HD, in1=ZT[:, ATT_TILES + t, 0:SEQ],
                                                   op0=ALU.mult, op1=ALU.add).then_inc(S["gn_chain"], 1)
                recur(4)
            recur(80)
            rotate(len(ROPE_TILES) - 1)
            dve.wait_ge(S["ot_mm"], 1)
            o, gate, bonus = (ZT[:, ATT_TILES + 8 * j:ATT_TILES + 8 * j + 8, SEQ:TOK] for j in range(3))
            eight = lambda x: x.rearrange("p (f n) -> p f n", n=N_DEC)
            vec8 = lambda name: VC[:, VEC_AT[name]:VEC_AT[name] + 8].rearrange("p (f a) -> p f a", a=1).to_broadcast([P, 8, N_DEC])
            nc.vector.tensor_copy(o, eight(ps[:, 4, 0:256])).then_inc(S["ot_ev"], 1)
            dve.wait_ge(S["gn_mu_mm"], PAIRS + 1)
            dve.wait_ge(S["ot_ev"], 1)
            dve.wait_ge(S["gn_ev"], PAIRS)
            x = eight(XC8)
            nc.vector.scalar_tensor_tensor(out=x, in0=eight(ps[:, 6, 0:256]), scalar=-1.0 / HD, in1=o, op0=ALU.mult, op1=ALU.add).then_inc(S["gn_chain"], 1)
            dve.wait_ge(S["gn_root"], 2 * PAIRS + 2)
            for i, (y, op) in enumerate(((eight(XS8), ALU.mult), (vec8("gn_g"), ALU.mult), (vec8("gn_b"), ALU.add), (bonus, ALU.add))):
                nc.vector.tensor_tensor(x, x, y, op).then_inc(S["gn_chain"], 1)
                dve.wait_ge(S["gn_chain"], 4 * PAIRS + 2 + i)
            nc.vector.tensor_tensor(o, x, gate, ALU.mult).then_inc(S["gn_ev"], 1)
            dve.wait_ge(S["gn_ev"], PAIRS + 1)
            dve.wait_ge(S["swap_mm"], 1)
            for kv in range(4):
                m, own = divmod(kv, 2)
                for e in range(2):
                    rows = slice(e * 64, e * 64 + 64)
                    src = ZT[rows, 8 + m, 0:SEQ] if e == own else ps[rows, 5 + m, :]
                    l = nc.vector.tensor_copy(KDUP[rows, kv], src)
            l.then_inc(S["kdup_ev"], 1)
            nc.vector.memset(QBD, 0.0).then_inc(S["qbd_zero"], 1)
            dve.wait_ge(S["qbd_zero"], 1)
            dve.wait_ge(S["qsw_ev"], 1)
            for pair in range(2):
                for kv2 in range(2):
                    rows = slice(kv2 * 64, kv2 * 64 + 64)
                    for g in range(4):
                        f = (2 * pair + kv2) * 2 + g // 2
                        src = ZT[rows, f, SEQ:TOK] if g % 2 == kv2 else QSW[rows, f]
                        dst = QBD[rows, pair, :, kv2 * 16:kv2 * 16 + 16].rearrange("p b (t g) -> p b t g", g=4)[:, :, :, g]
                        l = nc.vector.tensor_copy(dst, src.rearrange("p (b t) -> p b t", t=DEC_SEQ))
            l.then_inc(S["qbd_ev"], 1)
            dve.wait_ge(S["kvt_out"], 160)
            dve.sem_inc(S["ao_ev"], 1)
            with dve.Fori(0, 2) as v:

                def output(q):
                    dve.wait_ge(S["ao_mm"], 8 * v + 2 * q + 2)
                    nc.vector.tensor_copy(ZT[:, bass.ds(4 * v + q, 1), 0:SEQ].rearrange("p a t -> p (a t)"), ps[:, 7, :]).then_inc(S["ao_ev"], 1)
                for hd in range(8):
                    n = 8 * v + hd
                    b = hd % 2
                    for k, i in enumerate(BLOCKS):
                        dve.wait_ge(S["sc_mm"], 4 * n + k + 1)
                        nc.vector.tensor_reduce(STAT[:, 2 + b, i:i + 1], ps[:, i, 0:(i + 1) * P], AX, ALU.max).then_inc(S["att_chain"], 1)
                        dve.wait_ge(S["att_chain"], 5 * n + k + 1)
                        nc.vector.tensor_scalar(STAT[:, 4 + b, i:i + 1], STAT[:, 2 + b, i:i + 1], -SCALE, None, ALU.mult).then_inc(S["max_ev"], 1)
                    dve.wait_ge(S["pexp_ev"], 4 * n + 8)
                    nc.vector.reciprocal(STAT[:, 8 + b], STAT[:, 6 + b]).then_inc(S["att_chain"], 1)
                    dve.wait_ge(S["att_chain"], 5 * n + 5)
                    for i in range(4):
                        off = i * (i + 1) // 2 * P
                        x = PR[b][:, off:off + (i + 1) * P]
                        l = nc.vector.tensor_scalar(x, x, STAT[:, 8 + b, i:i + 1], None, ALU.mult)
                    l.then_inc(S["pnorm_ev"], 1)
                    if hd and b == 0:
                        output(hd // 2 - 1)
                output(3)
            dve.sem_inc(S["dec_ev"], 1)
            dve.wait_ge(S["ao_ev"], 9)
            with dve.Fori(0, 4) as bp:
                nc.vector.tensor_copy(QB, QBD[:, :, bass.ds(2 * bp, 2), :]).then_inc(S["qb_ev"], 1)
                for c in range(8):
                    j = (2 * c + 1) % 8
                    dve.wait_ge(page_free[j], 4 * bp + c // 4 + 2)
                    if c >= 2:
                        dve.wait_ge(S["qk_mm"], 9 * bp + c - 1)
                    nc.vector.tensor_copy(KTD[c % 2][1], ps[:, 2:4, :]).then_inc(S["kt_ev_d"], 1)
                dve.wait_ge(S["qk_mm"], 9 * bp + 9)
                dve.wait_ge(S["sc_ev"], 16 * bp + 20)
                own = C[:, bass.ds(CONST_AT["own"][0] + bp * N_DEC, N_DEC)]
                dc = [0]
                KD = 8

                def link(ins):
                    dc[0] += 1
                    ins.then_inc(S["dec_chain"], 1)
                    dve.wait_ge(S["dec_chain"], KD * bp + dc[0])
                nc.vector.tensor_tensor(SCR[:, PAST_LEN:SC_W], ps[:, 6, 0:N_DEC], own, ALU.add)
                gates = DS[:, 0:16]
                g_i = gates.rearrange("p (i a) -> p i a", a=1).to_broadcast([P, 16, 16])
                g_j = gates.rearrange("p (a j) -> p a j", a=1).to_broadcast([P, 16, 16])
                before = const("before").rearrange("p (i j) -> p i j", j=16)
                nc.vector.tensor_tensor(RK[:, 0], g_j, g_i, ALU.is_gt)
                link(nc.vector.tensor_tensor(RK[:, 1], g_j, g_i, ALU.is_ge))
                link(nc.vector.tensor_tensor(RK[:, 1], RK[:, 1], before, ALU.mult))
                link(nc.vector.tensor_tensor(RK[:, 0], RK[:, 0], RK[:, 1], ALU.max))
                link(nc.vector.tensor_reduce(DS[:, 16:32], RK[:, 0], AX, ALU.add))
                link(nc.vector.tensor_scalar(DS[:, 16:32], DS[:, 16:32], 2.5, NEG, ALU.is_gt, ALU.mult))
                blocks = SCR[:, 0:PAST_LEN].rearrange("p (n k) -> p n k", k=256)
                link(nc.vector.tensor_tensor(blocks, blocks, DS[:, 16:32].rearrange("p (n a) -> p n a", a=1).to_broadcast([P, 16, 256]), ALU.add))
                link(nc.vector.tensor_reduce(DS[:, 39:40], SCR[:, :], AX, ALU.max))
                nc.vector.tensor_scalar(DS[:, 40:41], DS[:, 39:40], -SCALE, None, ALU.mult).then_inc(S["soft_ev"], 1)
                dve.wait_ge(S["pexpd_ev"], bp + 1)
                link(nc.vector.reciprocal(DS[:, 42:43], DS[:, 41:42]))
                dve.wait_ge(S["pv_mm"], bp + 1)
                nc.vector.tensor_scalar(OQ, ps[:, 7, 0:P], DS[:, 42:43], None, ALU.mult).then_inc(S["oq_ev"], 1)
                dve.wait_ge(S["osw_mm"], bp + 1)
                cols_of = lambda x: x.rearrange("p (b r v t g) -> p b r v t g", b=2, r=2, v=2, t=4)
                for r in range(2):
                    for kv2 in range(2):
                        for g in range(4):
                            f = (2 * r + kv2) * 2 + g // 2
                            e = g % 2
                            rows = slice(e * 64, e * 64 + 64)
                            src = (OF if e == kv2 else ps[:, 1, 0:P])[rows]
                            src = cols_of(src)[:, :, r, kv2, :, g]
                            dst = ZT[rows, f:f + 1, bass.ds(SEQ + 8 * bp, 8)].rearrange("p a (b t) -> p (a b) t", t=DEC_SEQ)
                            l = nc.vector.tensor_copy(dst, src)
                l.then_inc(S["dec_ev"], 1)
                assert dc[0] == 8, dc
                dve.wait_ge(S["dec_ev"], bp + 2)
            with dve.Fori(0, 4) as i:
                for u in range(SLOTS):
                    dve.wait_ge(w_free[u], ROUND_OUT[u] + i + 2)
                    x = XT[:, bass.ds(4 * i + u, 1), :].rearrange("p a (h t) -> p (a h) t", h=2)
                    nc.vector.scalar_tensor_tensor(out=x, in0=x, scalar=ALPHA, in1=ps[:, 2 * (u % 2):2 * (u % 2) + 2, 0:HALF],
                                                   op0=ALU.mult, op1=ALU.add).then_inc(acc_free, 1)

            def layer_norm(which):
                dve.wait_ge(S["ln_mu_mm"], which + 1)
                for k in range(KT):
                    nc.vector.scalar_tensor_tensor(out=two(XT[:, k, :]), in0=ps[:, 4:6, 0:HALF], scalar=-1.0 / D_MODEL, in1=two(XT[:, k, :]),
                                                   op0=ALU.mult, op1=ALU.add).then_inc(S["ln_sub"], 1)
                dve.wait_ge(S["ln_root"], which + 1)
                nc.vector.reciprocal(RS, RS).then_inc(S["ln_rs"], 1)
                dve.wait_ge(S["ln_rs"], which + 1)
                for k in range(KT):
                    nc.vector.tensor_tensor(XT[:, k, :], XT[:, k, :], RS, ALU.mult).then_inc(S["ln_scaled"], 1)
            dve.wait_ge(acc_free, IN_TILES + KT + 2)
            layer_norm(0)
            dve.sem_inc(S["conv_ev"], 2)
            dve.sem_inc(S["h_ev"], 2)
            with dve.Fori(0, FT // 2) as i:
                for j in range(2):
                    f = 2 * i + j
                    taps = [VC[:, bass.ds(VEC_AT[f"conv{x}"] + f, 1)] for x in range(3)]
                    bias = VC[:, bass.ds(VEC_AT["conv_b"] + f, 1)]
                    dve.wait_ge(S["gate_ev"], f + 3)
                    dve.wait_ge(S["gp_hist"], f + 1)
                    dve.wait_ge(S["h_ev"], f + 1)
                    nc.vector.tensor_scalar(CO[j], GP[j][:, 2:GPW], taps[2], bias, ALU.mult, ALU.add).then_inc(S["conv_chain"], 1)
                    dve.wait_ge(S["conv_chain"], 2 * f + 1)
                    nc.vector.scalar_tensor_tensor(out=CO[j], in0=GP[j][:, 1:GPW - 1], scalar=taps[1], in1=CO[j], op0=ALU.mult, op1=ALU.add).then_inc(S["conv_chain"], 1)
                    dve.wait_ge(S["conv_chain"], 2 * f + 2)
                    nc.vector.scalar_tensor_tensor(out=CO[j], in0=GP[j][:, 0:GPW - 2], scalar=taps[0], in1=CO[j], op0=ALU.mult, op1=ALU.add).then_inc(S["conv_ev"], 1)
                    dve.wait_ge(S["silu_ev"], f + 1)
                    dve.wait_ge(w_free[2 * j + 1], ROUND_UP[2 * j + 1] + i + 2)
                    b0 = 4 * j + 2
                    ht = HT[:, bass.ds(f, 1), :].rearrange("p a t -> p (a t)")
                    nc.vector.tensor_tensor(ht[:, 0:HALF], CO[j][:, 0:HALF], ps[:, b0, 0:HALF], ALU.mult)
                    nc.vector.tensor_tensor(ht[:, HALF:SEQ], CO[j][:, HALF:SEQ], ps[:, b0 + 1, 0:SEQ - HALF], ALU.mult)
                    nc.vector.tensor_tensor(ht[:, SEQ:TOK].rearrange("p (b t) -> p b t", t=DEC_SEQ),
                                            co_dec[j], ps[:, b0 + 1, SEQ - HALF:HALF].rearrange("p (b t) -> p b t", t=DEC_SEQ), ALU.mult).then_inc(S["h_ev"], 1)
            with dve.Fori(0, KT // 2) as i:
                for m in range(2):
                    dve.wait_ge(w_free[3], ROUND_DOWN[3] + 2 * i + m + 2)
                    x = XT[:, bass.ds(2 * i + m, 1), :].rearrange("p a (h t) -> p (a h) t", h=2)
                    nc.vector.scalar_tensor_tensor(out=x, in0=x, scalar=ALPHA, in1=ps[:, 2 * m:2 * m + 2, 0:HALF],
                                                   op0=ALU.mult, op1=ALU.add).then_inc(acc_free, 1)
            for g in range(11):
                dve.wait_ge(S["cn_mm"], g + 1)
                nc.vector.tensor_copy(CN[:, g * 512:(g + 1) * 512], ps[0:18, g % 4, :]).then_inc(S["cn_ev"], 1)
            dve.wait_ge(acc_free, IN_TILES + 2 * KT + 2)
            layer_norm(1)

        @block.gpsimd
        def _(pool):
            nc.gpsimd.memset(shift_tok, 0.0).then_inc(pads_zero, 1)
            pool.wait_ge(pads_zero, 1)
            nc.gpsimd.memset(vec_tok, 0.0).then_inc(pads_zero, 1)

            BOTH = range(2)
            pool.sem_inc(S["pair_pool"], 1)
            pool.sem_inc(S["sv_out"], 16)
            pool.sem_inc(S["ld_ready"], 1)
            pool.wait_ge(S["bd_zero"], 6)
            with pool.Fori(0, PAIRS) as p:
                pool.wait_ge(S["lora_mm"], 3 * p + 1)
                cols = bass.ds(p * P, P)
                for dst, src in ((LW[0:64, 0], w2[0, :, cols]), (LW[64:128, 0], a2[0, :, cols]),
                                 (LW[:, 1], g2[0, 0:P, cols]), (LW[0:32, 2], g2[0, P:160, cols])):
                    pool.dma_start(dst, src).then_inc(S["lw_landed"], 16)
                pool.wait_ge(S["exp_ev"], 4 * p + 4)
                pool.wait_ge(S["ab_ready"], p + 1)
                for h in BOTH:
                    if h:
                        pool.wait_ge(S["solve_dve"], after("solve_dve", "g", 4 * p + 2, 1))
                    for e in BOTH:
                        rows = slice(e * 64, e * 64 + 64)
                        cut = lambda x: x[rows, h * 256:(h + 1) * 256].rearrange("p (c t) -> p c t", t=CHUNK)
                        zcut = lambda j: ZT[rows, bass.ds(ATT_TILES + 8 * j + p, 1), h * 256:(h + 1) * 256].rearrange("p a (c t) -> p (a c) t", t=CHUNK)
                        nc.gpsimd.tensor_tensor(KB[rows, :, e * 64:e * 64 + 64], zcut(1), cut(PN), ALU.mult)
                        l = nc.gpsimd.tensor_tensor(AR[rows, :, 1, e * 64:e * 64 + 64], zcut(0), cut(PX), ALU.mult)
                    l.then_inc(S["bd_pool"], 1)
                pool.wait_ge(S["bd_act"], 2 * p + 2)
                pool.wait_ge(S["bonus_ev"], p + 1)
                pool.wait_ge(S["bd_pool"], 2 * p + 2)
                pool.wait_ge(S["lora_ev"], 3 * p + 3)
                for j, x in ((2, BON), (1, G)):
                    l = nc.gpsimd.tensor_copy(ZT[:, bass.ds(ATT_TILES + 8 * j + p, 1), :].rearrange("p a t -> p (a t)"), x)
                l.then_inc(S["pair_pool"], 1)
            pool.wait_ge(S["wkv_ev"], PAIRS)
            pool.wait_ge(S["ld_ready"], PAIRS + 1)
            pool.dma_start(SD, st_v[:, 0:32]).then_inc(S["state_in"], 16)
            pool.wait_ge(S["rec_half"], 1)
            pool.dma_start(wst_v[:, 0:32], SD).then_inc(S["state_out"], 16)
            pool.wait_ge(S["state_out"], 16)
            pool.dma_start(SD, st_v[:, 32:64]).then_inc(S["state_in"], 16)
            pool.wait_ge(S["rec_half"], 2)
            pool.dma_start(wst_v[:, 32:64], SD).then_inc(S["state_out"], 16)
            for b in range(DEC_BATCH):
                pool.dma_start(dec_out[b * DEC_SEQ:(b + 1) * DEC_SEQ].rearrange("t (h i) -> h t i", i=HD), OD[b * 16:b * 16 + 16]).then_inc(S["dec_o"], 16)
            pool.wait_ge(S["dec_o"], 16 * DEC_BATCH)
            pool.dma_start(o_tok, dec_out).then_inc(S["dec_o_in"], 16)
            pool.wait_ge(S["kvt_ev"], 5)
            pool.wait_ge(S["kdup_ev"], 1)
            pool.wait_ge(S["rope_ev"], 10)
            for v in range(4):
                j = v % 2
                if v >= 2:
                    pool.wait_ge(S["ao_ev"], 2 * v - 1)
                nc.gpsimd.tensor_copy(KC[j], KDUP[:, v])
                nc.gpsimd.tensor_copy(Q2[j], ZT[:, 2 * v:2 * v + 2, 0:SEQ])
                nc.gpsimd.tensor_copy(VS[j], KVT[:, 0:4, 256 + v * HD:256 + (v + 1) * HD]).then_inc(S["stat_copy"], 1)
            load_pages(pool, 1)
            pool.wait_ge(S["dec_ev"], 5)
            pool.sem_inc(S["cvn_ev"], 2)
            nc.gpsimd.memset(GP[0][:, 0:2], 0.0)
            nc.gpsimd.memset(GP[1][:, 0:2], 0.0).then_inc(S["gp_zero"], 1)
            with pool.Fori(0, FT // 2) as i:
                for j in range(2):
                    f = 2 * i + j
                    dec = GP[j][:, SEQ + 2:GPW].rearrange("p (b t) -> p b t", t=DEC_SEQ + 2)
                    pool.wait_ge(S["conv_ev"], f + 1)
                    nc.gpsimd.tensor_copy(dec[:, :, 0:2], convT[:, bass.ds(f, 1), :].rearrange("p a (b r) -> p (a b) r", r=2)).then_inc(S["gp_hist"], 1)
                    pool.wait_ge(S["gate_ev"], f + 3)
                    nc.gpsimd.tensor_copy(CVN[:, bass.ds(f, 1), 0:2].rearrange("p a n -> p (a n)"), GP[j][:, SEQ:SEQ + 2])
                    nc.gpsimd.tensor_copy(CVN[:, bass.ds(f, 1), 2:18].rearrange("p a (b r) -> p (a b) r", r=2), dec[:, :, DEC_SEQ:]).then_inc(S["cvn_ev"], 1)


_INS = ["x_prompt", "x_sample", "cache_k", "cache_v", "page_table", "state_wkv", "state_shift", "state_conv",
        "w_in", "w_out", "shift_mu", "w0", "w2", "a0", "a2", "g2", "k_k", "k_a", "r_k", "gn_g", "gn_b",
        "ln1_g", "ln1_b", "ln2_g", "ln2_b", "w_up", "conv_w", "conv_b", "w_down"]
_OUTS = [(1, SEQ, D_MODEL), (DEC_BATCH, DEC_SEQ, D_MODEL), (1, 1, SEQ, 4, HD), (1, 1, SEQ, 4, HD),
         (1, 1, 16, HD, HD), (1, 1, RW_PROJ), (1, 1, 2, D_FF), (1, DEC_BATCH, DEC_SEQ, 4, HD),
         (1, DEC_BATCH, DEC_SEQ, 4, HD), (1, DEC_BATCH, 16, HD, HD), (1, DEC_BATCH, RW_PROJ), (1, DEC_BATCH, 2, D_FF)]


def kernel(**inputs):
    import numpy as _np
    import concourse.bacc as _bacc
    from concourse import mybir as _mybir
    from concourse.bass_utils import run_bass_kernel_spmd as _run

    nc = _bacc.Bacc("TRN2", target_bir_lowering=False, num_devices=1)
    arrays, args = {}, []
    given = [(name, _np.ascontiguousarray(inputs[name])) for name in _INS] + [("consts", constants())]
    for name, a in given:
        arrays[f"in_{name}_dram"] = a
        args.append(nc.dram_tensor(f"in_{name}_dram", a.shape, _mybir.dt.from_np(a.dtype), kind="ExternalInput").ap())
    for i, shape in enumerate(_OUTS):
        args.append(nc.dram_tensor(f"out_{i}_dram", shape, F32, kind="ExternalOutput").ap())
    hybrid_layer_kernel(nc, *args)
    r = _run(nc, [arrays], core_ids=[0])
    return tuple(r.results[0][f"out_{i}_dram"] for i in range(len(_OUTS)))
```
